# Optimizing a Trainium2 kernel written in Bass

```python
import math
import jax, jax.numpy as jnp
from jax import lax
import numpy as np

D_MODEL = 1024
BATCH = 1
SEQ = 1024
DEPTH = 2
DEC_BATCH = 8
DEC_SEQ = 16
PAST_LEN = 256

CHUNK = 64
HEAD_DIM = 64
A_HEADS = 6
A_KV_HEADS = 2
A_GROUP = A_HEADS // A_KV_HEADS
WINDOW = 128
WIN_CHUNKS = WINDOW // CHUNK
B_HEADS = 4
B_DIM = HEAD_DIM // 2
B_VDIM = 2 * B_DIM
C_HEADS = 6
MIX_WIDTH = A_HEADS * HEAD_DIM + B_HEADS * B_VDIM + C_HEADS * HEAD_DIM
IN_SIZES = (A_HEADS * HEAD_DIM, A_KV_HEADS * HEAD_DIM, A_KV_HEADS * HEAD_DIM,
            B_HEADS * 2 * B_DIM, B_HEADS * 2 * B_DIM, B_HEADS * B_VDIM,
            C_HEADS * HEAD_DIM, C_HEADS * HEAD_DIM, C_HEADS * HEAD_DIM, C_HEADS)
N_IN = sum(IN_SIZES)
IN_SPLITS = tuple(int(v) for v in np.cumsum(IN_SIZES)[:-1])
D_FF = -(-8 * D_MODEL // (3 * 256)) * 256
N_BUCKETS = 32
MAX_DISTANCE = 1024
QBLOCK = 128
RMS_EPS = 1e-6
NEG_INF = -1e30
FORGET_BIAS_MEAN = 2.0

kernel_name = "hymba_swa_diff_fox_streaming_step"

def rms_norm(x, g):
    xf = x.astype(jnp.float32)
    y = xf * lax.rsqrt(jnp.mean(xf * xf, axis=-1, keepdims=True) + RMS_EPS)
    return (y * g.astype(jnp.float32)).astype(x.dtype)

def t5_bucket(rel):
    half = N_BUCKETS // 2
    max_exact = half // 2
    n = jnp.abs(rel)
    large = max_exact + (jnp.log(jnp.maximum(n, 1).astype(jnp.float32) / max_exact)
                         / math.log(MAX_DISTANCE / max_exact) * (half - max_exact)).astype(jnp.int32)
    large = jnp.minimum(large, half - 1)
    return jnp.where(rel > 0, half, 0) + jnp.where(n < max_exact, n, large)

def rel_bias(q_pos, k_pos, table):
    b = t5_bucket(k_pos[None, :] - q_pos[:, None])
    return jnp.moveaxis(table[b], -1, 0).astype(jnp.float32)

def project(h, w_in, b_f, qn_a, kn_a, qn_b, kn_b, qn_c, kn_c):
    B, T, _ = h.shape
    qa, ka, va, qb, kb, vb, qc, kc, vc, fz = jnp.split(h @ w_in, IN_SPLITS, axis=-1)
    qa = rms_norm(qa.reshape(B, T, A_HEADS, HEAD_DIM), qn_a)
    ka = rms_norm(ka.reshape(B, T, A_KV_HEADS, HEAD_DIM), kn_a)
    va = va.reshape(B, T, A_KV_HEADS, HEAD_DIM)
    qb = rms_norm(qb.reshape(B, T, B_HEADS, 2, B_DIM), qn_b)
    kb = rms_norm(kb.reshape(B, T, B_HEADS, 2, B_DIM), kn_b)
    vb = vb.reshape(B, T, B_HEADS, B_VDIM)
    qc = rms_norm(qc.reshape(B, T, C_HEADS, HEAD_DIM), qn_c)
    kc = rms_norm(kc.reshape(B, T, C_HEADS, HEAD_DIM), kn_c)
    vc = vc.reshape(B, T, C_HEADS, HEAD_DIM)
    logf = jax.nn.log_sigmoid((fz + b_f).astype(jnp.float32))
    return qa, ka, va, qb, kb, vb, qc, kc, vc, logf

def swa_attend(q, k, v, q_pos, k_pos, table_a, sinks):
    B, Tq = q.shape[:2]
    Tk = k.shape[1]
    qg = q.reshape(B, Tq, A_KV_HEADS, A_GROUP, HEAD_DIM)
    s = jnp.einsum('bqkgd,bskd->bkgqs', qg, k).astype(jnp.float32) * HEAD_DIM ** -0.5
    s = s + rel_bias(q_pos, k_pos, table_a).reshape(A_KV_HEADS, A_GROUP, Tq, Tk)
    qch = q_pos // CHUNK
    kch = k_pos // CHUNK
    mask = ((kch[None, :] <= qch[:, None]) & (kch[None, :] >= qch[:, None] - WIN_CHUNKS)
            & (k_pos[None, :] >= 0))
    s = jnp.where(mask, s, NEG_INF)
    sink = sinks.astype(jnp.float32).reshape(A_KV_HEADS, A_GROUP, 1, 1)
    m = jnp.maximum(s.max(-1, keepdims=True), sink)
    e = jnp.exp(s - m)
    p = e / (e.sum(-1, keepdims=True) + jnp.exp(sink - m))
    o = jnp.einsum('bkgqs,bskd->bqkgd', p.astype(v.dtype), v)
    return o.reshape(B, Tq, A_HEADS * HEAD_DIM)

def swa_prompt(q, k, v, table_a, sinks):
    B, S = q.shape[:2]
    nc = S // CHUNK
    pad = WIN_CHUNKS * CHUNK

    def band(a):
        ap = jnp.pad(a, ((0, 0), (pad, 0), (0, 0), (0, 0))).reshape(B, nc + WIN_CHUNKS, CHUNK, *a.shape[2:])
        return jnp.concatenate([ap[:, i:i + nc] for i in range(WIN_CHUNKS + 1)], axis=2)

    kpos = jnp.arange(-pad, S).reshape(nc + WIN_CHUNKS, CHUNK)
    kpos_b = jnp.concatenate([kpos[i:i + nc] for i in range(WIN_CHUNKS + 1)], axis=1)
    qpos_b = jnp.arange(S).reshape(nc, CHUNK)
    qc = q.reshape(B, nc, CHUNK, A_HEADS, HEAD_DIM)
    o = jax.vmap(lambda qq, kk, vv, qp, kp: swa_attend(qq, kk, vv, qp, kp, table_a, sinks),
                 in_axes=(1, 1, 1, 0, 0), out_axes=1)(qc, band(k), band(v), qpos_b, kpos_b)
    return o.reshape(B, S, A_HEADS * HEAD_DIM)

def diff_attend(q, k, v, q_pos, k_pos, table_b, lam, lam_init, subln):
    B, Tq = q.shape[:2]
    s = jnp.einsum('bqhmd,bkhmd->bhmqk', q, k).astype(jnp.float32) * B_DIM ** -0.5
    s = s + rel_bias(q_pos, k_pos, table_b)[:, None]
    mask = (k_pos // CHUNK)[None, :] <= (q_pos // CHUNK)[:, None]
    p = jax.nn.softmax(jnp.where(mask, s, NEG_INF), axis=-1)
    w = p[:, :, 0] - lam * p[:, :, 1]
    o = jnp.einsum('bhqk,bkhe->bqhe', w.astype(v.dtype), v)
    o = rms_norm(o, subln) * (1.0 - lam_init)
    return o.reshape(B, Tq, B_HEADS * B_VDIM)

def fox_attend(q, k, v, cum_q, cum_k, q_pos, k_pos):
    B, Tq = q.shape[:2]
    s = jnp.einsum('bqhd,bkhd->bhqk', q, k).astype(jnp.float32) * HEAD_DIM ** -0.5
    s = s + (jnp.swapaxes(cum_q, 1, 2)[..., :, None] - jnp.swapaxes(cum_k, 1, 2)[..., None, :])
    mask = k_pos[None, :] <= q_pos[:, None]
    p = jax.nn.softmax(jnp.where(mask, s, NEG_INF), axis=-1)
    o = jnp.einsum('bhqk,bkhd->bqhd', p.astype(v.dtype), v)
    return o.reshape(B, Tq, C_HEADS * HEAD_DIM)

def sweep_query_blocks(fn, qs, q_pos):
    nb = q_pos.shape[0] // QBLOCK

    def blk(a):
        return jnp.swapaxes(a.reshape(a.shape[0], nb, QBLOCK, *a.shape[2:]), 0, 1)

    out = lax.map(lambda xs: fn(xs[0], xs[1]), (tuple(blk(a) for a in qs), q_pos.reshape(nb, QBLOCK)))
    return jnp.swapaxes(out, 0, 1).reshape(qs[0].shape[0], -1, out.shape[-1])

def swiglu(h, w_gate, w_up, w_down):
    return (jax.nn.silu(h @ w_gate) * (h @ w_up)) @ w_down

def setup_inputs(seed: int = 0) -> dict:
    key = jax.random.key(seed)
    ks = iter(jax.random.split(key, 40))

    def nrm(shape, scale):
        return scale * jax.random.normal(next(ks), shape, jnp.float32)

    def gain(shape):
        return 1.0 + nrm(shape, 0.02)

    n_win = min(WINDOW, PAST_LEN)
    return {
        "x_prompt": nrm((BATCH, SEQ, D_MODEL), 1.0),
        "x_sample": nrm((DEC_BATCH, DEC_SEQ, D_MODEL), 1.0),
        "cache_a_k": nrm((DEPTH, DEC_BATCH, n_win, A_KV_HEADS, HEAD_DIM), 1.0),
        "cache_a_v": nrm((DEPTH, DEC_BATCH, n_win, A_KV_HEADS, HEAD_DIM), 1.0),
        "cache_b_k": nrm((DEPTH, DEC_BATCH, PAST_LEN, B_HEADS, 2, B_DIM), 1.0),
        "cache_b_v": nrm((DEPTH, DEC_BATCH, PAST_LEN, B_HEADS, B_VDIM), 1.0),
        "cache_c_k": nrm((DEPTH, DEC_BATCH, PAST_LEN, C_HEADS, HEAD_DIM), 1.0),
        "cache_c_v": nrm((DEPTH, DEC_BATCH, PAST_LEN, C_HEADS, HEAD_DIM), 1.0),
        "cache_c_logf": jax.nn.log_sigmoid(FORGET_BIAS_MEAN + nrm((DEPTH, DEC_BATCH, PAST_LEN, C_HEADS), 1.0)),
        "rel_bias_table": nrm((N_BUCKETS, A_HEADS + B_HEADS), 0.5),
        "norm_mix": gain((DEPTH, D_MODEL)),
        "w_in": nrm((DEPTH, D_MODEL, N_IN), D_MODEL ** -0.5),
        "b_forget": FORGET_BIAS_MEAN + nrm((DEPTH, C_HEADS), 0.5),
        "q_norm_a": gain((DEPTH, HEAD_DIM)),
        "k_norm_a": gain((DEPTH, HEAD_DIM)),
        "sinks_a": nrm((DEPTH, A_HEADS), 0.5),
        "q_norm_b": gain((DEPTH, B_DIM)),
        "k_norm_b": gain((DEPTH, B_DIM)),
        "lam_q1": nrm((DEPTH, B_DIM), 0.1),
        "lam_k1": nrm((DEPTH, B_DIM), 0.1),
        "lam_q2": nrm((DEPTH, B_DIM), 0.1),
        "lam_k2": nrm((DEPTH, B_DIM), 0.1),
        "subln_b": gain((DEPTH, B_VDIM)),
        "q_norm_c": gain((DEPTH, HEAD_DIM)),
        "k_norm_c": gain((DEPTH, HEAD_DIM)),
        "w_out": nrm((DEPTH, MIX_WIDTH, D_MODEL), MIX_WIDTH ** -0.5),
        "norm_ffn": gain((DEPTH, D_MODEL)),
        "w_gate": nrm((DEPTH, D_MODEL, D_FF), D_MODEL ** -0.5),
        "w_up": nrm((DEPTH, D_MODEL, D_FF), D_MODEL ** -0.5),
        "w_down": nrm((DEPTH, D_FF, D_MODEL), D_FF ** -0.5),
    }

def reference(x_prompt, x_sample, cache_a_k, cache_a_v, cache_b_k, cache_b_v, cache_c_k, cache_c_v,
              cache_c_logf, rel_bias_table, norm_mix, w_in, b_forget, q_norm_a, k_norm_a, sinks_a,
              q_norm_b, k_norm_b, lam_q1, lam_k1, lam_q2, lam_k2, subln_b, q_norm_c, k_norm_c,
              w_out, norm_ffn, w_gate, w_up, w_down):
    f32 = jnp.float32
    table_a = rel_bias_table[:, :A_HEADS]
    table_b = rel_bias_table[:, A_HEADS:]
    S = x_prompt.shape[1]
    T = x_sample.shape[1]
    pos_p = jnp.arange(S)
    pos_s = PAST_LEN + jnp.arange(T)
    kpos_s = jnp.arange(PAST_LEN + T)
    n_win = cache_a_k.shape[2]
    kpos_a = jnp.arange(PAST_LEN - n_win, PAST_LEN + T)
    xp, xs = x_prompt, x_sample
    pak, pav, pbk, pbv, pck, pcv, pcf = [], [], [], [], [], [], []
    sak, sav, sbk, sbv, sck, scv, scf = [], [], [], [], [], [], []
    for l in range(DEPTH):
        lam_init = 0.8 - 0.6 * math.exp(-0.3 * l)
        lam = (jnp.exp(jnp.sum(lam_q1[l].astype(f32) * lam_k1[l].astype(f32)))
               - jnp.exp(jnp.sum(lam_q2[l].astype(f32) * lam_k2[l].astype(f32))) + lam_init)
        prj = (w_in[l], b_forget[l], q_norm_a[l], k_norm_a[l], q_norm_b[l], k_norm_b[l], q_norm_c[l], k_norm_c[l])

        qa, ka, va, qb, kb, vb, qc, kc, vc, logf = project(rms_norm(xp, norm_mix[l]), *prj)
        oa = swa_prompt(qa, ka, va, table_a, sinks_a[l])
        ob = sweep_query_blocks(
            lambda qt, qp: diff_attend(qt[0], kb, vb, qp, pos_p, table_b, lam, lam_init, subln_b[l]),
            (qb,), pos_p)
        cum = jnp.cumsum(logf, axis=1)
        oc = sweep_query_blocks(
            lambda qt, qp: fox_attend(qt[0], kc, vc, qt[1], cum, qp, pos_p),
            (qc, cum), pos_p)
        xp = xp + jnp.concatenate([oa, ob, oc], axis=-1) @ w_out[l]
        xp = xp + swiglu(rms_norm(xp, norm_ffn[l]), w_gate[l], w_up[l], w_down[l])
        pak.append(ka[:, -WINDOW:]); pav.append(va[:, -WINDOW:])
        pbk.append(kb); pbv.append(vb); pck.append(kc); pcv.append(vc); pcf.append(logf)

        qa, ka, va, qb, kb, vb, qc, kc, vc, logf = project(rms_norm(xs, norm_mix[l]), *prj)
        ka_all = jnp.concatenate([cache_a_k[l], ka], axis=1)
        va_all = jnp.concatenate([cache_a_v[l], va], axis=1)
        oa = swa_attend(qa, ka_all, va_all, pos_s, kpos_a, table_a, sinks_a[l])
        ob = diff_attend(qb, jnp.concatenate([cache_b_k[l], kb], axis=1),
                         jnp.concatenate([cache_b_v[l], vb], axis=1),
                         pos_s, kpos_s, table_b, lam, lam_init, subln_b[l])
        cum = jnp.cumsum(jnp.concatenate([cache_c_logf[l].astype(f32), logf], axis=1), axis=1)
        oc = fox_attend(qc, jnp.concatenate([cache_c_k[l], kc], axis=1),
                        jnp.concatenate([cache_c_v[l], vc], axis=1),
                        cum[:, PAST_LEN:], cum, pos_s, kpos_s)
        xs = xs + jnp.concatenate([oa, ob, oc], axis=-1) @ w_out[l]
        xs = xs + swiglu(rms_norm(xs, norm_ffn[l]), w_gate[l], w_up[l], w_down[l])
        sak.append(ka_all[:, -n_win:]); sav.append(va_all[:, -n_win:])
        sbk.append(kb); sbv.append(vb); sck.append(kc); scv.append(vc); scf.append(logf)

    return (xp, xs,
            jnp.stack(pak), jnp.stack(pav), jnp.stack(pbk), jnp.stack(pbv),
            jnp.stack(pck), jnp.stack(pcv), jnp.stack(pcf),
            jnp.stack(sak), jnp.stack(sav), jnp.stack(sbk), jnp.stack(sbv),
            jnp.stack(sck), jnp.stack(scv), jnp.stack(scf))


_drawn_inputs = setup_inputs


def setup_inputs(seed=0):
    import zlib

    import numpy as np

    out = dict(_drawn_inputs(seed))
    spreads = {}
    factors = {'q_norm_a': 8.0,
     'k_norm_a': 2.845,
     'sinks_a': 64.0,
     'q_norm_b': 4.251,
     'k_norm_b': 2.742,
     'lam_k2': 3.361,
     'subln_b': 5.684,
     'q_norm_c': 8.0,
     'k_norm_c': 2.887,
     'norm_ffn': 2.982}
    for name, (base, spread) in spreads.items():
        noise = np.random.default_rng([zlib.crc32(name.encode()), seed]).standard_normal(out[name].shape)
        drawn = base * np.exp(spread * noise) if base else spread * noise
        out[name] = __import__('jax').numpy.asarray(drawn.astype(out[name].dtype))
    for name, factor in factors.items():
        out[name] = (out[name] * factor).astype(out[name].dtype)
    return out
```

```python
from contextlib import ExitStack

import numpy as np

import concourse.bass as bass
from concourse import mybir

P = 128
D_MODEL, SEQ, DEPTH, DEC_BATCH, DEC_SEQ, PAST = 1024, 1024, 2, 8, 16, 256
CHUNK, HEAD = 64, 64
A_HEADS, A_KV, B_HEADS, B_DIM, C_HEADS = 6, 2, 4, 32, 6
WINDOW = 128
D_FF = 2816
N_BUCKETS, MAX_DISTANCE = 32, 1024
EPS, NEG = 1e-6, -1e30
TP = SEQ // P
T = TP + 1
TOK = T * P
KD = D_MODEL // P
KF = D_FF // P
QA, KA, VA = 0, 384, 512
QB, KB, VB = 640, 896, 1152
QC, KC, VC = 1408, 1792, 2176
FZ = 2560
N_IN = FZ + C_HEADS
IN_BLOCKS = [(QA, 512), (VA, 384), (KB, 512), (QC, 384), (KC, 384), (VC, 384 + C_HEADS)]
NORMED = [(0, 8, HEAD), (128, 8, B_DIM), (0, 8, B_DIM), (0, 6, HEAD), (0, 6, HEAD), None]
GAINS = [("q_norm_a", 0, 6, HEAD, HEAD ** -0.5), ("k_norm_a", 384, 2, HEAD, None),
         ("q_norm_b", 512, 8, B_DIM, B_DIM ** -0.5), ("k_norm_b", 768, 8, B_DIM, None),
         ("q_norm_c", 1024, 6, HEAD, HEAD ** -0.5), ("k_norm_c", 1408, 6, HEAD, None)]
GAIN_AT = [0, 512, 768, 1024, 1408]
REL0 = SEQ - 1 + P
REL = REL0 + P + 1

F32 = mybir.dt.float32
BF16 = mybir.dt.bfloat16
ALU = mybir.AluOpType
ACT = mybir.ActivationFunctionType
AX = mybir.AxisListType


def constants():
    i = np.arange(P)
    upper = (i[:, None] <= i[None, :]).astype(np.float32)
    same = (i[:, None] // DEC_SEQ == i[None, :] // DEC_SEQ)
    rel = np.arange(REL) - REL0
    n = np.abs(rel)
    half, exact = N_BUCKETS // 2, N_BUCKETS // 4
    large = exact + (np.log(np.maximum(n, 1).astype(np.float32) / exact)
                     / np.float32(np.log(MAX_DISTANCE / exact)) * (half - exact)).astype(np.int32)
    bucket = np.where(rel > 0, half, 0) + np.where(n < exact, n, np.minimum(large, half - 1))
    bh = np.arange(DEC_BATCH * C_HEADS)
    lam_init = 0.8 - 0.6 * np.exp(-0.3 * np.arange(DEPTH))
    return {
        "c_ident": np.eye(P, dtype=np.float32),
        "c_upper": np.concatenate([upper, np.ones((P, SEQ - P), np.float32)], 1),
        "c_upper_batch": upper * same,
        "c_causal": np.where(i[None, :] <= i[:, None], 0.0, NEG).astype(np.float32),
        "c_batch": np.where(same, 0.0, NEG).astype(np.float32),
        "c_batch_causal": np.where(same & (i[None, :] <= i[:, None]), 0.0, NEG).astype(np.float32),
        "c_buckets": (np.arange(N_BUCKETS)[:, None] == bucket[None, :]).astype(np.float32),
        "c_is_head": (bh[:, None] % C_HEADS == np.arange(C_HEADS)[None, :]).astype(np.float32),
        "c_is_batch": (bh[:, None] // C_HEADS == i[None, :] // DEC_SEQ).astype(np.float32),
        "c_lam": np.stack([lam_init, 1.0 - lam_init]).astype(np.float32),
    }


class Count:

    def __init__(self, sem, by=1):
        self.sem, self.by, self.n = sem, by, 0

    def on(self, instruction):
        self.n += self.by
        instruction.then_inc(self.sem, self.by)
        return self.n


class Phase:

    def __init__(self, nc, name):
        self.nc, self.name, self.ctx, self.sems = nc, name, ExitStack(), []

    def sb(self, name, shape, dt=F32):
        return self.ctx.enter_context(self.nc.sbuf_tensor(f"{self.name}_{name}", shape, dt))

    def ps(self, name, shape):
        return self.ctx.enter_context(self.nc.psum_tensor(f"{self.name}_{name}", shape, F32))

    def sem(self, name):
        s = self.ctx.enter_context(self.nc.semaphore(f"{self.name}_{name}"))
        self.sems.append(s)
        return s

    def close(self):
        with self.nc.Block() as block:
            @block.gpsimd
            def _(pool):
                for s in self.sems:
                    pool.sem_clear(s)
        self.ctx.close()


def rows(dram, offset, pattern):
    return bass.AP(dram.tensor, dram.offset + offset, pattern)


def build(nc, t):
    with ExitStack() as ctx:
        def sb(name, shape, dt=F32):
            return ctx.enter_context(nc.sbuf_tensor(name, shape, dt))

        k = {"x": sb("x", [P, T, D_MODEL]), "ident": sb("ident", [P, P]),
             "logf": sb("logf", [P, T, C_HEADS]), "cumq": sb("cumq", [P, T, C_HEADS]),
             "lam": sb("lam", [P, 1])}
        setup(nc, t, k)
        with nc.Fori(0, DEPTH) as layer:
            project(nc, t, k, layer)
            forget(nc, t, k, layer)
            mix_ctx = ExitStack()
            k["mixT"] = mix_ctx.enter_context(nc.sbuf_tensor("mixT", [P, KD, TOK], F32))
            for kind, groups in (("A", 3), ("B", 2), ("C", 3)):
                with nc.Fori(0, groups) as j:
                    attend(nc, t, k, layer, kind, j)
            mix(nc, t, k, layer)
            mix_ctx.close()
            feed(nc, t, k, layer)
        finish(nc, t, k)


def setup(nc, t, k):
    ph = Phase(nc, "set")
    heads = A_HEADS + B_HEADS
    table = ph.sb("table", [N_BUCKETS, heads])
    wide = ph.sb("wide", [N_BUCKETS, heads, P])
    buckets = ph.sb("buckets", [N_BUCKETS, REL])
    row = ph.sb("row", [P, 2, REL])
    tile_a = ph.sb("tile_a", [P, A_HEADS, 2 * P])
    tile_b = ph.sb("tile_b", [P, B_HEADS, SEQ])
    samp_a = ph.sb("samp_a", [P, A_HEADS, 2 * P])
    samp_b = ph.sb("samp_b", [P, B_HEADS, 3 * P])
    near = ph.sb("near", [P, heads, DEC_SEQ])
    batch = ph.sb("batch", [P, P])
    pr = ph.ps("pr", [P, 2, 3 * 512])
    loaded, widened, product, copied = ph.sem("loaded"), ph.sem("widened"), ph.sem("product"), ph.sem("copied")
    tiles_in, tiles_done, tiles_out = (ph.sem(n) for n in ("tiles_in", "tiles_done", "tiles_out"))
    rows_out = [ph.sem(f"rows_out{i}") for i in range(2)]
    x_in = ph.sem("x_in")
    cuts = [(c, min(c + 512, REL)) for c in range(0, REL, 512)]
    with nc.Block() as block:
        @block.sync
        def _(sp):
            sp.dma_start(table[:], t["rel_bias_table"]).then_inc(loaded, 16)
            sp.dma_start(buckets[:], t["c_buckets"]).then_inc(loaded, 16)
            sp.dma_start(batch[:], t["c_batch"]).then_inc(loaded, 16)
            sp.dma_start(k["ident"][:], t["c_ident"]).then_inc(x_in, 16)
            sp.dma_start(k["x"][:, 0:TP, :], t["x_prompt"].rearrange("a (t p) d -> p (a t) d", p=P)).then_inc(x_in, 16)
            sp.dma_start(k["x"][:, TP, :], t["x_sample"].rearrange("b s d -> (b s) d")).then_inc(x_in, 16)
            for h in range(heads):
                sp.wait_ge(copied, h + 1)
                sp.dma_start(t["bias_rows"][h], row[:, h % 2, :]).then_inc(rows_out[h % 2], 16)
            for out in rows_out:
                sp.wait_ge(out, 16 * heads // 2)
            skew = REL - 1
            for h in range(heads):
                at = h * P * REL + REL0
                if h < A_HEADS:
                    sp.dma_start(tile_a[:, h, :], rows(t["bias_rows"], at - P, [[skew, P], [1, 2 * P]])).then_inc(tiles_in, 16)
                    sp.dma_start(samp_a[:, h, 0:P], rows(t["bias_rows"], at - P, [[0, DEC_BATCH], [skew, DEC_SEQ], [1, P]])).then_inc(tiles_in, 16)
                else:
                    sp.dma_start(tile_b[:, h - A_HEADS, :], rows(t["bias_rows"], at - SEQ + P, [[skew, P], [1, SEQ]])).then_inc(tiles_in, 16)
                    sp.dma_start(samp_b[:, h - A_HEADS, 0:PAST], rows(t["bias_rows"], at - PAST, [[0, DEC_BATCH], [skew, DEC_SEQ], [1, PAST]])).then_inc(tiles_in, 16)
                sp.dma_start(near[:, h, :], rows(t["bias_rows"], at, [[0, DEC_BATCH], [skew, DEC_SEQ], [1, DEC_SEQ]])).then_inc(tiles_in, 16)
            sp.wait_ge(tiles_done, 4)
            sp.dma_start(t["bias_a"].rearrange("h p c -> p h c"), tile_a[:]).then_inc(tiles_out, 16)
            sp.dma_start(t["bias_b"].rearrange("h p c -> p h c"), tile_b[:]).then_inc(tiles_out, 16)
            sp.dma_start(t["bias_sa"].rearrange("h p c -> p h c"), samp_a[:]).then_inc(tiles_out, 16)
            sp.dma_start(t["bias_sb"].rearrange("h p c -> p h c"), samp_b[:]).then_inc(tiles_out, 16)
            sp.wait_ge(tiles_out, 64)
            sp.wait_ge(x_in, 48)

        @block.tensor
        def _(pe):
            pe.wait_ge(widened, 1)
            for h in range(heads):
                if h >= 2:
                    pe.wait_ge(copied, h - 1)
                for a, b in cuts:
                    last = pe.matmul(pr[:, h % 2, a:b], wide[:, h, :], buckets[:, a:b], start=True, stop=True)
                last.then_inc(product, 1)

        @block.vector
        def _(dve):
            dve.wait_ge(loaded, 48)
            dve.tensor_copy(wide[:], table[:].unsqueeze(2).broadcast_to([N_BUCKETS, heads, P])).then_inc(widened, 1)
            for h in range(heads):
                dve.wait_ge(product, h + 1)
                if h >= 2:
                    dve.wait_ge(rows_out[h % 2], 16 * (h // 2))
                dve.tensor_copy(row[:, h % 2, :], pr[:, h % 2, 0:REL]).then_inc(copied, 1)
            dve.wait_ge(tiles_in, 16 * 3 * heads)
            dve.memset(tile_a[0:64, :, 192:256], NEG).then_inc(tiles_done, 1)
            dve.memset(tile_a[64:128, :, 0:64], NEG).then_inc(tiles_done, 1)
            dve.memset(tile_b[0:64, :, SEQ - 64:SEQ], NEG).then_inc(tiles_done, 1)
            for h in range(heads):
                out = samp_a[:, h, P:2 * P] if h < A_HEADS else samp_b[:, h - A_HEADS, PAST:PAST + P]
                last = dve.tensor_tensor(out.rearrange("p (b s) -> p b s", b=DEC_BATCH),
                                         batch[:].rearrange("p (b s) -> p b s", b=DEC_BATCH),
                                         near[:, h, :].unsqueeze(1).broadcast_to([P, DEC_BATCH, DEC_SEQ]), ALU.add)
            last.then_inc(tiles_done, 1)
    ph.close()


def norm_transpose(ph, k, gain_row, hT):
    squares = ph.sb("squares", [P, D_MODEL])
    ms = ph.sb("ms", [P, T])
    root = ph.sb("root", [P, T])
    rstd = ph.sb("rstd", [P, T])
    xn = ph.sb("xn", [P, 2, D_MODEL])
    pt = ph.ps("pt", [P, 2, D_MODEL])
    summed, shifted, rooted, scaled = (ph.sem(n) for n in ("summed", "shifted", "rooted", "scaled"))
    normed, turned, ready = (ph.sem(n) for n in ("normed", "turned", "h_ready"))
    x = k["x"]

    def act(eng):
        for i in range(T):
            if i:
                eng.wait_ge(summed, i)
            eng.activation(squares[:], x[:, i, :], ACT.Square, accum_out=ms[:, i:i + 1]).then_inc(summed, 1)
        eng.wait_ge(shifted, 1)
        eng.activation(root[:], ms[:], ACT.Sqrt).then_inc(rooted, 1)
        eng.wait_ge(scaled, 1)
        for i in range(T):
            if i >= 2:
                eng.wait_ge(turned, i - 1)
            eng.activation(xn[:, i % 2, :], x[:, i, :], ACT.Copy, scale=rstd[:, i:i + 1]).then_inc(normed, 1)

    def dve(eng):
        eng.wait_ge(summed, T)
        eng.tensor_scalar(ms[:], ms[:], 1.0 / D_MODEL, EPS, ALU.mult, ALU.add).then_inc(shifted, 1)
        eng.wait_ge(rooted, 1)
        eng.reciprocal(rstd[:], root[:]).then_inc(scaled, 1)
        for i in range(T):
            eng.wait_ge(turned, i + 1)
            eng.tensor_tensor(hT[:, :, i * P:(i + 1) * P], pt[:, i % 2, :].rearrange("p (k n) -> p k n", k=KD),
                              gain_row[:].unsqueeze(2).broadcast_to([P, KD, P]), ALU.mult).then_inc(ready, 1)

    def pe(eng):
        for i in range(T):
            eng.wait_ge(normed, i + 1)
            if i >= 2:
                eng.wait_ge(ready, i - 1)
            for c in range(KD):
                last = eng.transpose(pt[:, i % 2, c * P:(c + 1) * P], xn[:, i % 2, c * P:(c + 1) * P], k["ident"][:])
            last.then_inc(turned, 1)

    return {"act": act, "dve": dve, "pe": pe, "ready": ready}


def stores(t, layer, block, i, nat):
    c0, n = IN_BLOCKS[block]
    n = min(n, FZ - c0)
    out = [(t["qkv"][i * P:(i + 1) * P, c0:c0 + n], nat[:, 0:n])]
    prompt, sample = i < TP, i == TP
    for first, count, name, shape in ((KA, 128, "a_k", "h d"), (VA, 128, "a_v", "h d"), (KB, 256, "b_k", "h m d"),
                                      (VB, 256, "b_v", "h d"), (KC, 384, "c_k", "h d"), (VC, 384, "c_v", "h d")):
        if not c0 <= first < c0 + n:
            continue
        src = nat[:, first - c0:first - c0 + count]
        flat = f"({shape})"
        if sample:
            dst = t["s_" + name][layer].rearrange(f"b s {shape} -> b s {flat}")
            if name[0] == "a":
                dst = dst[:, WINDOW - DEC_SEQ:WINDOW, :]
                for b in range(DEC_BATCH):
                    out.append((dst[b], src[b * DEC_SEQ:(b + 1) * DEC_SEQ, :]))
            else:
                out.append((dst.rearrange("b s n -> (b s) n"), src))
        elif name[0] != "a" or i == TP - 1:
            dst = t["p_" + name][layer, 0].rearrange(f"s {shape} -> s {flat}")
            out.append((dst if name[0] == "a" else dst[i * P:(i + 1) * P, :], src))
    return out


def project(nc, t, k, layer):
    ph = Phase(nc, "prj")
    hT = ph.sb("hT", [P, KD, TOK])
    gain = ph.sb("gain", [P, KD])
    w = ph.sb("w", [P, 2, KD, 512])
    qk_gain = ph.sb("qk_gain", [P, 1792])
    bf = ph.sb("bf", [P, C_HEADS])
    sq = ph.sb("sq", [P, 2, 512])
    ms, root, rstd = (ph.sb(n, [P, 2, 8]) for n in ("head_ms", "head_root", "head_rstd"))
    nat = ph.sb("nat", [P, 4, 512])
    z, z_abs, z_exp = (ph.sb(n, [P, T, C_HEADS]) for n in ("z", "z_abs", "z_exp"))
    acc = ph.ps("acc", [P, 4, 512])
    parts = norm_transpose(ph, k, gain, hT)
    g_in, w_even, w_odd, done = (ph.sem(n) for n in ("g_in", "w_even", "w_odd", "done"))
    w_in = (w_even, w_odd)
    squared, summed_h, shifted_h, rooted_h, inverse_h, gained, made = (
        ph.sem(n) for n in ("squared", "summed_h", "shifted_h", "rooted_h", "inverse_h", "gained", "made"))
    stored = [ph.sem(f"stored{i}") for i in range(4)]
    scaled_q, f_sum, f_abs, f_exp, f_ln, f_out, f_stored, rolled = (
        ph.sem(n) for n in ("scaled_q", "f_sum", "f_abs", "f_exp", "f_ln", "f_out", "f_stored", "rolled"))
    work = [(b, i) for b in range(len(IN_BLOCKS)) for i in range(T)]
    n_stores = [len(stores(t, layer, b, i, nat[:, 0, :])) for b, i in work]
    src = t["w_in"][layer].rearrange("(k p) n -> p k n", p=P)

    def stored_by(u):
        return 16 * sum(n_stores[v] for v in range(u % 4, u + 1, 4))

    with nc.Block() as block:
        @block.sync
        def _(sp):
            with nc.allow_non_contiguous_dma(reason="gain vectors"):
                sp.dma_start(gain[:], t["norm_mix"][layer].rearrange("(k p) -> p k", p=P)).then_inc(g_in, 16)
            for name, c, heads, width, _ in GAINS:
                sp.dma_start(qk_gain[:, c:c + heads * width].rearrange("p (h d) -> p h d", d=width),
                             t[name][layer].unsqueeze(0).unsqueeze(0).broadcast_to([P, heads, width])).then_inc(g_in, 16)
            sp.dma_start(bf[:], t["b_forget"][layer].unsqueeze(0).broadcast_to([P, C_HEADS])).then_inc(g_in, 16)
            for kv in "kv":
                sp.dma_start(t[f"s_a_{kv}"][layer, :, 0:WINDOW - DEC_SEQ], t[f"cache_a_{kv}"][layer, :, DEC_SEQ:WINDOW]).then_inc(rolled, 16)
            for u, (b, i) in enumerate(work):
                if NORMED[b]:
                    sp.wait_ge(made, sum(bool(NORMED[v[0]]) for v in work[:u + 1]))
                else:
                    sp.wait_ge(gained, u + 1)
                for dst, rows_ in stores(t, layer, b, i, nat[:, u % 4, :]):
                    sp.dma_start(dst, rows_).then_inc(stored[u % 4], 16)
            for u in range(len(work) - 4, len(work)):
                sp.wait_ge(stored[u % 4], stored_by(u))
            sp.wait_ge(rolled, 32)
            sp.wait_ge(f_out, 1)
            sp.dma_start(t["p_c_logf"][layer, 0].rearrange("(t p) h -> p t h", p=P), k["logf"][:, 0:TP, :]).then_inc(f_stored, 16)
            sp.dma_start(t["s_c_logf"][layer].rearrange("b s h -> (b s) h"), k["logf"][:, TP, :]).then_inc(f_stored, 16)
            sp.wait_ge(f_stored, 32)

        @block.tensor
        def _(pe):
            parts["pe"](pe)
            pe.wait_ge(parts["ready"], T)
            for u, (b, i) in enumerate(work):
                n = IN_BLOCKS[b][1]
                if i == 0:
                    pe.wait_ge(w_in[b % 2], 16 * (b // 2 + 1))
                if u >= 4:
                    pe.wait_ge(gained, u - 3)
                for c in range(KD):
                    last = pe.matmul(acc[:, u % 4, 0:n], hT[:, c, i * P:(i + 1) * P], w[:, b % 2, c, 0:n],
                                     start=(c == 0), stop=(c == KD - 1))
                last.then_inc(done, 1)

        @block.scalar
        def _(act):

            def load_w(b):
                c, n = IN_BLOCKS[b]
                act.dma_start(w[:, b % 2, :, 0:n], src[:, :, c:c + n]).then_inc(w_in[b % 2], 16)

            load_w(0)
            load_w(1)
            parts["act"](act)
            m = 0
            for u, (b, i) in enumerate(work):
                if i == 0 and 1 <= b < len(IN_BLOCKS) - 1:
                    act.wait_ge(done, u)
                    load_w(b + 1)
                if not NORMED[b]:
                    continue
                c, heads, width = NORMED[b]
                span = slice(c, c + heads * width)
                act.wait_ge(done, u + 1)
                if m >= 2:
                    act.wait_ge(summed_h, m - 1)
                act.activation(sq[:, m % 2, span], acc[:, u % 4, span], ACT.Square).then_inc(squared, 1)
                act.wait_ge(shifted_h, m + 1)
                if m >= 2:
                    act.wait_ge(inverse_h, m - 1)
                act.activation(root[:, m % 2, 0:heads], ms[:, m % 2, 0:heads], ACT.Sqrt).then_inc(rooted_h, 1)
                m += 1
            act.wait_ge(f_abs, 1)
            act.activation(z_exp[:], z_abs[:], ACT.Exp, scale=-1.0).then_inc(f_exp, 1)
            act.wait_ge(f_exp, 1)
            act.activation(z_abs[:], z_exp[:], ACT.Ln, bias=1.0).then_inc(f_ln, 1)

        @block.vector
        def _(dve):
            dve.wait_ge(g_in, 128)
            parts["dve"](dve)
            for name, c, heads, width, scale in GAINS:
                if scale:
                    span = qk_gain[:, c:c + heads * width]
                    last = dve.tensor_scalar(span, span, scale, None, ALU.mult)
            last.then_inc(scaled_q, 1)
            dve.wait_ge(scaled_q, 1)

            def read_out(u, m):
                b, i = work[u]
                n = IN_BLOCKS[b][1]
                dve.wait_ge(done, u + 1)
                if u >= 4:
                    dve.wait_ge(stored[u % 4], stored_by(u - 4))
                if not NORMED[b]:
                    dve.tensor_tensor(z[:, i, :], acc[:, u % 4, n - C_HEADS:n], bf[:], ALU.add).then_inc(f_sum, 1)
                    dve.tensor_copy(nat[:, u % 4, 0:n - C_HEADS], acc[:, u % 4, 0:n - C_HEADS]).then_inc(gained, 1)
                    return
                c, heads, width = NORMED[b]
                e = c + heads * width
                dve.wait_ge(squared, m + 1)
                for a_, e_ in ((0, c), (e, n)):
                    if a_ < e_:
                        dve.tensor_copy(nat[:, u % 4, a_:e_], acc[:, u % 4, a_:e_])
                g = GAIN_AT[b]
                dve.tensor_tensor(nat[:, u % 4, c:e], acc[:, u % 4, c:e], qk_gain[:, g:g + heads * width], ALU.mult).then_inc(gained, 1)
                dve.tensor_reduce(ms[:, m % 2, 0:heads], sq[:, m % 2, c:e].rearrange("p (h d) -> p h d", d=width), AX.X, ALU.add).then_inc(summed_h, 1)
                dve.wait_ge(summed_h, m + 1)
                dve.tensor_scalar(ms[:, m % 2, 0:heads], ms[:, m % 2, 0:heads], 1.0 / width, EPS, ALU.mult, ALU.add).then_inc(shifted_h, 1)

            def finish_rows(u, m):
                b, i = work[u]
                n = IN_BLOCKS[b][1]
                dve.wait_ge(gained, u + 1)
                if not NORMED[b]:
                    return
                c, heads, width = NORMED[b]
                dve.wait_ge(rooted_h, m + 1)
                dve.reciprocal(rstd[:, m % 2, 0:heads], root[:, m % 2, 0:heads]).then_inc(inverse_h, 1)
                dve.wait_ge(inverse_h, m + 1)
                view = nat[:, u % 4, c:c + heads * width].rearrange("p (h d) -> p h d", d=width)
                dve.tensor_tensor(view, view, rstd[:, m % 2, 0:heads].unsqueeze(2).broadcast_to([P, heads, width]), ALU.mult).then_inc(made, 1)

            order = [sum(bool(NORMED[v[0]]) for v in work[:u]) for u in range(len(work))]
            for u in range(len(work) + 1):
                if u < len(work):
                    read_out(u, order[u])
                if u >= 1:
                    finish_rows(u - 1, order[u - 1])
            dve.wait_ge(f_sum, T)
            dve.scalar_tensor_tensor(out=z_abs[:], in0=z[:], scalar=-1.0, in1=z[:], op0=ALU.mult, op1=ALU.max).then_inc(f_abs, 1)
            dve.wait_ge(f_ln, 1)
            dve.scalar_tensor_tensor(out=k["logf"][:], in0=z[:], scalar=0.0, in1=z_abs[:], op0=ALU.min, op1=ALU.subtract).then_inc(f_out, 1)
    ph.close()


def forget(nc, t, k, layer):
    ph = Phase(nc, "fgt")
    BH = DEC_BATCH * C_HEADS
    upper = ph.sb("upper", [P, SEQ])
    batch_upper = ph.sb("batch_upper", [P, P])
    is_head = ph.sb("is_head", [BH, C_HEADS])
    is_batch = ph.sb("is_batch", [BH, P])
    past = ph.sb("past", [P, 2, BH])
    total = ph.sb("total", [BH, P])
    past_row = ph.sb("past_row", [BH, PAST])
    prompt_row = ph.sb("prompt_row", [C_HEADS, SEQ])
    new_row = ph.sb("new_row", [C_HEADS, P])
    lams = ph.sb("lams", [P, 4, B_DIM])
    lam_c = ph.sb("lam_c", [P, 1])
    lam_x = ph.sb("lam_x", [P, 2, B_DIM])
    lam_s = ph.sb("lam_s", [P, 2])
    lam_e = ph.sb("lam_e", [P, 2])
    cols = ph.ps("cols", [P, 512])
    prow = ph.ps("prow", [P, SEQ])
    srow = ph.ps("srow", [P, 512])
    nrow = ph.ps("nrow", [P, 512])
    loaded, sums, past_sum, totals, negated, stored = (ph.sem(n) for n in ("loaded", "sums", "past_sum", "totals", "negated", "stored"))
    lam_prod, lam_exp, lam_diff = (ph.sem(n) for n in ("lam_prod", "lam_exp", "lam_diff"))
    logf = k["logf"]
    with nc.Block() as block:
        @block.sync
        def _(sp):
            sp.dma_start(upper[:], t["c_upper"]).then_inc(loaded, 16)
            sp.dma_start(batch_upper[:], t["c_upper_batch"]).then_inc(loaded, 16)
            sp.dma_start(is_head[:], t["c_is_head"]).then_inc(loaded, 16)
            sp.dma_start(is_batch[:], t["c_is_batch"]).then_inc(loaded, 16)
            with nc.allow_non_contiguous_dma(reason="six gates per position"):
                for half in range(2):
                    sp.dma_start(past[:, half, :].rearrange("p (b h) -> p b h", b=DEC_BATCH),
                                 t["cache_c_logf"][layer, :, half * P:(half + 1) * P, :].rearrange("b p h -> p b h")).then_inc(loaded, 16)
            for n, name in enumerate(("lam_q1", "lam_k1", "lam_q2", "lam_k2")):
                sp.dma_start(lams[:, n, :], t[name][layer].unsqueeze(0).broadcast_to([P, B_DIM])).then_inc(loaded, 16)
            sp.dma_start(lam_c[:], t["c_lam"][0:1, bass.ds(layer, 1)].broadcast_to([P, 1])).then_inc(loaded, 16)
            sp.wait_ge(negated, 3)
            sp.dma_start(t["cum_prompt"], prompt_row[:]).then_inc(stored, 16)
            sp.dma_start(t["cum_past"], past_row[:]).then_inc(stored, 16)
            sp.dma_start(t["cum_new"], new_row[:]).then_inc(stored, 16)
            sp.wait_ge(stored, 48)

        @block.tensor
        def _(pe):
            pe.wait_ge(loaded, 16 * 11)
            pe.matmul(srow[0:BH, 0:PAST], past[:, 0, :], upper[:, 0:PAST], start=True, stop=False)
            pe.matmul(srow[0:BH, P:PAST], past[:, 1, :], upper[:, 0:P], start=False, stop=True).then_inc(past_sum, 1)
            for i in range(TP):
                for c in range(i * P // 512, 2):
                    a = max(i * P, c * 512)
                    pe.matmul(prow[0:C_HEADS, a:(c + 1) * 512], logf[:, i, :], upper[:, a - i * P:(c + 1) * 512 - i * P],
                              start=(i == 0), stop=(i == 4 * c + 3))
            for i in range(TP):
                for j in range(i + 1):
                    pe.matmul(cols[:, i * C_HEADS:(i + 1) * C_HEADS], upper[:, 0:P] if j == i else upper[:, P:2 * P],
                              logf[:, j, :], start=(j == 0), stop=(j == i))
            pe.wait_ge(totals, 1)
            pe.matmul(cols[:, TP * C_HEADS:T * C_HEADS], batch_upper[:], logf[:, TP, :], start=True, stop=False)
            pe.matmul(cols[:, TP * C_HEADS:T * C_HEADS], total[:], is_head[:], start=False, stop=True)
            pe.matmul(nrow[0:C_HEADS, 0:P], logf[:, TP, :], batch_upper[:], start=True, stop=False)
            pe.matmul(nrow[0:C_HEADS, 0:P], is_head[:], total[:], start=False, stop=True).then_inc(sums, 1)

        @block.scalar
        def _(act):
            act.wait_ge(lam_prod, 1)
            act.activation(lam_e[:], lam_s[:], ACT.Exp).then_inc(lam_exp, 1)

        @block.vector
        def _(dve):
            dve.wait_ge(past_sum, 1)
            dve.tensor_scalar(total[:], is_batch[:], srow[0:BH, PAST - 1:PAST], None, ALU.mult).then_inc(totals, 1)
            for n in range(2):
                last = dve.tensor_tensor_reduce(lam_x[:, n, :], lams[:, 2 * n, :], lams[:, 2 * n + 1, :], 1.0, 0.0, ALU.mult, ALU.add, lam_s[:, n:n + 1])
            last.then_inc(lam_prod, 1)
            dve.wait_ge(lam_exp, 1)
            dve.tensor_tensor(lam_s[:, 0:1], lam_e[:, 0:1], lam_e[:, 1:2], ALU.subtract).then_inc(lam_diff, 1)
            dve.wait_ge(lam_diff, 1)
            dve.tensor_tensor(k["lam"][:], lam_s[:, 0:1], lam_c[:], ALU.add).then_inc(lam_diff, 1)
            dve.tensor_scalar(past_row[:], srow[0:BH, 0:PAST], -1.0, None, ALU.mult).then_inc(negated, 1)
            dve.wait_ge(sums, 1)
            dve.tensor_scalar(prompt_row[:], prow[0:C_HEADS, :], -1.0, None, ALU.mult).then_inc(negated, 1)
            dve.tensor_copy(k["cumq"][:], cols[:, 0:T * C_HEADS].rearrange("p (t h) -> p t h", t=T))
            dve.tensor_scalar(new_row[:], nrow[0:C_HEADS, 0:P], -1.0, None, ALU.mult).then_inc(negated, 1)
    ph.close()


def attend(nc, t, k, layer, kind, j):
    ph = Phase(nc, "at" + kind)
    D = B_DIM if kind == "B" else HEAD
    maps = P // D
    per_head = maps // 2
    packed = P // D
    nb = DEC_BATCH // packed
    halves = 1 if kind == "A" else PAST // P
    n_past = halves * P
    n_samp = n_past + P
    width = 2 * P if kind == "A" else SEQ
    qn, kn, vn, mixn = (ph.sb(n, [P, T, P]) for n in ("qn", "kn", "vn", "mixn"))
    kp = ph.sb("kp", [P, halves, DEC_BATCH, P])
    vp = ph.sb("vp", [P, halves, DEC_BATCH, P])
    kpm = ph.sb("kpm", [P, halves, maps, DEC_BATCH, D])
    n_q = maps if kind == "B" else 1
    qT = ph.sb("qT", [P, n_q, TOK])
    kT = ph.sb("kT", [P, TOK])
    qpast = ph.sb("qpast", [P, maps, nb, P])
    kpT = ph.sb("kpT", [P, maps * nb, n_past])
    add_p = ph.sb("add_p", [P, 2, width])
    add_s = ph.sb("add_s", [P, 2, n_samp])
    s = ph.sb("s", [P, 2, width])
    p = ph.sb("p", [P, 2, per_head, width])
    pT = ph.sb("pT", [P, 2, width])
    oT = ph.sb("oT", [HEAD, P])
    NJ = 2 * per_head * T
    mx, bias, total, inv = (ph.sb(n, [P, NJ]) for n in ("mx", "bias", "total", "inv"))
    coef = ph.sb("coef", [P, 2 * T])
    if kind == "A":
        sink, esink = ph.sb("sink", [P, 2]), ph.sb("esink", [P, NJ])
    if kind == "C":
        cumq = ph.sb("cumq", [P, T, 2])
        mask_f, mask_s = ph.sb("mask_f", [P, P]), ph.sb("mask_s", [P, P])
        mask_b, ident_b = ph.sb("mask_b", [P, P], BF16), ph.sb("ident_b", [P, P], BF16)
    if kind == "B":
        neg_lam, keep = ph.sb("neg_lam", [P, 1]), ph.sb("keep", [P, 1])
        subln = ph.sb("subln", [P, HEAD])
        sub_sq = ph.sb("sub_sq", [P, T, P])
        sub_ms, sub_root = ph.sb("sub_ms", [P, 2 * T]), ph.sb("sub_root", [P, 2 * T])
    S = ph.ps("S", [P, 2, 1024])
    TR = ph.ps("TR", [P, 2, 512])
    O = ph.ps("O", [P, 2, 512])

    q_in, k_in, v_in, kp_in, vp_in, add_in, more_in = (
        ph.sem(n) for n in ("q_in", "k_in", "v_in", "kp_in", "vp_in", "add_in", "more_in"))
    zeroed, regrouped, turned0, taken_v, taken_s, prepared = (
        ph.sem(n) for n in ("zeroed", "regrouped", "turned0", "taken_v", "taken_s", "prepared"))
    scored, biased, bias_ready, exped, sink_ready, inv_ready, coef_ready, weighed, normed = (
        ph.sem(n) for n in ("scored", "biased", "bias_ready", "exped", "sink_ready", "inv_ready", "coef_ready", "weighed", "normed"))
    turned, evacuated, multiplied, oT_ready, turned_back, taken_out = (
        ph.sem(n) for n in ("turned", "evacuated", "multiplied", "oT_ready", "turned_back", "taken_out"))
    steps, sub_squared, sub_rooted, sub_done, mix_turned, mix_taken = (
        ph.sem(n) for n in ("steps", "sub_squared", "sub_rooted", "sub_done", "mix_turned", "mix_taken"))
    g = {"A": 0, "B": 3, "C": 5}[kind] + j

    units = [(h, i) for h in range(2) for i in range(T)]
    NU = len(units)

    def keys(i):
        return list(range(max(i - 1, 0) if kind == "A" else 0, i + 1))

    def n_cols(i):
        return n_samp if i == TP else P * len(keys(i))

    def n_chunks(i):
        return -(-n_cols(i) // 512)

    chunks_to = [sum(n_chunks(i) for _, i in units[:u]) for u in range(NU + 1)]
    samples_to = [sum(i == TP for _, i in units[:u]) for u in range(NU + 1)]
    q_batches = [(0, 4), (4, 8), (8, 9)]
    first = [("q", a, e) for a, e in q_batches] + [("k", a, e) for a, e in q_batches] + [("p", n, n + 2) for n in range(0, maps * nb, 2)]
    v_batches = [n for n, f in enumerate(first) if f[0] != "p"]
    s_batches = [n for n, f in enumerate(first) if f[0] == "p"]

    def bank(n):
        return S[:, n % 4 // 2, n % 2 * 512:n % 2 * 512 + 512]

    with nc.Block() as block:
        @block.sync
        def _(sp):
            qkv = t["qkv"].rearrange("(t p) n -> p t n", p=P)
            if kind == "A":
                for h in range(2):
                    sp.dma_start(qn[:, :, h * HEAD:(h + 1) * HEAD], qkv[:, :, bass.ds(j * HEAD + 3 * h * HEAD, HEAD)]).then_inc(q_in, 8 * 2)
                sp.dma_start(kn[:], qkv[:, :, KA:KA + P]).then_inc(k_in, 16)
                sp.dma_start(vn[:], qkv[:, :, VA:VA + P]).then_inc(v_in, 16)
            else:
                cq, ck, cv = (QB, KB, VB) if kind == "B" else (QC, KC, VC)
                sp.dma_start(qn[:], qkv[:, :, bass.ds(j * P + cq, P)]).then_inc(q_in, 16)
                sp.dma_start(kn[:], qkv[:, :, bass.ds(j * P + ck, P)]).then_inc(k_in, 16)
                sp.dma_start(vn[:], qkv[:, :, bass.ds(j * P + cv, P)]).then_inc(v_in, 16)
            low = kind.lower()
            for name, dst, sem in (("k", kp, kp_in), ("v", vp, vp_in)):
                src = t[f"cache_{low}_{name}"][layer]
                src = src.rearrange("b p h m d -> p b (h m d)") if kind == "B" and name == "k" else src.rearrange("b p h d -> p b (h d)")
                for f in range(halves):
                    part = src[f * P:(f + 1) * P, :, :] if kind == "A" else src[f * P:(f + 1) * P, :, bass.ds(j * P, P)]
                    sp.dma_start(dst[:, f, :, :], part).then_inc(sem, 16)
            for h in range(2):
                if kind == "A":
                    sp.dma_start(add_p[:, h, :], t["bias_a"][bass.ds(j + 3 * h, 1)].rearrange("h p c -> p (h c)")).then_inc(add_in, 16)
                    sp.dma_start(add_s[:, h, :], t["bias_sa"][bass.ds(j + 3 * h, 1)].rearrange("h p c -> p (h c)")).then_inc(add_in, 16)
                    sp.dma_start(sink[:, h:h + 1], t["sinks_a"][bass.ds(layer, 1), bass.ds(j + 3 * h, 1)].broadcast_to([P, 1])).then_inc(more_in, 16)
                elif kind == "B":
                    sp.dma_start(add_p[:, h, :], t["bias_b"][bass.ds(2 * j + h, 1)].rearrange("h p c -> p (h c)")).then_inc(add_in, 16)
                    sp.dma_start(add_s[:, h, :], t["bias_sb"][bass.ds(2 * j + h, 1)].rearrange("h p c -> p (h c)")).then_inc(add_in, 16)
                else:
                    sp.dma_start(add_p[:, h, :], t["cum_prompt"][bass.ds(2 * j + h, 1), :].broadcast_to([P, SEQ])).then_inc(add_in, 16)
                    past = t["cum_past"].rearrange("(b h) n -> b h n", h=C_HEADS)[:, bass.ds(2 * j + h, 1), :]
                    sp.dma_start(add_s[:, h, 0:PAST], past.broadcast_to([DEC_BATCH, DEC_SEQ, PAST])).then_inc(add_in, 16)
                    sp.dma_start(add_s[:, h, PAST:n_samp], t["cum_new"][bass.ds(2 * j + h, 1), :].broadcast_to([P, P])).then_inc(add_in, 16)
            if kind == "B":
                sp.dma_start(subln[:], t["subln_b"][layer].unsqueeze(0).broadcast_to([P, HEAD])).then_inc(more_in, 16)
                sp.dma_start(keep[:], t["c_lam"][1:2, bass.ds(layer, 1)].broadcast_to([P, 1])).then_inc(more_in, 16)
            if kind == "C":
                sp.dma_start(mask_f[:], t["c_causal"]).then_inc(more_in, 16)
                sp.dma_start(mask_s[:], t["c_batch_causal"]).then_inc(more_in, 16)

        n_add = 16 * (6 if kind == "C" else 4)

        @block.gpsimd
        def _(pool):
            pool.memset(qpast[:], 0.0).then_inc(zeroed, 1)
            if kind == "B":
                pool.memset(qT[:], 0.0).then_inc(zeroed, 1)
            pool.wait_ge(kp_in, 16 * halves)
            for f in range(halves):
                for m in range(maps):
                    last = pool.tensor_copy(kpm[:, f, m, :, :], kp[:, f, :, m * D:(m + 1) * D])
            last.then_inc(regrouped, 1)

        @block.tensor
        def _(pe):
            def turn_first(n):
                what, a, e = first[n]
                if n >= 4:
                    if first[n - 4][0] == "p":
                        pe.wait_ge(taken_s, s_batches.index(n - 4) + 1)
                    else:
                        pe.wait_ge(taken_v, v_batches.index(n - 4) + 1)
                        if n - 4 == 2:
                            pe.wait_ge(taken_s, 1)
                if what == "p":
                    for x in range(a, e):
                        m, c = divmod(x, nb)
                        for f in range(halves):
                            last = pe.transpose(bank(n)[:, (x - a) * n_past + f * P:(x - a) * n_past + (f + 1) * P],
                                                kpm[:, f, m, c * packed:(c + 1) * packed, :].rearrange("p b d -> p (b d)"), k["ident"][:])
                else:
                    for x in range(a, e):
                        last = pe.transpose(bank(n)[:, (x - a) * P:(x - a + 1) * P], (qn if what == "q" else kn)[:, x, :], k["ident"][:])
                last.then_inc(turned0, 1)

            def q_of(m, i):
                cols = slice(i * P, (i + 1) * P)
                return qT[:, m, cols] if kind == "B" else qT[m * D:(m + 1) * D, 0, cols]

            def k_of(m, a, e):
                return kT[:, a:e] if kind == "B" else kT[m * D:(m + 1) * D, a:e]

            def score(job):
                u, r = divmod(job, per_head)
                h, i = units[u]
                m = h * per_head + r
                if job >= 2:
                    pe.wait_ge(biased, job - 1)
                out = S[:, job % 2, :]
                if i < TP:
                    k0, n = keys(i)[0] * P, n_cols(i)
                    for c in range(0, n, 512):
                        w = min(512, n - c)
                        diagonal = kind == "C" and c + w == n
                        last = pe.matmul(out[:, c:c + w], q_of(m, i), k_of(m, k0 + c, k0 + c + w), start=True, stop=not diagonal)
                    if kind == "C":
                        last = pe.matmul(out[:, n - P:n], ident_b[:], mask_b[:], start=False, stop=True)
                else:
                    for c in range(nb):
                        pe.matmul(out[:, 0:n_past], qpast[:, m, c, :], kpT[:, m * nb + c, :], start=(c == 0), stop=(c == nb - 1))
                    last = pe.matmul(out[:, n_past:n_samp], q_of(m, TP), k_of(m, SEQ, TOK), start=True, stop=True)
                last.then_inc(scored, 1)

            def turn(u):
                h, i = units[u]
                if i == TP:
                    pe.wait_ge(normed, samples_to[u + 1])
                elif kind == "B":
                    pe.wait_ge(weighed, u + 1)
                else:
                    pe.wait_ge(exped, u + 1)
                for c in range(n_chunks(i)):
                    cc = chunks_to[u] + c
                    if cc >= 2:
                        pe.wait_ge(evacuated, cc - 1)
                    for x in range(4 * c, min(4 * c + 4, n_cols(i) // P)):
                        last = pe.transpose(TR[:, cc % 2, x % 4 * P:(x % 4 + 1) * P], p[:, u % 2, 0, x * P:(x + 1) * P], k["ident"][:])
                    last.then_inc(turned, 1)

            def values(u):
                h, i = units[u]
                pe.wait_ge(evacuated, chunks_to[u + 1])
                if u >= 2:
                    pe.wait_ge(taken_out, u - 1)
                v = slice(h * HEAD, (h + 1) * HEAD)
                if i < TP:
                    ks = keys(i)
                    for x, kt in enumerate(ks):
                        last = pe.matmul(O[:, u % 2, 0:HEAD], pT[:, u % 2, x * P:(x + 1) * P], vn[:, kt, v],
                                         start=(x == 0), stop=(x == len(ks) - 1))
                else:
                    last = pe.matmul(O[0:HEAD, u % 2, 0:P], vn[:, TP, v], pT[:, u % 2, n_past:n_samp], start=True, stop=False,
                                     skip_group_check=True)
                    for b in range(DEC_BATCH):
                        for f in range(halves):
                            own = slice(b * DEC_SEQ, (b + 1) * DEC_SEQ)
                            last = pe.matmul(O[0:HEAD, u % 2, own], vp[:, f, b, v], pT[:, u % 2, f * P + b * DEC_SEQ:f * P + (b + 1) * DEC_SEQ],
                                             start=False, stop=(b == DEC_BATCH - 1 and f == halves - 1), skip_group_check=True)
                last.then_inc(multiplied, 1)

            def turn_back(u):
                if units[u][1] == TP:
                    pe.wait_ge(oT_ready, samples_to[u + 1])
                    pe.transpose(O[:, u % 2, P:P + HEAD], oT[:], k["ident"][0:HEAD, 0:HEAD]).then_inc(turned_back, 1)

            pe.wait_ge(q_in, 32 if kind == "A" else 16)
            for n in range(3):
                turn_first(n)
            pe.wait_ge(k_in, 16)
            for n in range(3, 6):
                turn_first(n)
            pe.wait_ge(regrouped, 1)
            for n in range(6, len(first)):
                turn_first(n)
            pe.wait_ge(taken_v, len(v_batches))
            pe.wait_ge(taken_s, 1 + len(s_batches))
            pe.wait_ge(v_in, 16)
            pe.wait_ge(vp_in, 16 * halves)
            if kind == "C":
                pe.wait_ge(prepared, 1)
            for u in range(NU + 3):
                if u < NU:
                    for r in range(per_head):
                        score(u * per_head + r)
                if 1 <= u <= NU:
                    turn(u - 1)
                if 2 <= u <= NU + 1:
                    values(u - 2)
                if u >= 3:
                    turn_back(u - 3)
            pe.wait_ge(sub_done if kind == "B" else taken_out, 1 if kind == "B" else NU)
            for n, (a, e) in enumerate(q_batches):
                for x in range(a, e):
                    last = pe.transpose(bank(n)[:, (x - a) * P:(x - a + 1) * P], mixn[:, x, :], k["ident"][:])
                last.then_inc(mix_turned, 1)

        @block.scalar
        def _(act):
            act.wait_ge(turned0, 3)
            act.wait_ge(zeroed, 1)
            for m in range(maps):
                for r in range(packed):
                    own = slice(r * DEC_SEQ, (r + 1) * DEC_SEQ)
                    dst = qpast[r * D:(r + 1) * D, m, 0, own]
                    dst = bass.AP(dst.tensor, dst.offset, [list(dst.ap[0]), [P + packed * DEC_SEQ, nb], [1, DEC_SEQ]])
                    src = bank(2)[m * D:(m + 1) * D, 0:P].rearrange("p (c r s) -> p c r s", c=nb, r=packed)[:, :, r, :]
                    last = act.activation(dst, src, ACT.Copy)
            last.then_inc(taken_s, 1)
            for n in s_batches:
                a, e = first[n][1:]
                act.wait_ge(turned0, n + 1)
                act.activation(kpT[:, a:e, :], bank(n)[:, 0:(e - a) * n_past].rearrange("p (x n) -> p x n", n=n_past), ACT.Copy).then_inc(taken_s, 1)

            def exps(u):
                h, i = units[u]
                n = n_cols(i)
                if u >= 2:
                    act.wait_ge(turned, chunks_to[u - 1])
                for r in range(per_head):
                    job = u * per_head + r
                    act.wait_ge(bias_ready, job + 1)
                    if kind == "A":
                        act.activation(esink[:, job:job + 1], sink[:, h:h + 1], ACT.Exp, bias=bias[:, job:job + 1]).then_inc(sink_ready, 1)
                    act.activation(p[:, u % 2, r, 0:n], s[:, job % 2, 0:n], ACT.Exp, bias=bias[:, job:job + 1],
                                   accum_out=total[:, job:job + 1]).then_inc(exped, 1)

            def evacuate(u):
                h, i = units[u]
                for c in range(n_chunks(i)):
                    act.wait_ge(turned, chunks_to[u] + c + 1)
                    if u >= 2 and c == 0:
                        act.wait_ge(multiplied, u - 1)
                    w = min(512, n_cols(i) - c * 512)
                    act.activation(pT[:, u % 2, c * 512:c * 512 + w], TR[:, (chunks_to[u] + c) % 2, 0:w], ACT.Copy).then_inc(evacuated, 1)

            def take_oT(u):
                if units[u][1] == TP:
                    act.wait_ge(multiplied, u + 1)
                    if samples_to[u]:
                        act.wait_ge(turned_back, samples_to[u])
                    act.activation(oT[:], O[0:HEAD, u % 2, 0:P], ACT.Copy).then_inc(oT_ready, 1)

            for u in range(NU + 3):
                if u < NU:
                    exps(u)
                if 1 <= u <= NU:
                    evacuate(u - 1)
                if 2 <= u <= NU + 1:
                    take_oT(u - 2)
            if kind == "B":
                act.wait_ge(taken_out, NU)
                act.activation(sub_sq[:], mixn[:], ACT.Square).then_inc(sub_squared, 1)
                act.wait_ge(sub_squared, 2)
                act.activation(sub_root[:], sub_ms[:], ACT.Sqrt).then_inc(sub_rooted, 1)
            for n, (a, e) in enumerate(q_batches):
                act.wait_ge(mix_turned, n + 1)
                act.activation(k["mixT"][:, bass.ds(g, 1), a * P:e * P], bank(n)[:, 0:(e - a) * P].unsqueeze(1), ACT.Copy).then_inc(mix_taken, 1)

        @block.vector
        def _(dve):
            chain = Count(steps)

            def then(ins):
                dve.wait_ge(steps, chain.on(ins))

            if kind == "B":
                dve.wait_ge(zeroed, 2)
            for x, n in enumerate(v_batches):
                what, a, e = first[n]
                cols, src = slice(a * P, e * P), bank(n)[:, 0:(e - a) * P]
                dve.wait_ge(turned0, n + 1)
                if n == 2:
                    dve.wait_ge(taken_s, 1)
                if what == "k":
                    last = dve.tensor_copy(kT[:, cols], src)
                elif kind != "B":
                    last = dve.tensor_copy(qT[:, 0, cols], src)
                else:
                    for m in range(maps):
                        own = slice(m * D, (m + 1) * D)
                        last = dve.tensor_copy(qT[own, m, cols], src[own, :])
                last.then_inc(taken_v, 1)
            n_more = {"A": 2, "B": 2, "C": 2}[kind]
            dve.wait_ge(more_in, 16 * n_more)
            dve.wait_ge(add_in, n_add)
            if kind == "B":
                then(dve.tensor_scalar(neg_lam[:], k["lam"][:], -1.0, None, ALU.mult))
                then(dve.tensor_scalar(subln[:], subln[:], keep[:, 0:1], None, ALU.mult))
            if kind == "C":
                dve.tensor_copy(mask_b[:], mask_f[:])
                dve.tensor_copy(ident_b[:], k["ident"][:]).then_inc(prepared, 1)
                then(dve.tensor_copy(cumq[:], k["cumq"][:, :, bass.ds(2 * j, 2)]))
                for h in range(2):
                    last = dve.tensor_tensor(add_s[:, h, PAST:n_samp], add_s[:, h, PAST:n_samp], mask_s[:], ALU.add)
                then(last)

            def front(u):
                h, i = units[u]
                n = n_cols(i)
                for r in range(per_head):
                    job = u * per_head + r
                    dve.wait_ge(scored, job + 1)
                    if job >= 2:
                        dve.wait_ge(exped, job - 1)
                    extra = add_s[:, h, 0:n] if i == TP else add_p[:, h, 0:n] if kind == "C" else add_p[:, h, width - n:width]
                    one = slice(job, job + 1)
                    dve.tensor_tensor_reduce(s[:, job % 2, 0:n], S[:, job % 2, 0:n], extra, 1.0, -3e38, ALU.add, ALU.max, mx[:, one]).then_inc(biased, 1)
                    dve.wait_ge(biased, job + 1)
                    if kind == "A":
                        dve.tensor_scalar(bias[:, one], mx[:, one], sink[:, h:h + 1], -1.0, ALU.max, ALU.mult).then_inc(bias_ready, 1)
                    elif kind == "B":
                        dve.tensor_scalar(bias[:, one], mx[:, one], -1.0, None, ALU.mult).then_inc(bias_ready, 1)
                    else:
                        then(dve.tensor_tensor(mx[:, one], mx[:, one], cumq[:, i, h:h + 1], ALU.add))
                        dve.tensor_tensor(bias[:, one], cumq[:, i, h:h + 1], mx[:, one], ALU.subtract).then_inc(bias_ready, 1)

            def back(u):
                h, i = units[u]
                n = n_cols(i)
                a, e = u * per_head, (u + 1) * per_head
                dve.wait_ge(exped, e)
                if kind == "A":
                    then(dve.tensor_tensor(total[:, a:e], total[:, a:e], esink[:, a:e], ALU.add))
                dve.reciprocal(inv[:, a:e], total[:, a:e]).then_inc(inv_ready, 1)
                dve.wait_ge(inv_ready, u + 1)
                if kind == "B":
                    then(dve.scalar_tensor_tensor(out=coef[:, u:u + 1], in0=total[:, a:a + 1], scalar=inv[:, a + 1:a + 2],
                                                  in1=neg_lam[:], op0=ALU.mult, op1=ALU.mult))
                    dve.scalar_tensor_tensor(out=p[:, u % 2, 0, 0:n], in0=p[:, u % 2, 1, 0:n], scalar=coef[:, u:u + 1],
                                             in1=p[:, u % 2, 0, 0:n], op0=ALU.mult, op1=ALU.add).then_inc(weighed, 1)
                    dve.wait_ge(weighed, u + 1)
                if i == TP:
                    dve.tensor_scalar(p[:, u % 2, 0, 0:n], p[:, u % 2, 0, 0:n], inv[:, a:a + 1], None, ALU.mult).then_inc(normed, 1)

            def take_out(u, late):
                h, i = units[u]
                if (i == TP) != late:
                    return
                dst = mixn[:, i, h * HEAD:(h + 1) * HEAD]
                if late:
                    dve.wait_ge(turned_back, samples_to[u + 1])
                    dve.tensor_copy(dst, O[:, u % 2, P:P + HEAD]).then_inc(taken_out, 1)
                else:
                    dve.wait_ge(multiplied, u + 1)
                    a = u * per_head
                    dve.tensor_scalar(dst, O[:, u % 2, 0:HEAD], inv[:, a:a + 1], None, ALU.mult).then_inc(taken_out, 1)

            for u in range(NU + 3):
                if u < NU:
                    front(u)
                if 1 <= u <= NU:
                    back(u - 1)
                if u >= 3:
                    take_out(u - 3, True)
                if 2 <= u <= NU + 1:
                    take_out(u - 2, False)
            if kind == "B":
                dve.wait_ge(sub_squared, 1)
                then(dve.tensor_reduce(sub_ms[:], sub_sq[:].rearrange("p t (h d) -> p (t h) d", d=HEAD), AX.X, ALU.add))
                dve.tensor_scalar(sub_ms[:], sub_ms[:], 1.0 / HEAD, EPS, ALU.mult, ALU.add).then_inc(sub_squared, 1)
                dve.wait_ge(sub_rooted, 1)
                then(dve.reciprocal(sub_ms[:], sub_root[:]))
                view = mixn[:].rearrange("p t (h d) -> p (t h) d", d=HEAD)
                then(dve.tensor_tensor(view, view, sub_ms[:].unsqueeze(2).broadcast_to([P, 2 * T, HEAD]), ALU.mult))
                dve.tensor_tensor(view, view, subln[:].unsqueeze(1).broadcast_to([P, 2 * T, HEAD]), ALU.mult).then_inc(sub_done, 1)
    ph.close()


def mix(nc, t, k, layer):
    ph = Phase(nc, "mix")
    w = ph.sb("w", [P, KD, D_MODEL])
    acc = ph.ps("acc", [P, 4, 512])
    w_in, done, added = (ph.sem(n) for n in ("w_in", "done", "added"))
    src = t["w_out"][layer]
    pieces = 2 * 3 + 5
    with nc.Block() as block:
        @block.sync
        def _(sp):
            for j in range(3):
                for h in range(2):
                    r = (j + 3 * h) * HEAD
                    sp.dma_start(w[h * HEAD:(h + 1) * HEAD, j, :], src[r:r + HEAD, :]).then_inc(w_in, 16)
            for g in range(3, KD):
                sp.dma_start(w[:, g, :], src[g * P:(g + 1) * P, :]).then_inc(w_in, 16)

        @block.tensor
        def _(pe):
            pe.wait_ge(w_in, 16 * pieces)
            for u in range(2 * T):
                i, c = divmod(u, 2)
                if u >= 4:
                    pe.wait_ge(added, u - 3)
                for g in range(KD):
                    last = pe.matmul(acc[:, u % 4, :], k["mixT"][:, g, i * P:(i + 1) * P], w[:, g, c * 512:(c + 1) * 512],
                                     start=(g == 0), stop=(g == KD - 1))
                last.then_inc(done, 1)

        @block.vector
        def _(dve):
            for u in range(2 * T):
                i, c = divmod(u, 2)
                x = k["x"][:, i, c * 512:(c + 1) * 512]
                dve.wait_ge(done, u + 1)
                dve.tensor_tensor(x, x, acc[:, u % 4, :], ALU.add).then_inc(added, 1)
    ph.close()


def feed(nc, t, k, layer):
    norm = Phase(nc, "nrm")
    hT = norm.sb("hT", [P, KD, TOK])
    gain = norm.sb("gain", [P, KD])
    inner = Phase(nc, "nri")
    parts = norm_transpose(inner, k, gain, hT)
    g_in = inner.sem("g_in")
    with nc.Block() as block:
        @block.sync
        def _(sp):
            with nc.allow_non_contiguous_dma(reason="gain vector"):
                sp.dma_start(gain[:], t["norm_ffn"][layer].rearrange("(k p) -> p k", p=P)).then_inc(g_in, 16)

        @block.tensor
        def _(pe):
            parts["pe"](pe)

        @block.scalar
        def _(act):
            parts["act"](act)

        @block.vector
        def _(dve):
            dve.wait_ge(g_in, 16)
            parts["dve"](dve)
    inner.close()
    ph = Phase(nc, "ffn")
    wg, wu = ph.sb("wg", [P, 2, KD, P]), ph.sb("wu", [P, 2, KD, P])
    wd = ph.sb("wd", [P, 2, D_MODEL])
    sg, aT = ph.sb("sg", [P, 2, 384]), ph.sb("aT", [P, 2, TOK])
    up = ph.ps("up", [P, 2, 2, 512])
    down = ph.ps("down", [P, 4, 512])
    g_w, d_w = [ph.sem(f"up_w{i}") for i in range(2)], [ph.sem(f"down_w{i}") for i in range(2)]
    upped, activated, gated, downed, added = (ph.sem(n) for n in ("upped", "activated", "gated", "downed", "added"))
    NT = 3
    ND = 2 * T
    src_g = t["w_gate"][layer].rearrange("(k p) n -> p k n", p=P)
    src_u = t["w_up"][layer].rearrange("(k p) n -> p k n", p=P)
    src_d = t["w_down"][layer]

    def each_pair(eng, body):
        for q in range(2):
            body(q, q, True)
        with eng.Fori(1, KF // 2) as pair:
            for q in range(2):
                body(2 * pair + q, q, False)

    with nc.Block() as block:
        @block.sync
        def _(sp):
            def load(f, q, first):
                if not first:
                    sp.wait_ge(upped, (f - 1) * NT)
                sp.dma_start(wg[:, q, :, :], src_g[:, :, bass.ds(f * P, P)]).then_inc(g_w[q], 16)
                sp.dma_start(wu[:, q, :, :], src_u[:, :, bass.ds(f * P, P)]).then_inc(g_w[q], 16)
                if not first:
                    sp.wait_ge(downed, (f - 1) * ND)
                sp.dma_start(wd[:, q, :], src_d[bass.ds(f * P, P), :]).then_inc(d_w[q], 16)
            each_pair(sp, load)

        @block.tensor
        def _(pe):
            def ups(f, q, first):
                pe.wait_ge(g_w[q], (f - q) * 16 + 32)
                for n in range(NT):
                    v = f * NT + n
                    b = (q * NT + n) % 2
                    if not (first and q == 0 and n < 2):
                        pe.wait_ge(gated, v - 1)
                    for which, w in ((0, wg), (1, wu)):
                        for c in range(KD):
                            last = pe.matmul(up[:, b, which, 0:384], w[:, q, c, :], hT[:, c, n * 384:(n + 1) * 384],
                                             start=(c == 0), stop=(c == KD - 1))
                    last.then_inc(upped, 1)

            def downs(f, q, first):
                pe.wait_ge(d_w[q], (f - q) * 8 + 16)
                pe.wait_ge(gated, f * NT + NT)
                for n in range(ND):
                    i, c = divmod(n, 2)
                    if not (first and q == 0 and n < 4):
                        pe.wait_ge(added, f * ND + n - 3)
                    pe.matmul(down[:, (q * ND + n) % 4, :], aT[:, q, i * P:(i + 1) * P], wd[:, q, c * 512:(c + 1) * 512],
                              start=True, stop=True).then_inc(downed, 1)

            ups(0, 0, True)
            ups(1, 1, True)
            downs(0, 0, True)
            with pe.Fori(1, KF // 2) as pair:
                f = 2 * pair
                ups(f, 0, False)
                downs(f - 1, 1, False)
                ups(f + 1, 1, False)
                downs(f, 0, False)
            downs(KF - 1, 1, False)

        @block.scalar
        def _(act):
            def silu(f, q, first):
                for n in range(NT):
                    v = f * NT + n
                    b = (q * NT + n) % 2
                    act.wait_ge(upped, v + 1)
                    if not (first and q == 0 and n < 2):
                        act.wait_ge(gated, v - 1)
                    act.activation(sg[:, b, :], up[:, b, 0, 0:384], ACT.Silu).then_inc(activated, 1)
            each_pair(act, silu)

        @block.vector
        def _(dve):
            def gate(f, q, first):
                for n in range(NT):
                    v = f * NT + n
                    b = (q * NT + n) % 2
                    dve.wait_ge(activated, v + 1)
                    if n == 0 and not first:
                        dve.wait_ge(downed, (f - 1) * ND)
                    dve.tensor_tensor(aT[:, q, n * 384:(n + 1) * 384], sg[:, b, :], up[:, b, 1, 0:384], ALU.mult).then_inc(gated, 1)

            def add(f, q, first):
                for n in range(ND):
                    i, c = divmod(n, 2)
                    x = k["x"][:, i, c * 512:(c + 1) * 512]
                    dve.wait_ge(downed, f * ND + n + 1)
                    dve.tensor_tensor(x, x, down[:, (q * ND + n) % 4, :], ALU.add).then_inc(added, 1)

            gate(0, 0, True)
            gate(1, 1, True)
            add(0, 0, True)
            with dve.Fori(1, KF // 2) as pair:
                f = 2 * pair
                gate(f, 0, False)
                add(f - 1, 1, False)
                gate(f + 1, 1, False)
                add(f, 0, False)
            add(KF - 1, 1, False)
    ph.close()
    norm.close()


def finish(nc, t, k):
    ph = Phase(nc, "fin")
    y_out = ph.sem("y_out")
    with nc.Block() as block:
        @block.sync
        def _(sp):
            sp.dma_start(t["y_prompt"].rearrange("a (t p) d -> p (a t) d", p=P), k["x"][:, 0:TP, :]).then_inc(y_out, 16)
            sp.dma_start(t["y_sample"].rearrange("b s d -> (b s) d"), k["x"][:, TP, :]).then_inc(y_out, 16)
            sp.wait_ge(y_out, 32)
    ph.close()


_INS = ["x_prompt", "x_sample", "cache_a_k", "cache_a_v", "cache_b_k", "cache_b_v", "cache_c_k", "cache_c_v",
        "cache_c_logf", "rel_bias_table", "norm_mix", "w_in", "b_forget", "q_norm_a", "k_norm_a", "sinks_a",
        "q_norm_b", "k_norm_b", "lam_q1", "lam_k1", "lam_q2", "lam_k2", "subln_b", "q_norm_c", "k_norm_c",
        "w_out", "norm_ffn", "w_gate", "w_up", "w_down"]


def _heads(lead):
    return {"a_k": lead + (A_KV, HEAD), "a_v": lead + (A_KV, HEAD), "b_k": lead + (B_HEADS, 2, B_DIM),
            "b_v": lead + (B_HEADS, HEAD), "c_k": lead + (C_HEADS, HEAD), "c_v": lead + (C_HEADS, HEAD),
            "c_logf": lead + (C_HEADS,)}


_OUTS = {"y_prompt": (1, SEQ, D_MODEL), "y_sample": (DEC_BATCH, DEC_SEQ, D_MODEL)}
_OUTS.update({"p_" + n: v for n, v in _heads((DEPTH, 1, SEQ)).items()})
_OUTS.update({"s_" + n: v for n, v in _heads((DEPTH, DEC_BATCH, DEC_SEQ)).items()})
for _kv in "kv":
    _OUTS[f"p_a_{_kv}"] = (DEPTH, 1, WINDOW, A_KV, HEAD)
    _OUTS[f"s_a_{_kv}"] = (DEPTH, DEC_BATCH, WINDOW, A_KV, HEAD)

_SCRATCH = {"qkv": (TOK, FZ), "bias_rows": (A_HEADS + B_HEADS, P, REL), "bias_a": (A_HEADS, P, 2 * P),
            "bias_b": (B_HEADS, P, SEQ), "bias_sa": (A_HEADS, P, 2 * P), "bias_sb": (B_HEADS, P, 3 * P),
            "cum_prompt": (C_HEADS, SEQ), "cum_past": (DEC_BATCH * C_HEADS, PAST), "cum_new": (C_HEADS, P)}


def kernel(**inputs):
    import concourse.bacc as _bacc
    from concourse.bass_utils import run_bass_kernel_spmd as _run

    nc = _bacc.Bacc("TRN2", target_bir_lowering=False, num_devices=1)
    arrays, t = {}, {}
    for name in _INS:
        arrays[f"in_{name}"] = np.ascontiguousarray(inputs[name])
    for name, a in constants().items():
        arrays[f"in_{name}"] = a
    for name, a in arrays.items():
        t[name[3:]] = nc.dram_tensor(name, a.shape, mybir.dt.from_np(a.dtype), kind="ExternalInput").ap()
    for name, shape in _OUTS.items():
        t[name] = nc.dram_tensor(f"out_{name}", shape, F32, kind="ExternalOutput").ap()
    for name, shape in _SCRATCH.items():
        t[name] = nc.dram_tensor(f"scratch_{name}", shape, F32).ap()
    build(nc, t)
    r = _run(nc, [arrays], core_ids=[0])
    return tuple(r.results[0][f"out_{name}"] for name in _OUTS)
```

```python
from contextlib import ExitStack

import numpy as np

import concourse.bass as bass
from concourse import mybir

P = 128
D_MODEL, SEQ, DEPTH, DEC_BATCH, DEC_SEQ, PAST = 1024, 1024, 2, 8, 16, 256
CHUNK, HEAD = 64, 64
A_HEADS, A_KV, B_HEADS, B_DIM, C_HEADS = 6, 2, 4, 32, 6
WINDOW = 128
D_FF = 2816
N_BUCKETS, MAX_DISTANCE = 32, 1024
EPS, NEG = 1e-6, -1e30
TP = SEQ // P
T = TP + 1
TOK = T * P
KD = D_MODEL // P
KF = D_FF // P
QA, KA, VA = 0, 384, 512
QB, KB, VB = 640, 896, 1152
QC, KC, VC = 1408, 1792, 2176
FZ = 2560
N_IN = FZ + C_HEADS
IN_BLOCKS = [(QA, 512), (VA, 384), (KB, 512), (QC, 384), (KC, 384), (VC, 384 + C_HEADS)]
NORMED = [(0, 8, HEAD), (128, 8, B_DIM), (0, 8, B_DIM), (0, 6, HEAD), (0, 6, HEAD), None]
GAINS = [("q_norm_a", 0, 6, HEAD, HEAD ** -0.5), ("k_norm_a", 384, 2, HEAD, None),
         ("q_norm_b", 512, 8, B_DIM, B_DIM ** -0.5), ("k_norm_b", 768, 8, B_DIM, None),
         ("q_norm_c", 1024, 6, HEAD, HEAD ** -0.5), ("k_norm_c", 1408, 6, HEAD, None)]
GAIN_AT = [0, 512, 768, 1024, 1408]
REL0 = SEQ - 1 + P
REL = REL0 + P + 1

F32 = mybir.dt.float32
BF16 = mybir.dt.bfloat16
F32R = mybir.dt.float32r
ALU = mybir.AluOpType
ACT = mybir.ActivationFunctionType
AX = mybir.AxisListType


def constants():
    i = np.arange(P)
    upper = (i[:, None] <= i[None, :]).astype(np.float32)
    same = (i[:, None] // DEC_SEQ == i[None, :] // DEC_SEQ)
    rel = np.arange(REL) - REL0
    n = np.abs(rel)
    half, exact = N_BUCKETS // 2, N_BUCKETS // 4
    large = exact + (np.log(np.maximum(n, 1).astype(np.float32) / exact)
                     / np.float32(np.log(MAX_DISTANCE / exact)) * (half - exact)).astype(np.int32)
    bucket = np.where(rel > 0, half, 0) + np.where(n < exact, n, np.minimum(large, half - 1))
    bh = np.arange(DEC_BATCH * C_HEADS)
    lam_init = 0.8 - 0.6 * np.exp(-0.3 * np.arange(DEPTH))
    return {
        "c_ident": np.eye(P, dtype=np.float32),
        "c_upper": np.concatenate([upper, np.ones((P, SEQ - P), np.float32)], 1),
        "c_upper_batch": upper * same,
        "c_causal": np.where(i[None, :] <= i[:, None], 0.0, NEG).astype(np.float32),
        "c_batch": np.where(same, 0.0, NEG).astype(np.float32),
        "c_batch_causal": np.where(same & (i[None, :] <= i[:, None]), 0.0, NEG).astype(np.float32),
        "c_buckets": (np.arange(N_BUCKETS)[:, None] == bucket[None, :]).astype(np.float32),
        "c_is_head": (bh[:, None] % C_HEADS == np.arange(C_HEADS)[None, :]).astype(np.float32),
        "c_is_batch": (bh[:, None] // C_HEADS == i[None, :] // DEC_SEQ).astype(np.float32),
        "c_lam": np.stack([lam_init, 1.0 - lam_init]).astype(np.float32),
    }


class Count:

    def __init__(self, sem, by=1):
        self.sem, self.by, self.n = sem, by, 0

    def on(self, instruction):
        self.n += self.by
        instruction.then_inc(self.sem, self.by)
        return self.n


class Phase:

    def __init__(self, nc, name):
        self.nc, self.name, self.ctx, self.sems = nc, name, ExitStack(), []

    def sb(self, name, shape, dt=F32):
        return self.ctx.enter_context(self.nc.sbuf_tensor(f"{self.name}_{name}", shape, dt))

    def ps(self, name, shape):
        return self.ctx.enter_context(self.nc.psum_tensor(f"{self.name}_{name}", shape, F32))

    def sem(self, name):
        s = self.ctx.enter_context(self.nc.semaphore(f"{self.name}_{name}"))
        self.sems.append(s)
        return s

    def close(self):
        with self.nc.Block() as block:
            @block.gpsimd
            def _(pool):
                for s in self.sems:
                    pool.sem_clear(s)
        self.ctx.close()


def rows(dram, offset, pattern):
    return bass.AP(dram.tensor, dram.offset + offset, pattern)


def build(nc, t):
    with ExitStack() as ctx:
        def sb(name, shape, dt=F32):
            return ctx.enter_context(nc.sbuf_tensor(name, shape, dt))

        k = {"x": sb("x", [P, T, D_MODEL]), "ident": sb("ident", [P, P]),
             "logf": sb("logf", [P, T, C_HEADS]), "cumq": sb("cumq", [P, T, C_HEADS]),
             "lam": sb("lam", [P, 1])}
        setup(nc, t, k)
        with nc.Fori(0, DEPTH) as layer:
            project(nc, t, k, layer)
            forget(nc, t, k, layer)
            attend(nc, t, k, layer)
            mix(nc, t, k, layer)
            feed(nc, t, k, layer)
        finish(nc, t, k)


def setup(nc, t, k):
    ph = Phase(nc, "set")
    heads = A_HEADS + B_HEADS
    table = ph.sb("table", [N_BUCKETS, heads])
    wide = ph.sb("wide", [N_BUCKETS, heads, P])
    buckets = ph.sb("buckets", [N_BUCKETS, REL])
    row = ph.sb("row", [P, 2, REL])
    tile_a = ph.sb("tile_a", [P, A_HEADS, 2 * P])
    tile_b = ph.sb("tile_b", [P, B_HEADS, SEQ])
    samp_a = ph.sb("samp_a", [P, A_HEADS, 2 * P])
    samp_b = ph.sb("samp_b", [P, B_HEADS, 3 * P])
    near = ph.sb("near", [P, heads, DEC_SEQ])
    batch = ph.sb("batch", [P, P])
    pr = ph.ps("pr", [P, 2, 3 * 512])
    loaded, widened, product, copied = ph.sem("loaded"), ph.sem("widened"), ph.sem("product"), ph.sem("copied")
    tiles_in, tiles_done, tiles_out = (ph.sem(n) for n in ("tiles_in", "tiles_done", "tiles_out"))
    rows_out = [ph.sem(f"rows_out{i}") for i in range(2)]
    x_in = ph.sem("x_in")
    cuts = [(c, min(c + 512, REL)) for c in range(0, REL, 512)]
    with nc.Block() as block:
        @block.sync
        def _(sp):
            sp.dma_start(table[:], t["rel_bias_table"]).then_inc(loaded, 16)
            sp.dma_start(buckets[:], t["c_buckets"]).then_inc(loaded, 16)
            sp.dma_start(batch[:], t["c_batch"]).then_inc(loaded, 16)
            sp.dma_start(k["ident"][:], t["c_ident"]).then_inc(x_in, 16)
            sp.dma_start(k["x"][:, 0:TP, :], t["x_prompt"].rearrange("a (t p) d -> p (a t) d", p=P)).then_inc(x_in, 16)
            sp.dma_start(k["x"][:, TP, :], t["x_sample"].rearrange("b s d -> (b s) d")).then_inc(x_in, 16)
            for h in range(heads):
                sp.wait_ge(copied, h + 1)
                sp.dma_start(t["bias_rows"][h], row[:, h % 2, :]).then_inc(rows_out[h % 2], 16)
            for out in rows_out:
                sp.wait_ge(out, 16 * heads // 2)
            skew = REL - 1
            for h in range(heads):
                at = h * P * REL + REL0
                if h < A_HEADS:
                    sp.dma_start(tile_a[:, h, :], rows(t["bias_rows"], at - P, [[skew, P], [1, 2 * P]])).then_inc(tiles_in, 16)
                    sp.dma_start(samp_a[:, h, 0:P], rows(t["bias_rows"], at - P, [[0, DEC_BATCH], [skew, DEC_SEQ], [1, P]])).then_inc(tiles_in, 16)
                else:
                    sp.dma_start(tile_b[:, h - A_HEADS, :], rows(t["bias_rows"], at - SEQ + P, [[skew, P], [1, SEQ]])).then_inc(tiles_in, 16)
                    sp.dma_start(samp_b[:, h - A_HEADS, 0:PAST], rows(t["bias_rows"], at - PAST, [[0, DEC_BATCH], [skew, DEC_SEQ], [1, PAST]])).then_inc(tiles_in, 16)
                sp.dma_start(near[:, h, :], rows(t["bias_rows"], at, [[0, DEC_BATCH], [skew, DEC_SEQ], [1, DEC_SEQ]])).then_inc(tiles_in, 16)
            sp.wait_ge(tiles_done, 4)
            sp.dma_start(t["bias_a"].rearrange("h p c -> p h c"), tile_a[:]).then_inc(tiles_out, 16)
            sp.dma_start(t["bias_b"].rearrange("h p c -> p h c"), tile_b[:]).then_inc(tiles_out, 16)
            sp.dma_start(t["bias_sa"].rearrange("h p c -> p h c"), samp_a[:]).then_inc(tiles_out, 16)
            sp.dma_start(t["bias_sb"].rearrange("h p c -> p h c"), samp_b[:]).then_inc(tiles_out, 16)
            sp.wait_ge(tiles_out, 64)
            sp.wait_ge(x_in, 48)

        @block.tensor
        def _(pe):
            pe.wait_ge(widened, 1)
            for h in range(heads):
                if h >= 2:
                    pe.wait_ge(copied, h - 1)
                for a, b in cuts:
                    last = pe.matmul(pr[:, h % 2, a:b], wide[:, h, :], buckets[:, a:b], start=True, stop=True)
                last.then_inc(product, 1)

        @block.vector
        def _(dve):
            dve.wait_ge(loaded, 48)
            dve.tensor_copy(wide[:], table[:].unsqueeze(2).broadcast_to([N_BUCKETS, heads, P])).then_inc(widened, 1)
            for h in range(heads):
                dve.wait_ge(product, h + 1)
                if h >= 2:
                    dve.wait_ge(rows_out[h % 2], 16 * (h // 2))
                dve.tensor_copy(row[:, h % 2, :], pr[:, h % 2, 0:REL]).then_inc(copied, 1)
            dve.wait_ge(tiles_in, 16 * 3 * heads)
            dve.memset(tile_a[0:64, :, 192:256], NEG).then_inc(tiles_done, 1)
            dve.memset(tile_a[64:128, :, 0:64], NEG).then_inc(tiles_done, 1)
            dve.memset(tile_b[0:64, :, SEQ - 64:SEQ], NEG).then_inc(tiles_done, 1)
            for h in range(heads):
                out = samp_a[:, h, P:2 * P] if h < A_HEADS else samp_b[:, h - A_HEADS, PAST:PAST + P]
                last = dve.tensor_tensor(out.rearrange("p (b s) -> p b s", b=DEC_BATCH),
                                         batch[:].rearrange("p (b s) -> p b s", b=DEC_BATCH),
                                         near[:, h, :].unsqueeze(1).broadcast_to([P, DEC_BATCH, DEC_SEQ]), ALU.add)
            last.then_inc(tiles_done, 1)
    ph.close()


def split_hi(eng, hi, x):
    return eng.activation(hi, x, ACT.Copy)


def split_lo(eng, lo, x, hi):
    return eng.tensor_tensor(lo, x, hi.bitcast(F32), ALU.subtract)


def norm_transpose(ph, k, gain_row, h_hi, h_lo, h32):
    squares = ph.sb("squares", [P, D_MODEL])
    ms = ph.sb("ms", [P, T])
    root = ph.sb("root", [P, T])
    rstd = ph.sb("rstd", [P, T])
    xn = ph.sb("xn", [P, 2, D_MODEL])
    pt = ph.ps("pt", [P, 2, D_MODEL])
    summed, shifted, rooted, scaled = (ph.sem(n) for n in ("summed", "shifted", "rooted", "scaled"))
    normed, turned, gained, hi_made, ready = (ph.sem(n) for n in ("normed", "turned", "h_gained", "h_hi_made", "h_ready"))
    x = k["x"]

    def act(eng):
        for i in range(T):
            if i:
                eng.wait_ge(summed, i)
            eng.activation(squares[:], x[:, i, :], ACT.Square, accum_out=ms[:, i:i + 1]).then_inc(summed, 1)
        eng.wait_ge(shifted, 1)
        eng.activation(root[:], ms[:], ACT.Sqrt).then_inc(rooted, 1)
        eng.wait_ge(scaled, 1)
        for i in range(T + 2):
            if i < T:
                if i >= 2:
                    eng.wait_ge(turned, i - 1)
                eng.activation(xn[:, i % 2, :], x[:, i, :], ACT.Copy, scale=rstd[:, i:i + 1]).then_inc(normed, 1)
            if i >= 2:
                j = i - 2
                eng.wait_ge(gained, j + 1)
                split_hi(eng, h_hi[:, :, j * P:(j + 1) * P], h32[:, j % 2, :].rearrange("p (k n) -> p k n", k=KD)).then_inc(hi_made, 1)

    def dve(eng):
        eng.wait_ge(summed, T)
        eng.tensor_scalar(ms[:], ms[:], 1.0 / D_MODEL, EPS, ALU.mult, ALU.add).then_inc(shifted, 1)
        eng.wait_ge(rooted, 1)
        eng.reciprocal(rstd[:], root[:]).then_inc(scaled, 1)
        for i in range(T + 1):
            if i < T:
                eng.wait_ge(turned, i + 1)
                if i >= 2:
                    eng.wait_ge(ready, i - 1)
                eng.tensor_tensor(h32[:, i % 2, :].rearrange("p (k n) -> p k n", k=KD),
                                  pt[:, i % 2, :].rearrange("p (k n) -> p k n", k=KD),
                                  gain_row[:].unsqueeze(2).broadcast_to([P, KD, P]), ALU.mult).then_inc(gained, 1)
            if i >= 1:
                j = i - 1
                span = slice(j * P, (j + 1) * P)
                eng.wait_ge(gained, j + 1)
                eng.wait_ge(hi_made, j + 1)
                split_lo(eng, h_lo[:, :, span], h32[:, j % 2, :].rearrange("p (k n) -> p k n", k=KD), h_hi[:, :, span]).then_inc(ready, 1)

    def pe(eng):
        for i in range(T):
            eng.wait_ge(normed, i + 1)
            if i >= 2:
                eng.wait_ge(gained, i - 1)
            for c in range(KD):
                last = eng.transpose(pt[:, i % 2, c * P:(c + 1) * P], xn[:, i % 2, c * P:(c + 1) * P], k["ident"][:])
            last.then_inc(turned, 1)

    return {"act": act, "dve": dve, "pe": pe, "ready": ready, "pt": pt}


def norm_transpose_one(ph, k, gain_row, hT):
    squares = ph.sb("squares", [P, D_MODEL])
    ms = ph.sb("ms", [P, T])
    root = ph.sb("root", [P, T])
    rstd = ph.sb("rstd", [P, T])
    xn = ph.sb("xn", [P, 2, D_MODEL])
    pt = ph.ps("pt", [P, 2, D_MODEL])
    summed, shifted, rooted, scaled = (ph.sem(n) for n in ("summed", "shifted", "rooted", "scaled"))
    normed, turned, ready = (ph.sem(n) for n in ("normed", "turned", "h_ready"))
    x = k["x"]

    def act(eng):
        for i in range(T):
            if i:
                eng.wait_ge(summed, i)
            eng.activation(squares[:], x[:, i, :], ACT.Square, accum_out=ms[:, i:i + 1]).then_inc(summed, 1)
        eng.wait_ge(shifted, 1)
        eng.activation(root[:], ms[:], ACT.Sqrt).then_inc(rooted, 1)
        eng.wait_ge(scaled, 1)
        for i in range(T):
            if i >= 2:
                eng.wait_ge(turned, i - 1)
            eng.activation(xn[:, i % 2, :], x[:, i, :], ACT.Copy, scale=rstd[:, i:i + 1]).then_inc(normed, 1)

    def dve(eng):
        eng.wait_ge(summed, T)
        eng.tensor_scalar(ms[:], ms[:], 1.0 / D_MODEL, EPS, ALU.mult, ALU.add).then_inc(shifted, 1)
        eng.wait_ge(rooted, 1)
        eng.reciprocal(rstd[:], root[:]).then_inc(scaled, 1)
        for i in range(T):
            eng.wait_ge(turned, i + 1)
            eng.tensor_tensor(hT[:, :, i * P:(i + 1) * P], pt[:, i % 2, :].rearrange("p (k n) -> p k n", k=KD),
                              gain_row[:].unsqueeze(2).broadcast_to([P, KD, P]), ALU.mult).then_inc(ready, 1)

    def pe(eng):
        for i in range(T):
            eng.wait_ge(normed, i + 1)
            if i >= 2:
                eng.wait_ge(ready, i - 1)
            for c in range(KD):
                last = eng.transpose(pt[:, i % 2, c * P:(c + 1) * P], xn[:, i % 2, c * P:(c + 1) * P], k["ident"][:])
            last.then_inc(turned, 1)

    return {"act": act, "dve": dve, "pe": pe, "ready": ready, "pt": pt}


def stores(t, layer, block, i, nat):
    c0, n = IN_BLOCKS[block]
    n = min(n, FZ - c0)
    out = [(t["qkv"][i * P:(i + 1) * P, c0:c0 + n], nat[:, 0:n])]
    prompt, sample = i < TP, i == TP
    for first, count, name, shape in ((KA, 128, "a_k", "h d"), (VA, 128, "a_v", "h d"), (KB, 256, "b_k", "h m d"),
                                      (VB, 256, "b_v", "h d"), (KC, 384, "c_k", "h d"), (VC, 384, "c_v", "h d")):
        if not c0 <= first < c0 + n:
            continue
        src = nat[:, first - c0:first - c0 + count]
        flat = f"({shape})"
        if sample:
            dst = t["s_" + name][layer].rearrange(f"b s {shape} -> b s {flat}")
            if name[0] == "a":
                dst = dst[:, WINDOW - DEC_SEQ:WINDOW, :]
                for b in range(DEC_BATCH):
                    out.append((dst[b], src[b * DEC_SEQ:(b + 1) * DEC_SEQ, :]))
            else:
                out.append((dst.rearrange("b s n -> (b s) n"), src))
        elif name[0] != "a" or i == TP - 1:
            dst = t["p_" + name][layer, 0].rearrange(f"s {shape} -> s {flat}")
            out.append((dst if name[0] == "a" else dst[i * P:(i + 1) * P, :], src))
    return out


def project(nc, t, k, layer):
    ph = Phase(nc, "prj")
    hT = ph.sb("hT", [P, KD, TOK])
    gain = ph.sb("gain", [P, KD])
    w = ph.sb("w", [P, 2, KD, 512])
    qk_gain = ph.sb("qk_gain", [P, 1792])
    bf = ph.sb("bf", [P, C_HEADS])
    sq = ph.sb("sq", [P, 2, 512])
    ms, root, rstd = (ph.sb(n, [P, 2, 8]) for n in ("head_ms", "head_root", "head_rstd"))
    nat = ph.sb("nat", [P, 4, 512])
    z, z_abs, z_exp = (ph.sb(n, [P, T, C_HEADS]) for n in ("z", "z_abs", "z_exp"))
    tT = ph.sb("tT", [P, 2, 4, P])
    acc = ph.ps("acc", [P, 4, 512])
    parts = norm_transpose_one(ph, k, gain, hT)
    g_in, w_even, w_odd, done = (ph.sem(n) for n in ("g_in", "w_even", "w_odd", "done"))
    w_in = (w_even, w_odd)
    squared, summed_h, shifted_h, rooted_h, inverse_h, gained, made = (
        ph.sem(n) for n in ("squared", "summed_h", "shifted_h", "rooted_h", "inverse_h", "gained", "made"))
    stored = [ph.sem(f"stored{i}") for i in range(4)]
    scaled_q, f_sum, f_abs, f_exp, f_ln, f_out, f_stored, rolled = (
        ph.sem(n) for n in ("scaled_q", "f_sum", "f_abs", "f_exp", "f_ln", "f_out", "f_stored", "rolled"))
    turned_qk, taken_qk = ph.sem("turned_qk"), ph.sem("taken_qk")
    qk_stored = [ph.sem(f"qk_stored{i}") for i in range(2)]
    work = [(b, i) for b in range(len(IN_BLOCKS)) for i in range(T)]
    normed_units = [u for u, (b, i) in enumerate(work) if NORMED[b]]
    n_stores = [len(stores(t, layer, b, i, nat[:, 0, :])) for b, i in work]
    src = t["w_in"][layer].rearrange("(k p) n -> p k n", p=P)

    def stored_by(u):
        return 16 * sum(n_stores[v] for v in range(u % 4, u + 1, 4))

    with nc.Block() as block:
        @block.sync
        def _(sp):
            with nc.allow_non_contiguous_dma(reason="gain vectors"):
                sp.dma_start(gain[:], t["norm_mix"][layer].rearrange("(k p) -> p k", p=P)).then_inc(g_in, 16)
            for name, c, heads, width, _ in GAINS:
                sp.dma_start(qk_gain[:, c:c + heads * width].rearrange("p (h d) -> p h d", d=width),
                             t[name][layer].unsqueeze(0).unsqueeze(0).broadcast_to([P, heads, width])).then_inc(g_in, 16)
            sp.dma_start(bf[:], t["b_forget"][layer].unsqueeze(0).broadcast_to([P, C_HEADS])).then_inc(g_in, 16)
            for kv in "kv":
                sp.dma_start(t[f"s_a_{kv}"][layer, :, 0:WINDOW - DEC_SEQ], t[f"cache_a_{kv}"][layer, :, DEC_SEQ:WINDOW]).then_inc(rolled, 16)
            def store_turned(m):
                b, i = work[normed_units[m]]
                n = NORMED[b][1] * NORMED[b][2] // P
                sp.wait_ge(taken_qk, m + 1)
                dst = t["qkT"][GAIN_AT[b]:GAIN_AT[b] + n * P, i * P:(i + 1) * P].rearrange("(x p) n -> p x n", p=P)
                sp.dma_start(dst, tT[:, m % 2, 0:n, :]).then_inc(qk_stored[m % 2], 16)

            for u, (b, i) in enumerate(work):
                if NORMED[b]:
                    sp.wait_ge(made, sum(bool(NORMED[v[0]]) for v in work[:u + 1]))
                else:
                    sp.wait_ge(gained, u + 1)
                for dst, rows_ in stores(t, layer, b, i, nat[:, u % 4, :]):
                    sp.dma_start(dst, rows_).then_inc(stored[u % 4], 16)
                if 2 <= u < len(normed_units) + 2:
                    store_turned(u - 2)
            for m in range(2):
                sp.wait_ge(qk_stored[m], 16 * len(range(m, len(normed_units), 2)))
            for u in range(len(work) - 4, len(work)):
                sp.wait_ge(stored[u % 4], stored_by(u))
            sp.wait_ge(rolled, 32)
            sp.wait_ge(f_out, 1)
            sp.dma_start(t["p_c_logf"][layer, 0].rearrange("(t p) h -> p t h", p=P), k["logf"][:, 0:TP, :]).then_inc(f_stored, 16)
            sp.dma_start(t["s_c_logf"][layer].rearrange("b s h -> (b s) h"), k["logf"][:, TP, :]).then_inc(f_stored, 16)
            sp.wait_ge(f_stored, 32)

        @block.tensor
        def _(pe):
            parts["pe"](pe)
            pe.wait_ge(parts["ready"], T)

            def turn_rows(m):
                b, i = work[normed_units[m]]
                c, heads, width = NORMED[b]
                pe.wait_ge(made, m + 1)
                if m >= 4:
                    pe.wait_ge(taken_qk, m - 3)
                for x in range(heads * width // P):
                    last = pe.transpose(parts["pt"][:, m % 4 // 2, m % 2 * 512 + x * P:m % 2 * 512 + (x + 1) * P],
                                        nat[:, normed_units[m] % 4, c + x * P:c + (x + 1) * P], k["ident"][:])
                last.then_inc(turned_qk, 1)

            for u, (b, i) in enumerate(work):
                n = IN_BLOCKS[b][1]
                if i == 0:
                    pe.wait_ge(w_in[b % 2], 16 * (b // 2 + 1))
                if u >= 4:
                    pe.wait_ge(gained, u - 3)
                for c in range(KD):
                    last = pe.matmul(acc[:, u % 4, 0:n], hT[:, c, i * P:(i + 1) * P], w[:, b % 2, c, 0:n],
                                     start=(c == 0), stop=(c == KD - 1))
                last.then_inc(done, 1)
                if 2 <= u < len(normed_units) + 2:
                    turn_rows(u - 2)

        @block.scalar
        def _(act):
            def take_turned(m):
                b, i = work[normed_units[m]]
                n = NORMED[b][1] * NORMED[b][2] // P
                act.wait_ge(turned_qk, m + 1)
                if m >= 2:
                    act.wait_ge(qk_stored[m % 2], 16 * (m // 2))
                act.activation(tT[:, m % 2, 0:n, :], parts["pt"][:, m % 4 // 2, m % 2 * 512:m % 2 * 512 + n * P].rearrange("p (x n) -> p x n", n=P),
                               ACT.Copy).then_inc(taken_qk, 1)

            def load_w(b):
                c, n = IN_BLOCKS[b]
                act.dma_start(w[:, b % 2, :, 0:n], src[:, :, c:c + n]).then_inc(w_in[b % 2], 16)

            load_w(0)
            load_w(1)
            parts["act"](act)
            m = 0
            for u, (b, i) in enumerate(work):
                if i == 0 and 1 <= b < len(IN_BLOCKS) - 1:
                    act.wait_ge(done, u)
                    load_w(b + 1)
                if 2 <= u < len(normed_units) + 2:
                    take_turned(u - 2)
                if not NORMED[b]:
                    continue
                c, heads, width = NORMED[b]
                span = slice(c, c + heads * width)
                act.wait_ge(done, u + 1)
                if m >= 2:
                    act.wait_ge(summed_h, m - 1)
                act.activation(sq[:, m % 2, span], acc[:, u % 4, span], ACT.Square).then_inc(squared, 1)
                act.wait_ge(shifted_h, m + 1)
                if m >= 2:
                    act.wait_ge(inverse_h, m - 1)
                act.activation(root[:, m % 2, 0:heads], ms[:, m % 2, 0:heads], ACT.Sqrt).then_inc(rooted_h, 1)
                m += 1
            act.wait_ge(f_abs, 1)
            act.activation(z_exp[:], z_abs[:], ACT.Exp, scale=-1.0).then_inc(f_exp, 1)
            act.wait_ge(f_exp, 1)
            act.activation(z_abs[:], z_exp[:], ACT.Ln, bias=1.0).then_inc(f_ln, 1)

        @block.vector
        def _(dve):
            dve.wait_ge(g_in, 128)
            parts["dve"](dve)
            for name, c, heads, width, scale in GAINS:
                if scale:
                    span = qk_gain[:, c:c + heads * width]
                    last = dve.tensor_scalar(span, span, scale, None, ALU.mult)
            last.then_inc(scaled_q, 1)
            dve.wait_ge(scaled_q, 1)

            def read_out(u, m):
                b, i = work[u]
                n = IN_BLOCKS[b][1]
                dve.wait_ge(done, u + 1)
                if u >= 4:
                    dve.wait_ge(stored[u % 4], stored_by(u - 4))
                    if NORMED[work[u - 4][0]]:
                        dve.wait_ge(turned_qk, normed_units.index(u - 4) + 1)
                if not NORMED[b]:
                    dve.tensor_tensor(z[:, i, :], acc[:, u % 4, n - C_HEADS:n], bf[:], ALU.add).then_inc(f_sum, 1)
                    dve.tensor_copy(nat[:, u % 4, 0:n - C_HEADS], acc[:, u % 4, 0:n - C_HEADS]).then_inc(gained, 1)
                    return
                c, heads, width = NORMED[b]
                e = c + heads * width
                dve.wait_ge(squared, m + 1)
                for a_, e_ in ((0, c), (e, n)):
                    if a_ < e_:
                        dve.tensor_copy(nat[:, u % 4, a_:e_], acc[:, u % 4, a_:e_])
                g = GAIN_AT[b]
                dve.tensor_tensor(nat[:, u % 4, c:e], acc[:, u % 4, c:e], qk_gain[:, g:g + heads * width], ALU.mult).then_inc(gained, 1)
                dve.tensor_reduce(ms[:, m % 2, 0:heads], sq[:, m % 2, c:e].rearrange("p (h d) -> p h d", d=width), AX.X, ALU.add).then_inc(summed_h, 1)
                dve.wait_ge(summed_h, m + 1)
                dve.tensor_scalar(ms[:, m % 2, 0:heads], ms[:, m % 2, 0:heads], 1.0 / width, EPS, ALU.mult, ALU.add).then_inc(shifted_h, 1)

            def finish_rows(u, m):
                b, i = work[u]
                n = IN_BLOCKS[b][1]
                dve.wait_ge(gained, u + 1)
                if not NORMED[b]:
                    return
                c, heads, width = NORMED[b]
                dve.wait_ge(rooted_h, m + 1)
                dve.reciprocal(rstd[:, m % 2, 0:heads], root[:, m % 2, 0:heads]).then_inc(inverse_h, 1)
                dve.wait_ge(inverse_h, m + 1)
                view = nat[:, u % 4, c:c + heads * width].rearrange("p (h d) -> p h d", d=width)
                dve.tensor_tensor(view, view, rstd[:, m % 2, 0:heads].unsqueeze(2).broadcast_to([P, heads, width]), ALU.mult).then_inc(made, 1)

            order = [sum(bool(NORMED[v[0]]) for v in work[:u]) for u in range(len(work))]
            for u in range(len(work) + 1):
                if u < len(work):
                    read_out(u, order[u])
                if u >= 1:
                    finish_rows(u - 1, order[u - 1])
            dve.wait_ge(f_sum, T)
            dve.scalar_tensor_tensor(out=z_abs[:], in0=z[:], scalar=-1.0, in1=z[:], op0=ALU.mult, op1=ALU.max).then_inc(f_abs, 1)
            dve.wait_ge(f_ln, 1)
            dve.scalar_tensor_tensor(out=k["logf"][:], in0=z[:], scalar=0.0, in1=z_abs[:], op0=ALU.min, op1=ALU.subtract).then_inc(f_out, 1)
    ph.close()


def forget(nc, t, k, layer):
    ph = Phase(nc, "fgt")
    BH = DEC_BATCH * C_HEADS
    upper = ph.sb("upper", [P, SEQ])
    batch_upper = ph.sb("batch_upper", [P, P])
    is_head = ph.sb("is_head", [BH, C_HEADS])
    is_batch = ph.sb("is_batch", [BH, P])
    past = ph.sb("past", [P, 2, BH])
    total = ph.sb("total", [BH, P])
    past_row = ph.sb("past_row", [BH, PAST])
    prompt_row = ph.sb("prompt_row", [C_HEADS, SEQ])
    new_row = ph.sb("new_row", [C_HEADS, P])
    lams = ph.sb("lams", [P, 4, B_DIM])
    lam_c = ph.sb("lam_c", [P, 1])
    lam_x = ph.sb("lam_x", [P, 2, B_DIM])
    lam_s = ph.sb("lam_s", [P, 2])
    lam_e = ph.sb("lam_e", [P, 2])
    cols = ph.ps("cols", [P, 512])
    prow = ph.ps("prow", [P, SEQ])
    srow = ph.ps("srow", [P, 512])
    nrow = ph.ps("nrow", [P, 512])
    loaded, sums, past_sum, totals, negated, stored = (ph.sem(n) for n in ("loaded", "sums", "past_sum", "totals", "negated", "stored"))
    lam_prod, lam_exp, lam_diff = (ph.sem(n) for n in ("lam_prod", "lam_exp", "lam_diff"))
    logf = k["logf"]
    with nc.Block() as block:
        @block.sync
        def _(sp):
            sp.dma_start(upper[:], t["c_upper"]).then_inc(loaded, 16)
            sp.dma_start(batch_upper[:], t["c_upper_batch"]).then_inc(loaded, 16)
            sp.dma_start(is_head[:], t["c_is_head"]).then_inc(loaded, 16)
            sp.dma_start(is_batch[:], t["c_is_batch"]).then_inc(loaded, 16)
            with nc.allow_non_contiguous_dma(reason="six gates per position"):
                for half in range(2):
                    sp.dma_start(past[:, half, :].rearrange("p (b h) -> p b h", b=DEC_BATCH),
                                 t["cache_c_logf"][layer, :, half * P:(half + 1) * P, :].rearrange("b p h -> p b h")).then_inc(loaded, 16)
            for n, name in enumerate(("lam_q1", "lam_k1", "lam_q2", "lam_k2")):
                sp.dma_start(lams[:, n, :], t[name][layer].unsqueeze(0).broadcast_to([P, B_DIM])).then_inc(loaded, 16)
            sp.dma_start(lam_c[:], t["c_lam"][0:1, bass.ds(layer, 1)].broadcast_to([P, 1])).then_inc(loaded, 16)
            sp.wait_ge(negated, 3)
            sp.dma_start(t["cum_prompt"], prompt_row[:]).then_inc(stored, 16)
            sp.dma_start(t["cum_past"], past_row[:]).then_inc(stored, 16)
            sp.dma_start(t["cum_new"], new_row[:]).then_inc(stored, 16)
            sp.wait_ge(stored, 48)

        @block.tensor
        def _(pe):
            pe.wait_ge(loaded, 16 * 11)
            pe.matmul(srow[0:BH, 0:PAST], past[:, 0, :], upper[:, 0:PAST], start=True, stop=False)
            pe.matmul(srow[0:BH, P:PAST], past[:, 1, :], upper[:, 0:P], start=False, stop=True).then_inc(past_sum, 1)
            for i in range(TP):
                for c in range(i * P // 512, 2):
                    a = max(i * P, c * 512)
                    pe.matmul(prow[0:C_HEADS, a:(c + 1) * 512], logf[:, i, :], upper[:, a - i * P:(c + 1) * 512 - i * P],
                              start=(i == 0), stop=(i == 4 * c + 3))
            for i in range(TP):
                for j in range(i + 1):
                    pe.matmul(cols[:, i * C_HEADS:(i + 1) * C_HEADS], upper[:, 0:P] if j == i else upper[:, P:2 * P],
                              logf[:, j, :], start=(j == 0), stop=(j == i))
            pe.wait_ge(totals, 1)
            pe.matmul(cols[:, TP * C_HEADS:T * C_HEADS], batch_upper[:], logf[:, TP, :], start=True, stop=False)
            pe.matmul(cols[:, TP * C_HEADS:T * C_HEADS], total[:], is_head[:], start=False, stop=True)
            pe.matmul(nrow[0:C_HEADS, 0:P], logf[:, TP, :], batch_upper[:], start=True, stop=False)
            pe.matmul(nrow[0:C_HEADS, 0:P], is_head[:], total[:], start=False, stop=True).then_inc(sums, 1)

        @block.scalar
        def _(act):
            act.wait_ge(lam_prod, 1)
            act.activation(lam_e[:], lam_s[:], ACT.Exp).then_inc(lam_exp, 1)

        @block.vector
        def _(dve):
            dve.wait_ge(past_sum, 1)
            dve.tensor_scalar(total[:], is_batch[:], srow[0:BH, PAST - 1:PAST], None, ALU.mult).then_inc(totals, 1)
            for n in range(2):
                last = dve.tensor_tensor_reduce(lam_x[:, n, :], lams[:, 2 * n, :], lams[:, 2 * n + 1, :], 1.0, 0.0, ALU.mult, ALU.add, lam_s[:, n:n + 1])
            last.then_inc(lam_prod, 1)
            dve.wait_ge(lam_exp, 1)
            dve.tensor_tensor(lam_s[:, 0:1], lam_e[:, 0:1], lam_e[:, 1:2], ALU.subtract).then_inc(lam_diff, 1)
            dve.wait_ge(lam_diff, 1)
            dve.tensor_tensor(k["lam"][:], lam_s[:, 0:1], lam_c[:], ALU.add).then_inc(lam_diff, 1)
            dve.tensor_scalar(past_row[:], srow[0:BH, 0:PAST], -1.0, None, ALU.mult).then_inc(negated, 1)
            dve.wait_ge(sums, 1)
            dve.tensor_scalar(prompt_row[:], prow[0:C_HEADS, :], -1.0, None, ALU.mult).then_inc(negated, 1)
            dve.tensor_copy(k["cumq"][:], cols[:, 0:T * C_HEADS].rearrange("p (t h) -> p t h", t=T))
            dve.tensor_scalar(new_row[:], nrow[0:C_HEADS, 0:P], -1.0, None, ALU.mult).then_inc(negated, 1)
    ph.close()


class Group:

    def __init__(self, index, kind, j):
        self.index, self.kind, self.j = index, kind, j
        self.D = B_DIM if kind == "B" else HEAD
        self.maps = P // self.D
        self.per_head = self.maps // 2
        self.packed = P // self.D
        self.nb = DEC_BATCH // self.packed
        self.halves = 1 if kind == "A" else PAST // P
        self.n_past = self.halves * P
        self.n_samp = self.n_past + P
        self.width = 2 * P if kind == "A" else SEQ
        self.tile = {"A": 0, "B": 3, "C": 5}[kind] + j
        self.q_row = {"A": lambda m: (j + 3 * m) * HEAD, "B": lambda m: 512 + j * P + m * B_DIM,
                      "C": lambda m: 1024 + j * P + m * HEAD}[kind]
        self.k_row = {"A": 384, "B": 768 + j * P, "C": 1408 + j * P}[kind]
        self.v_col = {"A": VA, "B": VB + j * P, "C": VC + j * P}[kind]
        self.past_chunks = self.maps * self.nb * self.halves // 4

    def keys(self, i):
        return list(range(max(i - 1, 0) if self.kind == "A" else 0, i + 1))

    def n_cols(self, i):
        return self.n_samp if i == TP else P * len(self.keys(i))

    def n_chunks(self, i):
        return -(-self.n_cols(i) // 512)


def attend(nc, t, k, layer):
    ph = Phase(nc, "att")
    groups = [Group(n, kind, j) for n, (kind, j) in enumerate(
        [("A", 0), ("A", 1), ("A", 2), ("C", 0), ("C", 1), ("C", 2), ("B", 0), ("B", 1)])]
    NG, UG = len(groups), 2 * T
    qT = ph.sb("qT", [P, 2, 4, TOK])
    kT, vn, mixn = ph.sb("kT", [P, 2, TOK]), ph.sb("vn", [P, 2, T, P]), ph.sb("mixn", [P, 2, T, P])
    kp, vp, kpT = ph.sb("kp", [P, 2 * DEC_BATCH, P]), ph.sb("vp", [P, 2, DEC_BATCH, P]), ph.sb("kpT", [P, 2 * DEC_BATCH * P])
    qpast = ph.sb("qpast", [P, 8, P])
    add_p, add_s = ph.sb("add_p", [P, 2, 2, SEQ]), ph.sb("add_s", [P, 2, 2, 3 * P])
    s, p, pT = ph.sb("s", [P, 2, SEQ]), ph.sb("p", [P, 2, 2, SEQ]), ph.sb("pT", [P, 2, SEQ])
    oT, mixTb = ph.sb("oT", [HEAD, P]), ph.sb("mixTb", [P, TOK])
    units = [(g, h, i) for g in groups for h in range(2) for i in range(T)]
    NU = len(units)
    jobs_to = [0]
    for g, h, i in units:
        jobs_to.append(jobs_to[-1] + g.per_head)
    NJ = jobs_to[-1]
    mx, bias, total, inv, esink = (ph.sb(n, [P, NJ]) for n in ("mx", "bias", "total", "inv", "esink"))
    coef = ph.sb("coef", [P, NU])
    sink = ph.sb("sink", [P, A_HEADS])
    mask_f, mask_s = ph.sb("mask_f", [P, P]), ph.sb("mask_s", [P, P])
    mask_b, ident_b = ph.sb("mask_b", [P, P], BF16), ph.sb("ident_b", [P, P], BF16)
    neg_lam, keep, subln = ph.sb("neg_lam", [P, 1]), ph.sb("keep", [P, 1]), ph.sb("subln", [P, HEAD])
    sub_sq = ph.sb("sub_sq", [P, T, P])
    sub_ms, sub_root = ph.sb("sub_ms", [P, UG]), ph.sb("sub_root", [P, UG])
    S, TR, O = ph.ps("S", [P, 2, SEQ]), ph.ps("TR", [P, 2, 512]), ph.ps("O", [P, 2, 512])

    qk_in, v_in, q_zeroed = ([ph.sem(f"{n}{i}") for i in range(2)] for n in ("qk_in", "v_in", "q_zeroed"))
    kp_in, vp_in, qpast_zeroed, qpast_in, const_in = (
        ph.sem(n) for n in ("kp_in", "vp_in", "qpast_zeroed", "qpast_in", "const_in"))
    prepared, masked, scored, biased, bias_ready, exped, sink_ready, inv_ready, weighed, normed = (
        ph.sem(n) for n in ("prepared", "masked", "scored", "biased", "bias_ready", "exped", "sink_ready", "inv_ready", "weighed", "normed"))
    turned, evacuated, multiplied, oT_ready, turned_back, taken_out = (
        ph.sem(n) for n in ("turned", "evacuated", "multiplied", "oT_ready", "turned_back", "taken_out"))
    steps, sub_squared, sub_mean, sub_rooted, sub_done, mix_stored = (
        ph.sem(n) for n in ("steps", "sub_squared", "sub_mean", "sub_rooted", "sub_done", "mix_stored"))

    extra = {}
    for g in groups:
        for c in range(g.past_chunks):
            extra.setdefault(g.index * UG + 2 + c, []).append(("past", g, c))
        for c in range(3):
            extra.setdefault((g.index + 1) * UG + 7 + c, []).append(("mix", g, c))
    N_ITER = NU + 11
    order = []
    for u in range(N_ITER):
        if 1 <= u <= NU:
            g, h, i = units[u - 1]
            order += [("p", u - 1, c) for c in range(g.n_chunks(i))]
        order += [(what, g.index, c) for what, g, c in extra.get(u, [])]
    place = {key: n for n, key in enumerate(order)}
    samples_to = [sum(x[2] == TP for x in units[:u]) for u in range(NU + 1)]
    weighed_to = [sum(x[0].kind == "B" for x in units[:u]) for u in range(NU + 1)]
    sinks_to = [sum(x[0].kind == "A" for x in units[:u]) for u in range(NU + 1)]
    n_qk = {"A": 2 + 1 + 4, "B": 4 + 1 + 4, "C": 2 + 1 + 6}

    def to(g, parity, count):
        return 16 * sum(count(x) for x in groups[:g.index + 1] if parity is None or x.index % 2 == parity)

    def qk_to(g):
        return to(g, g.index % 2, lambda x: n_qk[x.kind])

    def chunk_of_mix(c):
        return c * 4, min(c * 4 + 4, T)

    with nc.Block() as block:
        @block.sync
        def _(sp):
            sp.dma_start(mask_f[:], t["c_causal"]).then_inc(const_in, 16)
            sp.dma_start(mask_s[:], t["c_batch_causal"]).then_inc(const_in, 16)
            sp.dma_start(sink[:], t["sinks_a"][layer].unsqueeze(0).broadcast_to([P, A_HEADS])).then_inc(const_in, 16)
            sp.dma_start(subln[:], t["subln_b"][layer].unsqueeze(0).broadcast_to([P, HEAD])).then_inc(const_in, 16)
            sp.dma_start(keep[:], t["c_lam"][1:2, bass.ds(layer, 1)].broadcast_to([P, 1])).then_inc(const_in, 16)
            qkv = t["qkv"].rearrange("(t p) n -> p t n", p=P)

            def load_front(g):
                b, j, kind, sem = g.index % 2, g.j, g.kind, qk_in[g.index % 2]
                if g.index >= 2:
                    sp.wait_ge(scored, jobs_to[(g.index - 1) * UG])
                    sp.wait_ge(biased, jobs_to[(g.index - 1) * UG])
                sp.wait_ge(q_zeroed[b], 1 + (kind == "B"))
                for m in range(g.maps):
                    sp.dma_start(qT[m * g.D:(m + 1) * g.D, b, m, :], t["qkT"][g.q_row(m):g.q_row(m) + g.D, :]).then_inc(sem, 16)
                sp.dma_start(kT[:, b, :], t["qkT"][g.k_row:g.k_row + P, :]).then_inc(sem, 16)
                for h in range(2):
                    if kind == "A":
                        sp.dma_start(add_p[:, b, h, 0:g.width], t["bias_a"][j + 3 * h]).then_inc(sem, 16)
                        sp.dma_start(add_s[:, b, h, 0:g.n_samp], t["bias_sa"][j + 3 * h]).then_inc(sem, 16)
                    elif kind == "B":
                        sp.dma_start(add_p[:, b, h, :], t["bias_b"][2 * j + h]).then_inc(sem, 16)
                        sp.dma_start(add_s[:, b, h, :], t["bias_sb"][2 * j + h]).then_inc(sem, 16)
                    else:
                        head = slice(2 * j + h, 2 * j + h + 1)
                        sp.dma_start(add_p[:, b, h, :], t["cum_prompt"][head, :].broadcast_to([P, SEQ])).then_inc(sem, 16)
                        past = t["cum_past"].rearrange("(b h) n -> b h n", h=C_HEADS)[:, head, :]
                        sp.dma_start(add_s[:, b, h, 0:PAST], past.broadcast_to([DEC_BATCH, DEC_SEQ, PAST])).then_inc(sem, 16)
                        sp.dma_start(add_s[:, b, h, PAST:g.n_samp], t["cum_new"][head, :].broadcast_to([P, P])).then_inc(sem, 16)
                if g.index >= 2:
                    sp.wait_ge(multiplied, (g.index - 1) * UG)
                sp.dma_start(vn[:, b, :, :], qkv[:, :, g.v_col:g.v_col + P]).then_inc(v_in[b], 16)

            def load_past(g):
                low, D = g.kind.lower(), g.D
                src = t[f"cache_{low}_k"][layer]
                src = src.rearrange("b p h m d -> b p (h m) d") if g.kind == "B" else src
                if g.index:
                    sp.wait_ge(turned, place["past", g.index - 1, groups[g.index - 1].past_chunks - 1] + 1)
                for f in range(g.halves):
                    for m in range(g.maps):
                        head = m if g.kind == "A" else g.j * g.maps + m
                        at = (f * g.maps + m) * DEC_BATCH * D
                        sp.dma_start(kp[:].rearrange("p x n -> p (x n)")[:, at:at + DEC_BATCH * D].rearrange("p (b d) -> p b d", d=D),
                                     src[:, f * P:(f + 1) * P, head, :].rearrange("b p d -> p b d")).then_inc(kp_in, 16)
                if g.index:
                    sp.wait_ge(multiplied, g.index * UG)
                src = t[f"cache_{low}_v"][layer].rearrange("b p h d -> p b (h d)")
                for f in range(g.halves):
                    cols = slice(0, P) if g.kind == "A" else slice(g.j * P, (g.j + 1) * P)
                    sp.dma_start(vp[:, f, :, :], src[f * P:(f + 1) * P, :, cols]).then_inc(vp_in, 16)
                sp.wait_ge(qpast_zeroed, g.index + 1)
                with nc.allow_non_contiguous_dma(reason="16 tokens per batch"):
                    for m in range(g.maps):
                        for r in range(g.packed):
                            dst = qpast[r * D:(r + 1) * D, m * g.nb, r * DEC_SEQ:(r + 1) * DEC_SEQ]
                            dst = bass.AP(dst.tensor, dst.offset, [list(dst.ap[0]), [P + g.packed * DEC_SEQ, g.nb], [1, DEC_SEQ]])
                            row = t["qkT"][g.q_row(m):g.q_row(m) + D, SEQ:TOK]
                            sp.dma_start(dst, row.rearrange("d (c r s) -> d c r s", r=g.packed, s=DEC_SEQ)[:, :, r, :]).then_inc(qpast_in, 16)

            load_front(groups[0])
            load_past(groups[0])
            load_front(groups[1])
            for g in groups:
                if g.index + 1 < NG:
                    load_past(groups[g.index + 1])
                if g.index + 2 < NG:
                    load_front(groups[g.index + 2])
                sp.wait_ge(evacuated, place["mix", g.index, 2] + 1)
                sp.dma_start(t["mixT"][g.tile * P:(g.tile + 1) * P, :], mixTb[:]).then_inc(mix_stored, 16)
            sp.wait_ge(mix_stored, 16 * NG)

        @block.gpsimd
        def _(pool):
            for b in range(2):
                pool.memset(qT[:, b, 0:2, :], 0.0).then_inc(q_zeroed[b], 1)
            for g in groups:
                if g.index:
                    pool.wait_ge(scored, jobs_to[g.index * UG])
                pool.memset(qpast[:], 0.0).then_inc(qpast_zeroed, 1)
                if g.index + 1 < NG and groups[g.index + 1].kind == "B":
                    pool.memset(qT[:, (g.index + 1) % 2, :, :], 0.0).then_inc(q_zeroed[(g.index + 1) % 2], 1)

        @block.tensor
        def _(pe):
            def score(u):
                g, h, i = units[u]
                b = g.index % 2
                if u % UG == 0:
                    pe.wait_ge(qk_in[b], qk_to(g))
                if i == TP:
                    pe.wait_ge(qpast_in, to(g, None, lambda x: x.maps * x.packed))
                    pe.wait_ge(evacuated, place["past", g.index, g.past_chunks - 1] + 1)
                if g.kind == "C" and u % UG == 0:
                    pe.wait_ge(prepared, 1)
                for r in range(g.per_head):
                    job = jobs_to[u] + r
                    m = h * g.per_head + r
                    if job >= 2:
                        pe.wait_ge(biased, job - 1)
                    out, q = S[:, job % 2, :], qT[:, b, m, i * P:(i + 1) * P]
                    if i < TP:
                        k0, n = g.keys(i)[0] * P, g.n_cols(i)
                        for c in range(0, n, 512):
                            w = min(512, n - c)
                            last = pe.matmul(out[:, c:c + w], q, kT[:, b, k0 + c:k0 + c + w], start=True,
                                             stop=not (g.kind == "C" and c + w == n))
                        if g.kind == "C":
                            last = pe.matmul(out[:, n - P:n], ident_b[:], mask_b[:], start=False, stop=True)
                    else:
                        for c in range(g.nb):
                            x = m * g.nb + c
                            pe.matmul(out[:, 0:g.n_past], qpast[:, x, :], kpT[:, x * g.n_past:(x + 1) * g.n_past],
                                      start=(c == 0), stop=(c == g.nb - 1))
                        last = pe.matmul(out[:, g.n_past:g.n_samp], q, kT[:, b, SEQ:TOK], start=True, stop=True)
                    last.then_inc(scored, 1)

            def turn(u):
                g, h, i = units[u]
                if i == TP:
                    pe.wait_ge(normed, samples_to[u + 1])
                elif g.kind == "B":
                    pe.wait_ge(weighed, weighed_to[u + 1])
                else:
                    pe.wait_ge(exped, jobs_to[u + 1])
                for c in range(g.n_chunks(i)):
                    n = place["p", u, c]
                    if n >= 2:
                        pe.wait_ge(evacuated, n - 1)
                    for x in range(4 * c, min(4 * c + 4, g.n_cols(i) // P)):
                        last = pe.transpose(TR[:, n % 2, x % 4 * P:(x % 4 + 1) * P], p[:, u % 2, 0, x * P:(x + 1) * P], k["ident"][:])
                    last.then_inc(turned, 1)

            def turn_extra(what, g, c):
                n = place[what, g.index, c]
                if n >= 2:
                    pe.wait_ge(evacuated, n - 1)
                if what == "past":
                    if c == 0:
                        pe.wait_ge(kp_in, to(g, None, lambda x: x.halves * x.maps))
                    for x in range(4 * c, 4 * c + 4):
                        mb, f = divmod(x, g.halves)
                        m, nb = divmod(mb, g.nb)
                        at = ((f * g.maps + m) * g.nb + nb)
                        last = pe.transpose(TR[:, n % 2, x % 4 * P:(x % 4 + 1) * P], kp[:, at, :], k["ident"][:])
                else:
                    if c == 0 and g.kind == "B":
                        pe.wait_ge(sub_done, g.j + 1)
                    elif c == 0:
                        pe.wait_ge(taken_out, (g.index + 1) * UG)
                    a, e = chunk_of_mix(c)
                    for x in range(a, e):
                        last = pe.transpose(TR[:, n % 2, (x - a) * P:(x - a + 1) * P], mixn[:, g.index % 2, x, :], k["ident"][:])
                last.then_inc(turned, 1)

            def values(u):
                g, h, i = units[u]
                b = g.index % 2
                if u % UG == 0:
                    pe.wait_ge(v_in[b], to(g, b, lambda x: 1))
                pe.wait_ge(evacuated, place["p", u, g.n_chunks(i) - 1] + 1)
                if u >= 2:
                    pe.wait_ge(taken_out, u - 1)
                v = slice(h * HEAD, (h + 1) * HEAD)
                if i < TP:
                    ks = g.keys(i)
                    for x, kt in enumerate(ks):
                        last = pe.matmul(O[:, u % 2, 0:HEAD], pT[:, u % 2, x * P:(x + 1) * P], vn[:, b, kt, v],
                                         start=(x == 0), stop=(x == len(ks) - 1))
                else:
                    pe.wait_ge(vp_in, to(g, None, lambda x: x.halves))
                    pe.matmul(O[0:HEAD, u % 2, 0:P], vn[:, b, TP, v], pT[:, u % 2, g.n_past:g.n_samp], start=True, stop=False,
                              skip_group_check=True)
                    for d in range(DEC_BATCH):
                        for f in range(g.halves):
                            own = slice(d * DEC_SEQ, (d + 1) * DEC_SEQ)
                            last = pe.matmul(O[0:HEAD, u % 2, own], vp[:, f, d, v], pT[:, u % 2, f * P + d * DEC_SEQ:f * P + (d + 1) * DEC_SEQ],
                                             start=False, stop=(d == DEC_BATCH - 1 and f == g.halves - 1), skip_group_check=True)
                last.then_inc(multiplied, 1)

            def turn_back(u):
                if units[u][2] == TP:
                    pe.wait_ge(oT_ready, samples_to[u + 1])
                    pe.transpose(O[:, u % 2, P:P + HEAD], oT[:], k["ident"][0:HEAD, 0:HEAD]).then_inc(turned_back, 1)

            for u in range(N_ITER):
                if u < NU:
                    score(u)
                if 1 <= u <= NU:
                    turn(u - 1)
                for what, g, c in extra.get(u, []):
                    turn_extra(what, g, c)
                if 2 <= u <= NU + 1:
                    values(u - 2)
                if 3 <= u <= NU + 2:
                    turn_back(u - 3)

        @block.scalar
        def _(act):
            def exps(u):
                g, h, i = units[u]
                n = g.n_cols(i)
                if u >= 2:
                    g2, _, i2 = units[u - 2]
                    act.wait_ge(turned, place["p", u - 2, g2.n_chunks(i2) - 1] + 1)
                for r in range(g.per_head):
                    job = jobs_to[u] + r
                    act.wait_ge(bias_ready, job + 1)
                    act.activation(p[:, u % 2, r, 0:n], s[:, job % 2, 0:n], ACT.Exp, bias=bias[:, job:job + 1],
                                   accum_out=total[:, job:job + 1]).then_inc(exped, 1)
                    if g.kind == "A":
                        head = g.j + 3 * h
                        act.activation(esink[:, job:job + 1], sink[:, head:head + 1], ACT.Exp, bias=bias[:, job:job + 1]).then_inc(sink_ready, 1)

            def evacuate(u):
                g, h, i = units[u]
                for c in range(g.n_chunks(i)):
                    n = place["p", u, c]
                    act.wait_ge(turned, n + 1)
                    if u >= 2 and c == 0:
                        act.wait_ge(multiplied, u - 1)
                    w = min(512, g.n_cols(i) - c * 512)
                    act.activation(pT[:, u % 2, c * 512:c * 512 + w], TR[:, n % 2, 0:w], ACT.Copy).then_inc(evacuated, 1)

            def evacuate_extra(what, g, c):
                n = place[what, g.index, c]
                act.wait_ge(turned, n + 1)
                if what == "past":
                    if c == 0 and g.index:
                        act.wait_ge(scored, jobs_to[g.index * UG])
                    act.activation(kpT[:, c * 512:(c + 1) * 512], TR[:, n % 2, :], ACT.Copy).then_inc(evacuated, 1)
                else:
                    if c == 0 and g.index:
                        act.wait_ge(mix_stored, 16 * g.index)
                    a, e = chunk_of_mix(c)
                    act.activation(mixTb[:, a * P:e * P], TR[:, n % 2, 0:(e - a) * P], ACT.Copy).then_inc(evacuated, 1)

            def take_oT(u):
                if units[u][2] == TP:
                    act.wait_ge(multiplied, u + 1)
                    if samples_to[u]:
                        act.wait_ge(turned_back, samples_to[u])
                    act.activation(oT[:], O[0:HEAD, u % 2, 0:P], ACT.Copy).then_inc(oT_ready, 1)

            def sub_root_of(g):
                act.wait_ge(sub_mean, g.j + 1)
                act.activation(sub_root[:], sub_ms[:], ACT.Sqrt).then_inc(sub_rooted, 1)

            for u in range(N_ITER):
                if 1 <= u <= NU:
                    evacuate(u - 1)
                if u < NU:
                    exps(u)
                for what, g, c in extra.get(u, []):
                    evacuate_extra(what, g, c)
                if 2 <= u <= NU + 1:
                    take_oT(u - 2)
                for g in groups:
                    if g.kind == "B" and u == (g.index + 1) * UG + 4:
                        sub_root_of(g)

        @block.vector
        def _(dve):
            chain = Count(steps)

            def then(ins):
                dve.wait_ge(steps, chain.on(ins))

            dve.wait_ge(const_in, 16 * 5)
            then(dve.tensor_scalar(neg_lam[:], k["lam"][:], -1.0, None, ALU.mult))
            then(dve.tensor_scalar(subln[:], subln[:], keep[:, 0:1], None, ALU.mult))
            dve.tensor_copy(mask_b[:], mask_f[:])
            dve.tensor_copy(ident_b[:], k["ident"][:]).then_inc(prepared, 1)

            def front(u):
                g, h, i = units[u]
                b, n = g.index % 2, g.n_cols(i)
                if u % UG == 0:
                    dve.wait_ge(qk_in[b], qk_to(g))
                    if g.kind == "C":
                        for x in range(2):
                            last = dve.tensor_tensor(add_s[:, b, x, PAST:g.n_samp], add_s[:, b, x, PAST:g.n_samp], mask_s[:], ALU.add)
                        then(last)
                for r in range(g.per_head):
                    job = jobs_to[u] + r
                    dve.wait_ge(scored, job + 1)
                    if job >= 2:
                        dve.wait_ge(exped, job - 1)
                    extra_row = (add_s[:, b, h, 0:n] if i == TP else add_p[:, b, h, 0:n] if g.kind == "C"
                                 else add_p[:, b, h, g.width - n:g.width])
                    one = slice(job, job + 1)
                    dve.tensor_tensor_reduce(s[:, job % 2, 0:n], S[:, job % 2, 0:n], extra_row, 1.0, -3e38, ALU.add, ALU.max, mx[:, one]).then_inc(biased, 1)
                    dve.wait_ge(biased, job + 1)
                    if g.kind == "A":
                        head = g.j + 3 * h
                        dve.tensor_scalar(bias[:, one], mx[:, one], sink[:, head:head + 1], -1.0, ALU.max, ALU.mult).then_inc(bias_ready, 1)
                    elif g.kind == "B":
                        dve.tensor_scalar(bias[:, one], mx[:, one], -1.0, None, ALU.mult).then_inc(bias_ready, 1)
                    else:
                        own = k["cumq"][:, i, 2 * g.j + h:2 * g.j + h + 1]
                        then(dve.tensor_tensor(mx[:, one], mx[:, one], own, ALU.add))
                        dve.tensor_tensor(bias[:, one], own, mx[:, one], ALU.subtract).then_inc(bias_ready, 1)

            def back(u):
                g, h, i = units[u]
                n = g.n_cols(i)
                a, e = jobs_to[u], jobs_to[u + 1]
                dve.wait_ge(exped, e)
                if g.kind == "A":
                    dve.wait_ge(sink_ready, sinks_to[u + 1])
                    then(dve.tensor_tensor(total[:, a:e], total[:, a:e], esink[:, a:e], ALU.add))
                dve.reciprocal(inv[:, a:e], total[:, a:e]).then_inc(inv_ready, 1)
                if g.kind != "B" and i < TP:
                    return
                dve.wait_ge(inv_ready, u + 1)
                if g.kind == "B":
                    then(dve.scalar_tensor_tensor(out=coef[:, u:u + 1], in0=total[:, a:a + 1], scalar=inv[:, a + 1:a + 2],
                                                  in1=neg_lam[:], op0=ALU.mult, op1=ALU.mult))
                    dve.scalar_tensor_tensor(out=p[:, u % 2, 0, 0:n], in0=p[:, u % 2, 1, 0:n], scalar=coef[:, u:u + 1],
                                             in1=p[:, u % 2, 0, 0:n], op0=ALU.mult, op1=ALU.add).then_inc(weighed, 1)
                    if i == TP:
                        dve.wait_ge(weighed, weighed_to[u + 1])
                if i == TP:
                    dve.tensor_scalar(p[:, u % 2, 0, 0:n], p[:, u % 2, 0, 0:n], inv[:, a:a + 1], None, ALU.mult).then_inc(normed, 1)

            def take_out(u, late):
                g, h, i = units[u]
                if (i == TP) != late:
                    return
                if h == 0 and i == 0 and g.index >= 2:
                    dve.wait_ge(turned, place["mix", g.index - 2, 2] + 1)
                dst = mixn[:, g.index % 2, i, h * HEAD:(h + 1) * HEAD]
                if late:
                    dve.wait_ge(turned_back, samples_to[u + 1])
                    dve.tensor_copy(dst, O[:, u % 2, P:P + HEAD]).then_inc(taken_out, 1)
                else:
                    dve.wait_ge(multiplied, u + 1)
                    dve.wait_ge(inv_ready, u + 1)
                    a = jobs_to[u]
                    dve.tensor_scalar(dst, O[:, u % 2, 0:HEAD], inv[:, a:a + 1], None, ALU.mult).then_inc(taken_out, 1)

            def sub_norm(g):
                rows_ = mixn[:, g.index % 2, :, :].rearrange("p t (h d) -> p (t h) d", d=HEAD)
                sq = sub_sq[:].rearrange("p t (h d) -> p (t h) d", d=HEAD)
                dve.wait_ge(taken_out, (g.index + 1) * UG)
                then(dve.tensor_tensor(sq, rows_, rows_, ALU.mult))
                then(dve.tensor_reduce(sub_ms[:], sq, AX.X, ALU.add))
                dve.tensor_scalar(sub_ms[:], sub_ms[:], 1.0 / HEAD, EPS, ALU.mult, ALU.add).then_inc(sub_mean, 1)

            def sub_scale(g):
                rows_ = mixn[:, g.index % 2, :, :].rearrange("p t (h d) -> p (t h) d", d=HEAD)
                dve.wait_ge(sub_rooted, g.j + 1)
                then(dve.reciprocal(sub_ms[:], sub_root[:]))
                then(dve.tensor_tensor(rows_, rows_, sub_ms[:].unsqueeze(2).broadcast_to([P, UG, HEAD]), ALU.mult))
                dve.tensor_tensor(rows_, rows_, subln[:].unsqueeze(1).broadcast_to([P, UG, HEAD]), ALU.mult).then_inc(sub_done, 1)

            for u in range(N_ITER):
                if 1 <= u <= NU:
                    back(u - 1)
                if u < NU:
                    front(u)
                if 3 <= u <= NU + 2:
                    take_out(u - 3, True)
                if 2 <= u <= NU + 1:
                    take_out(u - 2, False)
                for g in groups:
                    if g.kind == "B" and u == (g.index + 1) * UG + 3:
                        sub_norm(g)
                    if g.kind == "B" and u == (g.index + 1) * UG + 5:
                        sub_scale(g)
    ph.close()

def mix(nc, t, k, layer):
    ph = Phase(nc, "mix")
    w = ph.sb("w", [P, KD, D_MODEL])
    mixT = ph.sb("mixT", [P, KD, TOK])
    acc = ph.ps("acc", [P, 4, 512])
    w_in, done, added = (ph.sem(n) for n in ("w_in", "done", "added"))
    src = t["w_out"][layer]
    pieces = 1 + 2 * 3 + 5
    with nc.Block() as block:
        @block.sync
        def _(sp):
            sp.dma_start(mixT[:], t["mixT"].rearrange("(g p) n -> p g n", p=P)).then_inc(w_in, 16)
            for j in range(3):
                for h in range(2):
                    r = (j + 3 * h) * HEAD
                    sp.dma_start(w[h * HEAD:(h + 1) * HEAD, j, :], src[r:r + HEAD, :]).then_inc(w_in, 16)
            for g in range(3, KD):
                sp.dma_start(w[:, g, :], src[g * P:(g + 1) * P, :]).then_inc(w_in, 16)

        @block.tensor
        def _(pe):
            pe.wait_ge(w_in, 16 * pieces)
            for u in range(2 * T):
                i, c = divmod(u, 2)
                if u >= 4:
                    pe.wait_ge(added, u - 3)
                for g in range(KD):
                    last = pe.matmul(acc[:, u % 4, :], mixT[:, g, i * P:(i + 1) * P], w[:, g, c * 512:(c + 1) * 512],
                                     start=(g == 0), stop=(g == KD - 1))
                last.then_inc(done, 1)

        @block.vector
        def _(dve):
            for u in range(2 * T):
                i, c = divmod(u, 2)
                x = k["x"][:, i, c * 512:(c + 1) * 512]
                dve.wait_ge(done, u + 1)
                dve.tensor_tensor(x, x, acc[:, u % 4, :], ALU.add).then_inc(added, 1)
    ph.close()


def feed(nc, t, k, layer):
    norm = Phase(nc, "nrm")
    h_hi, h_lo = norm.sb("h_hi", [P, KD, TOK], F32R), norm.sb("h_lo", [P, KD, TOK], F32R)
    gain = norm.sb("gain", [P, KD])
    inner = Phase(nc, "nri")
    parts = norm_transpose(inner, k, gain, h_hi, h_lo, inner.sb("h32", [P, 2, D_MODEL]))
    g_in = inner.sem("g_in")
    with nc.Block() as block:
        @block.sync
        def _(sp):
            with nc.allow_non_contiguous_dma(reason="gain vector"):
                sp.dma_start(gain[:], t["norm_ffn"][layer].rearrange("(k p) -> p k", p=P)).then_inc(g_in, 16)

        @block.tensor
        def _(pe):
            parts["pe"](pe)

        @block.scalar
        def _(act):
            parts["act"](act)

        @block.vector
        def _(dve):
            dve.wait_ge(g_in, 16)
            parts["dve"](dve)
    inner.close()
    ph = Phase(nc, "ffn")
    NT = 3
    ND = 2 * T
    raw = {n: ph.sb(f"raw_{n}", shape) for n, shape in (("g", [P, KD, P]), ("u", [P, KD, P]), ("d", [P, D_MODEL]))}
    hi = {n: ph.sb(f"hi_{n}", [P, 2] + shape, F32R) for n, shape in (("g", [KD, P]), ("u", [KD, P]), ("d", [D_MODEL]))}
    lo = {n: ph.sb(f"lo_{n}", [P, 2] + shape, F32R) for n, shape in (("g", [KD, P]), ("u", [KD, P]), ("d", [D_MODEL]))}
    sg, a32 = ph.sb("sg", [P, 2, 384]), ph.sb("a32", [P, 2, 384])
    a_hi, a_lo = ph.sb("a_hi", [P, 2, TOK], F32R), ph.sb("a_lo", [P, 2, TOK], F32R)
    up = ph.ps("up", [P, 2, 2, 512])
    down = ph.ps("down", [P, 4, 512])
    came = {n: ph.sem(f"came_{n}") for n in "gud"}
    high = {n: ph.sem(f"high_{n}") for n in "gud"}
    cut = {n: ph.sem(f"cut_{n}") for n in "gud"}
    upped, activated, gated, a_high, a_cut, downed, added = (
        ph.sem(n) for n in ("upped", "activated", "gated", "a_high", "a_cut", "downed", "added"))
    src = {"g": t["w_gate"][layer].rearrange("(k p) n -> p k n", p=P),
           "u": t["w_up"][layer].rearrange("(k p) n -> p k n", p=P)}

    def steps(eng, step):
        step(0, 0)
        step(1, 1)
        with eng.Fori(1, KF // 2 - 1) as pair:
            for q in range(2):
                step(2 * pair + q, q)
        step(KF - 2, 0)
        step(KF - 1, 1)

    def at(f, *tiles):
        return isinstance(f, int) and f in tiles

    def three_passes(pe, out, l_hi, l_lo, r_hi, r_lo, first, final):
        pe.matmul(out, l_hi, r_hi, start=first, stop=False)
        pe.matmul(out, l_hi, r_lo, start=False, stop=False)
        return pe.matmul(out, l_lo, r_hi, start=False, stop=final)

    with nc.Block() as block:
        @block.sync
        def _(sp):
            def load(n, f):
                if not at(f, 0):
                    sp.wait_ge(cut[n], f)
                piece = t["w_down"][layer][bass.ds(f * P, P), :] if n == "d" else src[n][:, :, bass.ds(f * P, P)]
                sp.dma_start(raw[n][:], piece).then_inc(came[n], 16)

            def step(f, q):
                if not at(f, KF - 1):
                    load("g", f + 1)
                    load("u", f + 1)
                load("d", f)

            load("g", 0)
            load("u", 0)
            steps(sp, step)

        @block.tensor
        def _(pe):
            def ups(f, q):
                for n in range(NT):
                    v = f * NT + n
                    b = (q * NT + n) % 2
                    if not (at(f, 0) and n < 2):
                        pe.wait_ge(gated, v - 1)
                    span = slice(n * 384, (n + 1) * 384)
                    for which, w in ((0, "g"), (1, "u")):
                        if n == 0:
                            pe.wait_ge(cut[w], f + 1)
                        for c in range(KD):
                            last = three_passes(pe, up[:, b, which, 0:384], hi[w][:, q, c, :], lo[w][:, q, c, :],
                                                h_hi[:, c, span], h_lo[:, c, span], c == 0, c == KD - 1)
                    last.then_inc(upped, 1)

            def downs(f, q):
                pe.wait_ge(cut["d"], f + 1)
                pe.wait_ge(a_cut, f * NT + NT)
                for n in range(ND):
                    i, c = divmod(n, 2)
                    if not (at(f, 0) and n < 4):
                        pe.wait_ge(added, f * ND + n - 3)
                    tok, col = slice(i * P, (i + 1) * P), slice(c * 512, (c + 1) * 512)
                    three_passes(pe, down[:, (q * ND + n) % 4, :], a_hi[:, q, tok], a_lo[:, q, tok],
                                 hi["d"][:, q, col], lo["d"][:, q, col], True, True).then_inc(downed, 1)

            def step(f, q):
                ups(f, q)
                if not at(f, 0):
                    downs(f - 1, 1 - q)

            steps(pe, step)
            downs(KF - 1, 1)

        @block.scalar
        def _(act):
            def raise_weight(n, f, q):
                act.wait_ge(came[n], f * 16 + 16)
                if not at(f, 0, 1):
                    act.wait_ge(*((downed, (f - 1) * ND) if n == "d" else (upped, (f - 1) * NT)))
                split_hi(act, hi[n][:, q], raw[n][:]).then_inc(high[n], 1)

            def step(f, q):
                if not at(f, KF - 1):
                    raise_weight("g", f + 1, 1 - q)
                    raise_weight("u", f + 1, 1 - q)
                raise_weight("d", f, q)
                for n in range(NT):
                    v = f * NT + n
                    b = (q * NT + n) % 2
                    span = slice(n * 384, (n + 1) * 384)
                    act.wait_ge(upped, v + 1)
                    if not (at(f, 0) and n < 2):
                        act.wait_ge(gated, v - 1)
                    act.activation(sg[:, b, :], up[:, b, 0, 0:384], ACT.Silu).then_inc(activated, 1)
                    act.wait_ge(gated, v + 1)
                    split_hi(act, a_hi[:, q, span], a32[:, b, :]).then_inc(a_high, 1)

            raise_weight("g", 0, 0)
            raise_weight("u", 0, 0)
            steps(act, step)

        @block.vector
        def _(dve):
            def cut_weight(n, f, q):
                dve.wait_ge(high[n], f + 1)
                split_lo(dve, lo[n][:, q], raw[n][:], hi[n][:, q]).then_inc(cut[n], 1)

            def add(f, q):
                for n in range(ND):
                    i, c = divmod(n, 2)
                    x = k["x"][:, i, c * 512:(c + 1) * 512]
                    dve.wait_ge(downed, f * ND + n + 1)
                    dve.tensor_tensor(x, x, down[:, (q * ND + n) % 4, :], ALU.add).then_inc(added, 1)

            def step(f, q):
                if not at(f, KF - 1):
                    cut_weight("g", f + 1, 1 - q)
                    cut_weight("u", f + 1, 1 - q)
                cut_weight("d", f, q)
                for n in range(NT):
                    v = f * NT + n
                    b = (q * NT + n) % 2
                    span = slice(n * 384, (n + 1) * 384)
                    dve.wait_ge(activated, v + 1)
                    if not (at(f, 0) and n < 2):
                        dve.wait_ge(a_cut, v - 1)
                    if n == 0 and not at(f, 0, 1):
                        dve.wait_ge(downed, (f - 1) * ND)
                    dve.tensor_tensor(a32[:, b, :], sg[:, b, :], up[:, b, 1, 0:384], ALU.mult).then_inc(gated, 1)
                    dve.wait_ge(gated, v + 1)
                    dve.wait_ge(a_high, v + 1)
                    split_lo(dve, a_lo[:, q, span], a32[:, b, :], a_hi[:, q, span]).then_inc(a_cut, 1)
                if not at(f, 0):
                    add(f - 1, 1 - q)

            cut_weight("g", 0, 0)
            cut_weight("u", 0, 0)
            steps(dve, step)
            add(KF - 1, 1)
    ph.close()
    norm.close()


def finish(nc, t, k):
    ph = Phase(nc, "fin")
    y_out = ph.sem("y_out")
    with nc.Block() as block:
        @block.sync
        def _(sp):
            sp.dma_start(t["y_prompt"].rearrange("a (t p) d -> p (a t) d", p=P), k["x"][:, 0:TP, :]).then_inc(y_out, 16)
            sp.dma_start(t["y_sample"].rearrange("b s d -> (b s) d"), k["x"][:, TP, :]).then_inc(y_out, 16)
            sp.wait_ge(y_out, 32)
    ph.close()


_INS = ["x_prompt", "x_sample", "cache_a_k", "cache_a_v", "cache_b_k", "cache_b_v", "cache_c_k", "cache_c_v",
        "cache_c_logf", "rel_bias_table", "norm_mix", "w_in", "b_forget", "q_norm_a", "k_norm_a", "sinks_a",
        "q_norm_b", "k_norm_b", "lam_q1", "lam_k1", "lam_q2", "lam_k2", "subln_b", "q_norm_c", "k_norm_c",
        "w_out", "norm_ffn", "w_gate", "w_up", "w_down"]


def _heads(lead):
    return {"a_k": lead + (A_KV, HEAD), "a_v": lead + (A_KV, HEAD), "b_k": lead + (B_HEADS, 2, B_DIM),
            "b_v": lead + (B_HEADS, HEAD), "c_k": lead + (C_HEADS, HEAD), "c_v": lead + (C_HEADS, HEAD),
            "c_logf": lead + (C_HEADS,)}


_OUTS = {"y_prompt": (1, SEQ, D_MODEL), "y_sample": (DEC_BATCH, DEC_SEQ, D_MODEL)}
_OUTS.update({"p_" + n: v for n, v in _heads((DEPTH, 1, SEQ)).items()})
_OUTS.update({"s_" + n: v for n, v in _heads((DEPTH, DEC_BATCH, DEC_SEQ)).items()})
for _kv in "kv":
    _OUTS[f"p_a_{_kv}"] = (DEPTH, 1, WINDOW, A_KV, HEAD)
    _OUTS[f"s_a_{_kv}"] = (DEPTH, DEC_BATCH, WINDOW, A_KV, HEAD)

_SCRATCH = {"qkv": (TOK, FZ), "qkT": (1792, TOK), "mixT": (D_MODEL, TOK), "bias_rows": (A_HEADS + B_HEADS, P, REL), "bias_a": (A_HEADS, P, 2 * P),
            "bias_b": (B_HEADS, P, SEQ), "bias_sa": (A_HEADS, P, 2 * P), "bias_sb": (B_HEADS, P, 3 * P),
            "cum_prompt": (C_HEADS, SEQ), "cum_past": (DEC_BATCH * C_HEADS, PAST), "cum_new": (C_HEADS, P)}


def kernel(**inputs):
    import concourse.bacc as _bacc
    from concourse.bass_utils import run_bass_kernel_spmd as _run

    nc = _bacc.Bacc("TRN2", target_bir_lowering=False, num_devices=1)
    arrays, t = {}, {}
    for name in _INS:
        arrays[f"in_{name}"] = np.ascontiguousarray(inputs[name])
    for name, a in constants().items():
        arrays[f"in_{name}"] = a
    for name, a in arrays.items():
        t[name[3:]] = nc.dram_tensor(name, a.shape, mybir.dt.from_np(a.dtype), kind="ExternalInput").ap()
    for name, shape in _OUTS.items():
        t[name] = nc.dram_tensor(f"out_{name}", shape, F32, kind="ExternalOutput").ap()
    for name, shape in _SCRATCH.items():
        t[name] = nc.dram_tensor(f"scratch_{name}", shape, F32).ap()
    build(nc, t)
    r = _run(nc, [arrays], core_ids=[0])
    return tuple(r.results[0][f"out_{name}"] for name in _OUTS)
```

```python
from contextlib import ExitStack

import numpy as np

import concourse.bass as bass
from concourse import mybir

P = 128
D_MODEL, SEQ, DEPTH, DEC_BATCH, DEC_SEQ, PAST = 1024, 1024, 2, 8, 16, 256
CHUNK, HEAD = 64, 64
A_HEADS, A_KV, B_HEADS, B_DIM, C_HEADS = 6, 2, 4, 32, 6
WINDOW = 128
D_FF = 2816
N_BUCKETS, MAX_DISTANCE = 32, 1024
EPS, NEG = 1e-6, -1e30
TP = SEQ // P
T = TP + 1
TOK = T * P
KD = D_MODEL // P
KF = D_FF // P
QA, KA, VA = 0, 384, 512
QB, KB, VB = 640, 896, 1152
QC, KC, VC = 1408, 1792, 2176
FZ = 2560
N_IN = FZ + C_HEADS
IN_BLOCKS = [(QA, 512), (VA, 384), (KB, 512), (QC, 384), (KC, 384), (VC, 384)]
GATE_BLOCK = 1
NORMED = [(0, 8, HEAD), (128, 8, B_DIM), (0, 8, B_DIM), (0, 6, HEAD), (0, 6, HEAD), None]
GAINS = [("q_norm_a", 0, 6, HEAD, HEAD ** -0.5), ("k_norm_a", 384, 2, HEAD, None),
         ("q_norm_b", 512, 8, B_DIM, B_DIM ** -0.5), ("k_norm_b", 768, 8, B_DIM, None),
         ("q_norm_c", 1024, 6, HEAD, HEAD ** -0.5), ("k_norm_c", 1408, 6, HEAD, None)]
GAIN_AT = [0, 512, 768, 1024, 1408]
REL0 = SEQ - 1 + P
REL = REL0 + P + 1
COPIES = DEC_SEQ

F32 = mybir.dt.float32
BF16 = mybir.dt.bfloat16
F32R = mybir.dt.float32r
ALU = mybir.AluOpType
ACT = mybir.ActivationFunctionType
AX = mybir.AxisListType


def constants():
    i = np.arange(P)
    upper = (i[:, None] <= i[None, :]).astype(np.float32)
    same = (i[:, None] // DEC_SEQ == i[None, :] // DEC_SEQ)
    rel = np.arange(REL) - REL0
    n = np.abs(rel)
    half, exact = N_BUCKETS // 2, N_BUCKETS // 4
    large = exact + (np.log(np.maximum(n, 1).astype(np.float32) / exact)
                     / np.float32(np.log(MAX_DISTANCE / exact)) * (half - exact)).astype(np.int32)
    bucket = np.where(rel > 0, half, 0) + np.where(n < exact, n, np.minimum(large, half - 1))
    bh = np.arange(DEC_BATCH * C_HEADS)
    lam_init = 0.8 - 0.6 * np.exp(-0.3 * np.arange(DEPTH))
    return {
        "c_ident": np.eye(P, dtype=np.float32),
        "c_upper": np.concatenate([upper, np.ones((P, P), np.float32)], 1),
        "c_upper_batch": upper * same,
        "c_causal": np.where(i[None, :] <= i[:, None], 0.0, NEG).astype(np.float32),
        "c_batch": np.where(same, 0.0, NEG).astype(np.float32),
        "c_batch_causal": np.where(same & (i[None, :] <= i[:, None]), 0.0, NEG).astype(np.float32),
        "c_buckets": (np.arange(N_BUCKETS)[:, None] == bucket[None, :]).astype(np.float32),
        "c_is_head": (bh[:, None] % C_HEADS == np.arange(C_HEADS)[None, :]).astype(np.float32),
        "c_is_batch": (bh[:, None] // C_HEADS == i[None, :] // DEC_SEQ).astype(np.float32),
        "c_lam": np.stack([lam_init, 1.0 - lam_init]).astype(np.float32),
    }


class Count:

    def __init__(self, sem, by=1):
        self.sem, self.by, self.n = sem, by, 0

    def on(self, instruction):
        self.n += self.by
        instruction.then_inc(self.sem, self.by)
        return self.n


class Phase:

    def __init__(self, nc, name):
        self.nc, self.name, self.ctx, self.sems = nc, name, ExitStack(), []

    def sb(self, name, shape, dt=F32):
        return self.ctx.enter_context(self.nc.sbuf_tensor(f"{self.name}_{name}", shape, dt))

    def ps(self, name, shape):
        return self.ctx.enter_context(self.nc.psum_tensor(f"{self.name}_{name}", shape, F32))

    def sem(self, name):
        s = self.ctx.enter_context(self.nc.semaphore(f"{self.name}_{name}"))
        self.sems.append(s)
        return s

    def close(self):
        with self.nc.Block() as block:
            @block.gpsimd
            def _(pool):
                numbers = sorted(s.num for s in self.sems)
                assert numbers == list(range(numbers[0], numbers[-1] + 1))
                pool.sem_clear(range(numbers[0], numbers[-1] + 1))
        self.ctx.close()


def rows(dram, offset, pattern):
    return bass.AP(dram.tensor, dram.offset + offset, pattern)


def build(nc, t):
    with ExitStack() as ctx:
        def sb(name, shape, dt=F32):
            return ctx.enter_context(nc.sbuf_tensor(name, shape, dt))

        k = {"x": sb("x", [P, T, D_MODEL]), "ident": sb("ident", [P, P]),
             "ms": sb("ms", [P, T]), "logf": sb("logf", [P, T, C_HEADS]), "cumq": sb("cumq", [P, T, C_HEADS]),
             "lam": sb("lam", [P, 1])}
        setup(nc, t, k)
        with nc.Fori(0, DEPTH) as layer:
            project(nc, t, k, layer)
            attend(nc, t, k, layer)
            mix(nc, t, k, layer)
            feed(nc, t, k, layer)


def setup(nc, t, k):
    ph = Phase(nc, "set")
    heads = A_HEADS + B_HEADS
    table = ph.sb("table", [N_BUCKETS, heads])
    buckets = ph.sb("buckets", [N_BUCKETS, REL])
    row = ph.sb("row", [heads, REL])
    tile_a = ph.sb("tile_a", [P, A_HEADS, 2 * P])
    tile_b = ph.sb("tile_b", [P, B_HEADS, SEQ])
    samp_a = ph.sb("samp_a", [P, A_HEADS, 2 * P])
    samp_b = ph.sb("samp_b", [P, B_HEADS, 3 * P])
    near = ph.sb("near", [P, heads, DEC_SEQ])
    batch = ph.sb("batch", [P, P])
    pr = ph.ps("pr", [heads, 3 * 512])
    loaded, product, copied = ph.sem("loaded"), ph.sem("product"), ph.sem("copied")
    tiles_in, tiles_done, tiles_out = (ph.sem(n) for n in ("tiles_in", "tiles_done", "tiles_out"))
    rows_out = ph.sem("rows_out")
    x_in, squared = ph.sem("x_in"), ph.sem("squared")
    squares = ph.sb("squares", [P, D_MODEL])
    cuts = [(c, min(c + 512, REL)) for c in range(0, REL, 512)]
    with nc.Block() as block:
        @block.sync
        def _(sp):
            sp.dma_start(table[:], t["rel_bias_table"]).then_inc(loaded, 16)
            sp.dma_start(buckets[:], t["c_buckets"]).then_inc(loaded, 16)
            sp.dma_start(batch[:], t["c_batch"]).then_inc(loaded, 16)
            sp.dma_start(k["x"][:, 0:TP, :], t["x_prompt"].rearrange("a (t p) d -> p (a t) d", p=P)).then_inc(x_in, 16)
            sp.dma_start(k["x"][:, TP, :], t["x_sample"].rearrange("b s d -> (b s) d")).then_inc(x_in, 16)
            sp.wait_ge(copied, 1)
            sp.dma_start(t["bias_rows"], row[:].unsqueeze(1).broadcast_to([heads, COPIES, REL])).then_inc(rows_out, 16)
            sp.dma_start(k["ident"][:], t["c_ident"]).then_inc(x_in, 16)
            sp.wait_ge(rows_out, 16)
            skew = REL - 1
            for a in range(0, P, COPIES):
                own = slice(a, a + COPIES)
                sp.dma_start(tile_a[own], rows(t["bias_rows"], REL0 - P - a, [[skew, COPIES], [COPIES * REL, A_HEADS], [1, 2 * P]])).then_inc(tiles_in, 16)
                sp.dma_start(tile_b[own], rows(t["bias_rows"], A_HEADS * COPIES * REL + REL0 - SEQ + P - a,
                                               [[skew, COPIES], [COPIES * REL, B_HEADS], [1, SEQ]])).then_inc(tiles_in, 16)
            for h in range(heads):
                at = h * COPIES * REL + REL0
                out, n = (samp_a[:, h, 0:P], P) if h < A_HEADS else (samp_b[:, h - A_HEADS, 0:PAST], PAST)
                sp.dma_start(out, rows(t["bias_rows"], at - n, [[0, DEC_BATCH], [skew, DEC_SEQ], [1, n]])).then_inc(tiles_in, 16)
                sp.dma_start(near[:, h, :], rows(t["bias_rows"], at, [[0, DEC_BATCH], [skew, DEC_SEQ], [1, DEC_SEQ]])).then_inc(tiles_in, 16)
            sp.wait_ge(tiles_done, 4)
            sp.dma_start(t["bias_a"].rearrange("h p c -> p h c"), tile_a[:]).then_inc(tiles_out, 16)
            sp.dma_start(t["bias_b"].rearrange("h p c -> p h c"), tile_b[:]).then_inc(tiles_out, 16)
            sp.dma_start(t["bias_sa"].rearrange("h p c -> p h c"), samp_a[:]).then_inc(tiles_out, 16)
            sp.dma_start(t["bias_sb"].rearrange("h p c -> p h c"), samp_b[:]).then_inc(tiles_out, 16)
            sp.wait_ge(tiles_out, 64)

        @block.scalar
        def _(act):
            act.wait_ge(x_in, 48)
            for i in range(T):
                if i:
                    act.wait_ge(squared, i)
                act.activation(squares[:], k["x"][:, i, :], ACT.Square, accum_out=k["ms"][:, i:i + 1]).then_inc(squared, 1)

        @block.tensor
        def _(pe):
            pe.wait_ge(loaded, 48)
            for a, b in cuts:
                last = pe.matmul(pr[:, a:b], table[:], buckets[:, a:b], start=True, stop=True)
            last.then_inc(product, 1)

        @block.vector
        def _(dve):
            dve.wait_ge(loaded, 48)
            dve.wait_ge(product, 1)
            dve.tensor_copy(row[:], pr[:, 0:REL]).then_inc(copied, 1)
            dve.wait_ge(tiles_in, 16 * (2 * P // COPIES + 2 * heads))
            dve.memset(tile_a[0:64, :, 192:256], NEG).then_inc(tiles_done, 1)
            dve.memset(tile_a[64:128, :, 0:64], NEG).then_inc(tiles_done, 1)
            dve.memset(tile_b[0:64, :, SEQ - 64:SEQ], NEG).then_inc(tiles_done, 1)
            for h in range(heads):
                out = samp_a[:, h, P:2 * P] if h < A_HEADS else samp_b[:, h - A_HEADS, PAST:PAST + P]
                last = dve.tensor_tensor(out.rearrange("p (b s) -> p b s", b=DEC_BATCH),
                                         batch[:].rearrange("p (b s) -> p b s", b=DEC_BATCH),
                                         near[:, h, :].unsqueeze(1).broadcast_to([P, DEC_BATCH, DEC_SEQ]), ALU.add)
            last.then_inc(tiles_done, 1)
    ph.close()


def split_hi(eng, hi, x):
    return eng.activation(hi, x, ACT.Copy)


def split_lo(eng, lo, x, hi):
    return eng.tensor_tensor(lo, x, hi.bitcast(F32), ALU.subtract)


class NormTranspose:

    def __init__(self, ph, k, gain_row, h_hi, h_lo, xn, h32, pt):
        self.k, self.gain_row, self.h_hi, self.h_lo, self.xn, self.h32, self.pt = k, gain_row, h_hi, h_lo, xn, h32, pt
        self.mean, self.root, self.rstd = (ph.sb(n, [P, T]) for n in ("mean", "root", "rstd"))
        self.shifted, self.rooted, self.scaled = (ph.sem(n) for n in ("h_shifted", "h_rooted", "h_scaled"))
        self.normed, self.turned, self.gained, self.hi_made, self.ready = (
            ph.sem(n) for n in ("h_normed", "h_turned", "h_gained", "h_hi_made", "h_ready"))

    def parts(self, i):
        span = slice(i * P, (i + 1) * P)
        return (self.h32[:, i % 2, :].rearrange("p (k n) -> p k n", k=KD), self.h_hi[:, :, span], self.h_lo[:, :, span])

    def dve_start(self, dve):
        dve.tensor_scalar(self.mean[:], self.k["ms"][:], 1.0 / D_MODEL, EPS, ALU.mult, ALU.add).then_inc(self.shifted, 1)

    def act_start(self, act):
        act.wait_ge(self.shifted, 1)
        act.activation(self.root[:], self.mean[:], ACT.Sqrt).then_inc(self.rooted, 1)

    def dve_scales(self, dve):
        dve.wait_ge(self.rooted, 1)
        dve.reciprocal(self.rstd[:], self.root[:]).then_inc(self.scaled, 1)

    def act_norm(self, act, i):
        act.wait_ge(self.scaled, 1)
        if i >= 2:
            act.wait_ge(self.turned, i - 1)
        act.activation(self.xn[:, i % 2, :], self.k["x"][:, i, :], ACT.Copy, scale=self.rstd[:, i:i + 1]).then_inc(self.normed, 1)

    def pe_turn(self, pe, i):
        pe.wait_ge(self.normed, i + 1)
        if i >= 2:
            pe.wait_ge(self.gained, i - 1)
        for c in range(KD):
            last = pe.transpose(self.pt[:, i % 2, c * P:(c + 1) * P], self.xn[:, i % 2, c * P:(c + 1) * P], self.k["ident"][:])
        last.then_inc(self.turned, 1)

    def dve_gain(self, dve, i):
        dve.wait_ge(self.turned, i + 1)
        if i >= 2:
            dve.wait_ge(self.ready, i - 1)
        dve.tensor_tensor(self.parts(i)[0], self.pt[:, i % 2, :].rearrange("p (k n) -> p k n", k=KD),
                          self.gain_row[:].unsqueeze(2).broadcast_to([P, KD, P]), ALU.mult).then_inc(self.gained, 1)

    def act_hi(self, act, i):
        h, hi, _ = self.parts(i)
        act.wait_ge(self.gained, i + 1)
        split_hi(act, hi, h).then_inc(self.hi_made, 1)

    def dve_lo(self, dve, i):
        h, hi, lo = self.parts(i)
        dve.wait_ge(self.gained, i + 1)
        dve.wait_ge(self.hi_made, i + 1)
        split_lo(dve, lo, h, hi).then_inc(self.ready, 1)


class GateSums:
    LOADS = 11

    def __init__(self, nc, ph, t, k, layer, xn, h32, pt):
        self.nc, self.t, self.k, self.layer = nc, t, k, layer
        BH = DEC_BATCH * C_HEADS
        flat = xn[:].rearrange("p a n -> p (a n)")
        self.upper, self.batch_upper, self.is_batch = flat[:, 0:2 * P], flat[:, 2 * P:3 * P], flat[0:BH, 3 * P:4 * P]
        at = 4 * P
        self.past = flat[:, at:at + 2 * BH].rearrange("p (f n) -> p f n", f=2)
        at += 2 * BH
        self.is_head = flat[0:BH, at:at + C_HEADS]
        at += C_HEADS
        self.lams = flat[:, at:at + 4 * B_DIM].rearrange("p (f n) -> p f n", f=4)
        at += 4 * B_DIM
        self.lam_c = flat[:, at:at + 1]
        rows_ = h32[:].rearrange("p a n -> p (a n)")
        self.prompt_row, self.new_row = rows_[0:C_HEADS, 0:SEQ], rows_[0:C_HEADS, SEQ:SEQ + P]
        self.past_row, self.total = rows_[0:BH, SEQ + P:SEQ + P + PAST], rows_[0:BH, SEQ + P + PAST:SEQ + 2 * P + PAST]
        at = SEQ + 2 * P + PAST
        self.lam_x = rows_[:, at:at + 2 * B_DIM].rearrange("p (f n) -> p f n", f=2)
        at += 2 * B_DIM
        self.lam_s, self.lam_e = rows_[:, at:at + 2], rows_[:, at + 2:at + 4]
        self.prow, self.srow = pt[:, 0, :], pt[:, 1, 0:PAST]
        self.cols, self.nrow = pt[:, 1, 512:512 + T * C_HEADS], pt[:, 1, PAST:PAST + P]
        self.loaded, self.past_sum, self.col_sums, self.totals, self.sums, self.negated, self.stored = (
            ph.sem(n) for n in ("gate_loaded", "past_sum", "col_sums", "totals", "sums", "negated", "cum_stored"))
        self.lam_prod, self.lam_exp, self.lam_diff = (ph.sem(n) for n in ("lam_prod", "lam_exp", "lam_diff"))
        self.BH = BH

    def load(self, sp):
        t, layer = self.t, self.layer
        for dst, name in ((self.upper, "c_upper"), (self.batch_upper, "c_upper_batch"),
                          (self.is_head, "c_is_head"), (self.is_batch, "c_is_batch")):
            sp.dma_start(dst, t[name]).then_inc(self.loaded, 16)
        with self.nc.allow_non_contiguous_dma(reason="six gates per position"):
            for half in range(2):
                sp.dma_start(self.past[:, half, :].rearrange("p (b h) -> p b h", b=DEC_BATCH),
                             t["cache_c_logf"][layer, :, half * P:(half + 1) * P, :].rearrange("b p h -> p b h")).then_inc(self.loaded, 16)
        for n, name in enumerate(("lam_q1", "lam_k1", "lam_q2", "lam_k2")):
            sp.dma_start(self.lams[:, n, :], t[name][layer].unsqueeze(0).broadcast_to([P, B_DIM])).then_inc(self.loaded, 16)
        sp.dma_start(self.lam_c, t["c_lam"][0:1, bass.ds(layer, 1)].broadcast_to([P, 1])).then_inc(self.loaded, 16)

    def store(self, sp):
        sp.wait_ge(self.negated, 3)
        sp.dma_start(self.t["cum_prompt"], self.prompt_row).then_inc(self.stored, 16)
        sp.dma_start(self.t["cum_past"], self.past_row).then_inc(self.stored, 16)
        sp.dma_start(self.t["cum_new"], self.new_row).then_inc(self.stored, 16)

    def dve_lam_products(self, dve):
        dve.wait_ge(self.loaded, 16 * self.LOADS)
        for n in range(2):
            last = dve.tensor_tensor_reduce(self.lam_x[:, n, :], self.lams[:, 2 * n, :], self.lams[:, 2 * n + 1, :],
                                            1.0, 0.0, ALU.mult, ALU.add, self.lam_s[:, n:n + 1])
        last.then_inc(self.lam_prod, 1)

    def act_lam(self, act):
        act.wait_ge(self.lam_prod, 1)
        act.activation(self.lam_e, self.lam_s, ACT.Exp).then_inc(self.lam_exp, 1)

    def dve_lam(self, dve):
        dve.wait_ge(self.lam_exp, 1)
        dve.tensor_tensor(self.lam_s[:, 0:1], self.lam_e[:, 0:1], self.lam_e[:, 1:2], ALU.subtract).then_inc(self.lam_diff, 1)
        dve.wait_ge(self.lam_diff, 1)
        dve.tensor_tensor(self.k["lam"][:], self.lam_s[:, 0:1], self.lam_c, ALU.add).then_inc(self.lam_diff, 1)

    def pe_sums(self, pe):
        logf, upper = self.k["logf"], self.upper
        pe.wait_ge(self.loaded, 16 * self.LOADS)
        pe.matmul(self.srow[0:self.BH, 0:PAST], self.past[:, 0, :], upper[:, 0:PAST], start=True, stop=False)
        pe.matmul(self.srow[0:self.BH, P:PAST], self.past[:, 1, :], upper[:, 0:P], start=False, stop=True).then_inc(self.past_sum, 1)
        for d in range(TP):
            last = pe.matmul(self.cols[:, d * C_HEADS:TP * C_HEADS], upper[:, 0:P] if d == 0 else upper[:, P:2 * P],
                      logf[:, 0:TP - d, :].rearrange("p t h -> p (t h)"), start=(d == 0), stop=(d == TP - 1), skip_group_check=True)
        last.then_inc(self.col_sums, 1)

    def dve_totals(self, dve):
        dve.wait_ge(self.past_sum, 1)
        dve.tensor_scalar(self.past_row, self.srow[0:self.BH, :], -1.0, None, ALU.mult).then_inc(self.negated, 1)
        dve.tensor_scalar(self.total, self.is_batch, self.srow[0:self.BH, PAST - 1:PAST], None, ALU.mult).then_inc(self.totals, 1)
        dve.wait_ge(self.col_sums, 1)
        dve.tensor_copy(self.k["cumq"][:, 0:TP, :], self.cols[:, 0:TP * C_HEADS].rearrange("p (t h) -> p t h", t=TP)).then_inc(self.totals, 1)

    def pe_totals(self, pe):
        new, cols = self.k["logf"][:, TP, :], self.cols[:, TP * C_HEADS:T * C_HEADS]
        pe.wait_ge(self.totals, 2)
        for i in range(TP):
            pe.transpose(self.prow[0:C_HEADS, i * P:(i + 1) * P], self.k["cumq"][:, i, :], self.k["ident"][:])
        pe.matmul(cols, self.batch_upper, new, start=True, stop=False)
        pe.matmul(cols, self.total, self.is_head, start=False, stop=True)
        pe.matmul(self.nrow[0:C_HEADS, :], new, self.batch_upper, start=True, stop=False)
        pe.matmul(self.nrow[0:C_HEADS, :], self.is_head, self.total, start=False, stop=True).then_inc(self.sums, 1)

    def dve_sums(self, dve):
        dve.wait_ge(self.sums, 1)
        dve.tensor_scalar(self.prompt_row, self.prow[0:C_HEADS, :], -1.0, None, ALU.mult).then_inc(self.negated, 1)
        dve.tensor_copy(self.k["cumq"][:, TP, :], self.cols[:, TP * C_HEADS:T * C_HEADS])
        dve.tensor_scalar(self.new_row, self.nrow[0:C_HEADS, :], -1.0, None, ALU.mult).then_inc(self.negated, 1)


def three_passes(pe, out, l_hi, l_lo, r_hi, r_lo, first, final):
    pe.matmul(out, l_hi, r_hi, start=first, stop=False)
    pe.matmul(out, l_hi, r_lo, start=False, stop=False)
    return pe.matmul(out, l_lo, r_hi, start=False, stop=final)


def stores(t, layer, block, i, nat):
    c0, n = IN_BLOCKS[block]
    out = [(t["qkv"][i * P:(i + 1) * P, c0:c0 + n], nat[:, 0:n])]
    prompt, sample = i < TP, i == TP
    for first, count, name, shape in ((KA, 128, "a_k", "h d"), (VA, 128, "a_v", "h d"), (KB, 256, "b_k", "h m d"),
                                      (VB, 256, "b_v", "h d"), (KC, 384, "c_k", "h d"), (VC, 384, "c_v", "h d")):
        if not c0 <= first < c0 + n:
            continue
        src = nat[:, first - c0:first - c0 + count]
        flat = f"({shape})"
        if sample:
            dst = t["s_" + name][layer].rearrange(f"b s {shape} -> b s {flat}")
            if name[0] == "a":
                dst = dst[:, WINDOW - DEC_SEQ:WINDOW, :]
                for b in range(DEC_BATCH):
                    out.append((dst[b], src[b * DEC_SEQ:(b + 1) * DEC_SEQ, :]))
            else:
                out.append((dst.rearrange("b s n -> (b s) n"), src))
        elif name[0] != "a" or i == TP - 1:
            dst = t["p_" + name][layer, 0].rearrange(f"s {shape} -> s {flat}")
            out.append((dst if name[0] == "a" else dst[i * P:(i + 1) * P, :], src))
    return out


def project(nc, t, k, layer):
    ph = Phase(nc, "prj")
    h_hi, h_lo = ph.sb("h_hi", [P, KD, TOK], F32R), ph.sb("h_lo", [P, KD, TOK], F32R)
    gain = ph.sb("gain", [P, KD])
    RAW, RING = 3, 12
    LEAD = 2
    GATES = (GATE_BLOCK + 1) * T + 2
    w_raw = ph.sb("w_raw", [P, RAW, 512])
    w_hi, w_lo = ph.sb("w_hi", [P, RING, 512], F32R), ph.sb("w_lo", [P, RING, 512], F32R)
    qk_gain = ph.sb("qk_gain", [P, 1792])
    bf = ph.sb("bf", [P, C_HEADS])
    sq = ph.sb("sq", [P, 2, 512])
    ms, root, rstd = (ph.sb(n, [P, 2, 8]) for n in ("head_ms", "head_root", "head_rstd"))
    nat = ph.sb("nat", [P, 4, 512])
    z, z_abs, z_exp = (ph.sb(n, [P, T, C_HEADS]) for n in ("z", "z_abs", "z_exp"))
    tT = ph.sb("tT", [P, 4, 512])
    acc = ph.ps("acc", [P, 2, 512])
    turn = ph.ps("turn", [P, 2, 512])
    pt = ph.ps("pt", [P, 2, D_MODEL])
    xn, h32 = ph.sb("xn", [P, 2, D_MODEL]), ph.sb("h32", [P, 2, D_MODEL])
    norm = NormTranspose(ph, k, gain, h_hi, h_lo, xn, h32, pt)
    gates = GateSums(nc, ph, t, k, layer, xn, h32, pt)
    g_in, qg_in, done = ph.sem("g_in"), ph.sem("qg_in"), ph.sem("done")
    w_came = [ph.sem(f"w_came{i}") for i in range(RAW)]
    w_high, w_cut, w_used = (ph.sem(n) for n in ("w_high", "w_cut", "w_used"))
    squared, summed_h, shifted_h, rooted_h, inverse_h, gained, made = (
        ph.sem(n) for n in ("squared", "summed_h", "shifted_h", "rooted_h", "inverse_h", "gained", "made"))
    stored = [ph.sem(f"stored{i}") for i in range(4)]
    scaled_q, f_sum, f_abs, f_exp, f_ln, f_out, f_stored, rolled = (
        ph.sem(n) for n in ("scaled_q", "f_sum", "f_abs", "f_exp", "f_ln", "f_out", "f_stored", "rolled"))
    turned_qk, taken_qk = ph.sem("turned_qk"), ph.sem("taken_qk")
    qk_stored = [ph.sem(f"qk_stored{i}") for i in range(4)]
    work = [(b, i) for b in range(len(IN_BLOCKS)) for i in range(T)]
    normed_units = [u for u, (b, i) in enumerate(work) if NORMED[b]]
    n_stores = [len(stores(t, layer, b, i, nat[:, 0, :])) for b, i in work]
    src = t["w_in"][layer].rearrange("(k p) n -> p k n", p=P)

    def stored_by(u):
        return 16 * sum(n_stores[v] for v in range(u % 4, u + 1, 4))

    def width_of(b):
        return IN_BLOCKS[b][1] + (C_HEADS if b == GATE_BLOCK else 0)

    NB, NW, SLOTS = len(IN_BLOCKS), len(work), len(IN_BLOCKS) * KD
    order = [sum(bool(NORMED[v[0]]) for v in work[:u]) for u in range(NW)]

    def splits_at(u):
        b, i = work[u]
        first = (b + 1) * KD
        return [] if b == NB - 1 else [first + i] if i < RING - KD else [*range(first + RING - KD, first + KD)] if i == T - 1 else []

    with nc.Block() as block:
        @block.sync
        def _(sp):
            def load(s):
                b, c = divmod(s, KD)
                c0, n = IN_BLOCKS[b]
                if s >= RAW:
                    sp.wait_ge(w_cut, s - RAW + 1)
                sp.dma_start(w_raw[:, s % RAW, 0:n], src[:, c, c0:c0 + n]).then_inc(w_came[s % RAW], 16)
                if b == GATE_BLOCK:
                    with nc.allow_non_contiguous_dma(reason="six gates per feature"):
                        sp.dma_start(w_raw[:, s % RAW, n:n + C_HEADS], src[:, c, FZ:N_IN]).then_inc(w_came[s % RAW], 16)

            def store_turned(m):
                b, i = work[normed_units[m]]
                n = NORMED[b][1] * NORMED[b][2] // P
                sp.wait_ge(taken_qk, m + 1)
                dst = t["qkT"][GAIN_AT[b]:GAIN_AT[b] + n * P, i * P:(i + 1) * P].rearrange("(x p) n -> p x n", p=P)
                sp.dma_start(dst, tT[:, m % 4, 0:n * P].rearrange("p (x n) -> p x n", n=P)).then_inc(qk_stored[m % 4], 16)

            for s in range(RAW):
                load(s)
            with nc.allow_non_contiguous_dma(reason="gain vectors"):
                sp.dma_start(gain[:], t["norm_mix"][layer].rearrange("(k p) -> p k", p=P)).then_inc(g_in, 16)
            for s in range(RAW, KD):
                load(s)
            for name, c, heads, width, _ in GAINS:
                sp.dma_start(qk_gain[:, c:c + heads * width].rearrange("p (h d) -> p h d", d=width),
                             t[name][layer].unsqueeze(0).unsqueeze(0).broadcast_to([P, heads, width])).then_inc(qg_in, 16)
            sp.dma_start(bf[:], t["b_forget"][layer].unsqueeze(0).broadcast_to([P, C_HEADS])).then_inc(qg_in, 16)
            for s in range(KD, KD + RAW):
                load(s)
            for kv in "kv":
                sp.dma_start(t[f"s_a_{kv}"][layer, :, 0:WINDOW - DEC_SEQ], t[f"cache_a_{kv}"][layer, :, DEC_SEQ:WINDOW]).then_inc(rolled, 16)
            for u, (b, i) in enumerate(work):
                for s in (splits_at(0) if u == 0 else []) + (splits_at(u + 1) if u + 1 < NW else []):
                    if s + RAW < SLOTS:
                        load(s + RAW)
                if NORMED[b]:
                    sp.wait_ge(made, order[u] + 1)
                else:
                    sp.wait_ge(gained, u + 1)
                for dst, rows_ in stores(t, layer, b, i, nat[:, u % 4, :]):
                    sp.dma_start(dst, rows_).then_inc(stored[u % 4], 16)
                if u >= 1 and NORMED[work[u - 1][0]]:
                    store_turned(order[u - 1])
                if u == T - 1:
                    sp.wait_ge(norm.turned, T)
                    sp.wait_ge(norm.ready, T)
                    gates.load(sp)
                if u == GATES + 2:
                    sp.wait_ge(f_out, 1)
                    sp.dma_start(t["p_c_logf"][layer, 0].rearrange("(t p) h -> p t h", p=P), k["logf"][:, 0:TP, :]).then_inc(f_stored, 16)
                    sp.dma_start(t["s_c_logf"][layer].rearrange("b s h -> (b s) h"), k["logf"][:, TP, :]).then_inc(f_stored, 16)
                if u == GATES + 6:
                    gates.store(sp)
            for m in range(4):
                sp.wait_ge(qk_stored[m], 16 * len(range(m, len(normed_units), 4)))
            for u in range(NW - 4, NW):
                sp.wait_ge(stored[u % 4], stored_by(u))
            sp.wait_ge(rolled, 32)
            sp.wait_ge(f_stored, 32)
            sp.wait_ge(gates.stored, 48)

        @block.tensor
        def _(pe):
            def turn_rows(m):
                b, i = work[normed_units[m]]
                c, heads, width = NORMED[b]
                pe.wait_ge(made, m + 1)
                if m >= 2:
                    pe.wait_ge(taken_qk, m - 1)
                for x in range(heads * width // P):
                    last = pe.transpose(turn[:, m % 2, x * P:(x + 1) * P],
                                        nat[:, normed_units[m] % 4, c + x * P:c + (x + 1) * P], k["ident"][:])
                last.then_inc(turned_qk, 1)

            for i in range(LEAD):
                norm.pe_turn(pe, i)
            for u, (b, i) in enumerate(work):
                if u + LEAD < T:
                    norm.pe_turn(pe, u + LEAD)
                n = width_of(b)
                if b == 0:
                    pe.wait_ge(norm.ready, i + 1)
                if u >= 2:
                    pe.wait_ge(gained, u - 1)
                tok = slice(i * P, (i + 1) * P)
                for c in range(KD):
                    s = b * KD + c
                    if i == 0:
                        pe.wait_ge(w_cut, s + 1)
                    last = three_passes(pe, acc[:, u % 2, 0:n], h_hi[:, c, tok], h_lo[:, c, tok],
                                        w_hi[:, s % RING, 0:n], w_lo[:, s % RING, 0:n], c == 0, c == KD - 1)
                    if i == T - 1 and c < KD - 1:
                        last.then_inc(w_used, 1)
                last.then_inc(done, 1)
                if u >= 2 and NORMED[work[u - 2][0]]:
                    turn_rows(order[u - 2])
                if u == GATES + 2:
                    pe.wait_ge(f_out, 1)
                    gates.pe_sums(pe)
                if u == GATES + 4:
                    gates.pe_totals(pe)

        @block.scalar
        def _(act):
            def raise_weights(s):
                n = width_of(s // KD)
                act.wait_ge(w_came[s % RAW], 16 * sum(2 if v // KD == GATE_BLOCK else 1 for v in range(s % RAW, s + 1, RAW)))
                if s >= RING:
                    b, c = divmod(s - RING, KD)
                    if c < KD - 1:
                        act.wait_ge(w_used, b * (KD - 1) + c + 1)
                    else:
                        act.wait_ge(done, (b + 1) * T)
                split_hi(act, w_hi[:, s % RING, 0:n], w_raw[:, s % RAW, 0:n]).then_inc(w_high, 1)

            def take_turned(m):
                b, i = work[normed_units[m]]
                n = NORMED[b][1] * NORMED[b][2]
                act.wait_ge(turned_qk, m + 1)
                if m >= 4:
                    act.wait_ge(qk_stored[m % 4], 16 * (m // 4))
                act.activation(tT[:, m % 4, 0:n], turn[:, m % 2, 0:n], ACT.Copy).then_inc(taken_qk, 1)

            def unit(u):
                for s in splits_at(u):
                    raise_weights(s)
                b, i = work[u]
                m = order[u]
                if NORMED[b]:
                    c, heads, width = NORMED[b]
                    span = slice(c, c + heads * width)
                    act.wait_ge(done, u + 1)
                    if m >= 2:
                        act.wait_ge(summed_h, m - 1)
                    act.activation(sq[:, m % 2, span], acc[:, u % 2, span], ACT.Square).then_inc(squared, 1)
                if u >= 2 and NORMED[work[u - 2][0]]:
                    take_turned(order[u - 2])
                if NORMED[b]:
                    act.wait_ge(shifted_h, m + 1)
                    if m >= 2:
                        act.wait_ge(inverse_h, m - 1)
                    act.activation(root[:, m % 2, 0:heads], ms[:, m % 2, 0:heads], ACT.Sqrt).then_inc(rooted_h, 1)

            norm.act_start(act)
            for i in range(T + LEAD + 1):
                if i < T:
                    norm.act_norm(act, i)
                for s in range(3 * i, min(3 * i + 3, KD)):
                    raise_weights(s)
                if 1 <= i <= T:
                    norm.act_hi(act, i - 1)
                if i >= LEAD + 1:
                    unit(i - LEAD - 1)
            for u in range(T, NW + 1):
                if u == GATES + 1:
                    act.wait_ge(f_abs, 1)
                    act.activation(z_exp[:], z_abs[:], ACT.Exp, scale=-1.0).then_inc(f_exp, 1)
                    gates.act_lam(act)
                    act.wait_ge(f_exp, 1)
                    act.activation(z_abs[:], z_exp[:], ACT.Ln, bias=1.0).then_inc(f_ln, 1)
                if u < NW:
                    unit(u)

        @block.vector
        def _(dve):
            def cut_weights(s):
                n = width_of(s // KD)
                dve.wait_ge(w_high, s + 1)
                split_lo(dve, w_lo[:, s % RING, 0:n], w_raw[:, s % RAW, 0:n], w_hi[:, s % RING, 0:n]).then_inc(w_cut, 1)

            def scale_gains():
                dve.wait_ge(qg_in, 112)
                for name, c, heads, width, scale in GAINS:
                    if scale:
                        span = qk_gain[:, c:c + heads * width]
                        last = dve.tensor_scalar(span, span, scale, None, ALU.mult)
                last.then_inc(scaled_q, 1)
                dve.wait_ge(scaled_q, 1)

            def read_out(u):
                for s in splits_at(u):
                    cut_weights(s)
                b, i = work[u]
                m = order[u]
                n = IN_BLOCKS[b][1]
                dve.wait_ge(done, u + 1)
                if u >= 4:
                    dve.wait_ge(stored[u % 4], stored_by(u - 4))
                    if NORMED[work[u - 4][0]]:
                        dve.wait_ge(turned_qk, normed_units.index(u - 4) + 1)
                if not NORMED[b]:
                    dve.tensor_copy(nat[:, u % 4, 0:n], acc[:, u % 2, 0:n]).then_inc(gained, 1)
                    return
                c, heads, width = NORMED[b]
                e = c + heads * width
                dve.wait_ge(squared, m + 1)
                if b == GATE_BLOCK:
                    dve.tensor_tensor(z[:, i, :], acc[:, u % 2, n:n + C_HEADS], bf[:], ALU.add).then_inc(f_sum, 1)
                for a_, e_ in ((0, c), (e, n)):
                    if a_ < e_:
                        dve.tensor_copy(nat[:, u % 4, a_:e_], acc[:, u % 2, a_:e_])
                g = GAIN_AT[b]
                dve.tensor_tensor(nat[:, u % 4, c:e], acc[:, u % 2, c:e], qk_gain[:, g:g + heads * width], ALU.mult).then_inc(gained, 1)
                dve.tensor_reduce(ms[:, m % 2, 0:heads], sq[:, m % 2, c:e].rearrange("p (h d) -> p h d", d=width), AX.X, ALU.add).then_inc(summed_h, 1)
                dve.wait_ge(summed_h, m + 1)
                dve.tensor_scalar(ms[:, m % 2, 0:heads], ms[:, m % 2, 0:heads], 1.0 / width, EPS, ALU.mult, ALU.add).then_inc(shifted_h, 1)

            def finish_rows(u):
                b, i = work[u]
                m = order[u]
                dve.wait_ge(gained, u + 1)
                if not NORMED[b]:
                    return
                c, heads, width = NORMED[b]
                dve.wait_ge(rooted_h, m + 1)
                dve.reciprocal(rstd[:, m % 2, 0:heads], root[:, m % 2, 0:heads]).then_inc(inverse_h, 1)
                dve.wait_ge(inverse_h, m + 1)
                view = nat[:, u % 4, c:c + heads * width].rearrange("p (h d) -> p h d", d=width)
                dve.tensor_tensor(view, view, rstd[:, m % 2, 0:heads].unsqueeze(2).broadcast_to([P, heads, width]), ALU.mult).then_inc(made, 1)

            norm.dve_start(dve)
            norm.dve_scales(dve)
            dve.wait_ge(g_in, 16)
            for i in range(T + LEAD + 1):
                if i < T:
                    norm.dve_gain(dve, i)
                for s in range(3 * i, min(3 * i + 3, KD)):
                    cut_weights(s)
                if 1 <= i <= T:
                    norm.dve_lo(dve, i - 1)
                if i == LEAD + 1:
                    scale_gains()
                if i >= LEAD + 1:
                    read_out(i - LEAD - 1)
                if i >= LEAD + 2:
                    finish_rows(i - LEAD - 2)
            for u in range(T, NW + 1):
                if u == GATES + 3:
                    gates.dve_totals(dve)
                if u < NW:
                    read_out(u)
                finish_rows(u - 1)
                if u == GATES:
                    dve.wait_ge(f_sum, T)
                    dve.scalar_tensor_tensor(out=z_abs[:], in0=z[:], scalar=-1.0, in1=z[:], op0=ALU.mult, op1=ALU.max).then_inc(f_abs, 1)
                    gates.dve_lam_products(dve)
                if u == GATES + 1:
                    dve.wait_ge(f_ln, 1)
                    dve.scalar_tensor_tensor(out=k["logf"][:], in0=z[:], scalar=0.0, in1=z_abs[:], op0=ALU.min, op1=ALU.subtract).then_inc(f_out, 1)
                    gates.dve_lam(dve)
                if u == GATES + 5:
                    gates.dve_sums(dve)
    ph.close()


class Group:

    def __init__(self, index, kind, j):
        self.index, self.kind, self.j = index, kind, j
        self.D = B_DIM if kind == "B" else HEAD
        self.maps = P // self.D
        self.per_head = self.maps // 2
        self.packed = P // self.D
        self.nb = DEC_BATCH // self.packed
        self.halves = 1 if kind == "A" else PAST // P
        self.n_past = self.halves * P
        self.n_samp = self.n_past + P
        self.width = 2 * P if kind == "A" else SEQ
        self.tile = {"A": 0, "B": 3, "C": 5}[kind] + j
        self.q_row = {"A": lambda m: (j + 3 * m) * HEAD, "B": lambda m: 512 + j * P + m * B_DIM,
                      "C": lambda m: 1024 + j * P + m * HEAD}[kind]
        self.k_row = {"A": 384, "B": 768 + j * P, "C": 1408 + j * P}[kind]
        self.v_col = {"A": VA, "B": VB + j * P, "C": VC + j * P}[kind]
        self.past_chunks = self.maps * self.nb * self.halves // 4

    def keys(self, i):
        return list(range(max(i - 1, 0) if self.kind == "A" else 0, i + 1))

    def n_cols(self, i):
        return self.n_samp if i == TP else P * len(self.keys(i))

    def n_chunks(self, i):
        return -(-self.n_cols(i) // 512)


def attend(nc, t, k, layer):
    ph = Phase(nc, "att")
    groups = [Group(n, kind, j) for n, (kind, j) in enumerate(
        [("A", 0), ("A", 1), ("A", 2), ("B", 0), ("B", 1), ("C", 0), ("C", 1), ("C", 2)])]
    NG, UG = len(groups), 2 * T
    qT = ph.sb("qT", [P, 2, 4, TOK])
    kT, vn, mixn = ph.sb("kT", [P, 2, TOK]), ph.sb("vn", [P, 2, T, P]), ph.sb("mixn", [P, 2, T, P])
    kp, vp, kpT = ph.sb("kp", [P, 2 * DEC_BATCH, P]), ph.sb("vp", [P, 2, DEC_BATCH, P]), ph.sb("kpT", [P, 2 * DEC_BATCH * P])
    qpast = ph.sb("qpast", [P, 8, P])
    add_p, add_s = ph.sb("add_p", [P, 2, 2, SEQ]), ph.sb("add_s", [P, 2, 2, 3 * P])
    s, p, pT = ph.sb("s", [P, 2, SEQ]), ph.sb("p", [P, 3, 2, SEQ]), ph.sb("pT", [P, 2, SEQ])
    oT, mixTb = ph.sb("oT", [HEAD, P]), ph.sb("mixTb", [P, TOK])
    units = [(g, h, i) for g in groups for h in range(2) for i in range(T)]
    NU = len(units)
    jobs_to = [0]
    for g, h, i in units:
        jobs_to.append(jobs_to[-1] + g.per_head)
    NJ = jobs_to[-1]
    mx, bias, total, inv, esink = (ph.sb(n, [P, NJ]) for n in ("mx", "bias", "total", "inv", "esink"))
    coef = ph.sb("coef", [P, NU])
    sink = ph.sb("sink", [P, A_HEADS])
    mask_f, mask_s = ph.sb("mask_f", [P, P]), ph.sb("mask_s", [P, P])
    mask_b, ident_b = ph.sb("mask_b", [P, P], BF16), ph.sb("ident_b", [P, P], BF16)
    neg_lam, keep, subln = ph.sb("neg_lam", [P, 1]), ph.sb("keep", [P, 1]), ph.sb("subln", [P, HEAD])
    sub_sq = ph.sb("sub_sq", [P, T, P])
    sub_ms, sub_root = ph.sb("sub_ms", [P, UG]), ph.sb("sub_root", [P, UG])
    S, TR, O = ph.ps("S", [P, 2, SEQ]), ph.ps("TR", [P, 2, 512]), ph.ps("O", [P, 2, 512])

    qk_in, v_in, q_zeroed = ([ph.sem(f"{n}{i}") for i in range(2)] for n in ("qk_in", "v_in", "q_zeroed"))
    kp_in, vp_in, qpast_zeroed, qpast_in, const_in = (
        ph.sem(n) for n in ("kp_in", "vp_in", "qpast_zeroed", "qpast_in", "const_in"))
    prepared, masked, scored, biased, bias_ready, exped, sink_ready, inv_ready, weighed, normed = (
        ph.sem(n) for n in ("prepared", "masked", "scored", "biased", "bias_ready", "exped", "sink_ready", "inv_ready", "weighed", "normed"))
    turned, evacuated, multiplied, oT_ready, turned_back, taken_out = (
        ph.sem(n) for n in ("turned", "evacuated", "multiplied", "oT_ready", "turned_back", "taken_out"))
    steps, sub_squared, sub_mean, sub_rooted, sub_done, mix_stored = (
        ph.sem(n) for n in ("steps", "sub_squared", "sub_mean", "sub_rooted", "sub_done", "mix_stored"))

    extra = {}
    for g in groups:
        for c in range(g.past_chunks):
            extra.setdefault(g.index * UG + 2 + c, []).append(("past", g, c))
        for c in range(3):
            extra.setdefault((g.index + 1) * UG + 7 + c, []).append(("mix", g, c))
    N_ITER = NU + 11
    order = []
    for u in range(N_ITER):
        if 2 <= u <= NU + 1:
            g, h, i = units[u - 2]
            order += [("p", u - 2, c) for c in range(g.n_chunks(i))]
        order += [(what, g.index, c) for what, g, c in extra.get(u, [])]
    place = {key: n for n, key in enumerate(order)}
    samples_to = [sum(x[2] == TP for x in units[:u]) for u in range(NU + 1)]
    weighed_to = [sum(x[0].kind == "B" for x in units[:u]) for u in range(NU + 1)]
    sinks_to = [sum(x[0].kind == "A" for x in units[:u]) for u in range(NU + 1)]
    n_qk = {"A": 2 + 1 + 4, "B": 4 + 1 + 4, "C": 2 + 1 + 6}

    def fresh(g):
        return g.index < 2 or "B" in (g.kind, groups[g.index - 2].kind)

    def to(g, parity, count):
        return 16 * sum(count(x) for x in groups[:g.index + 1] if parity is None or x.index % 2 == parity)

    def qk_to(g):
        return to(g, g.index % 2, lambda x: n_qk[x.kind])

    def chunk_of_mix(c):
        return c * 4, min(c * 4 + 4, T)

    with nc.Block() as block:
        @block.sync
        def _(sp):
            qkv = t["qkv"].rearrange("(t p) n -> p t n", p=P)

            def load_front(g):
                b, j, kind, sem = g.index % 2, g.j, g.kind, qk_in[g.index % 2]
                if g.index >= 2:
                    sp.wait_ge(scored, jobs_to[(g.index - 1) * UG])
                    sp.wait_ge(biased, jobs_to[(g.index - 1) * UG])
                sp.dma_start(kT[:, b, :], t["qkT"][g.k_row:g.k_row + P, :]).then_inc(sem, 16)
                for h in range(2):
                    if kind == "A":
                        sp.dma_start(add_p[:, b, h, 0:g.width], t["bias_a"][j + 3 * h]).then_inc(sem, 16)
                        sp.dma_start(add_s[:, b, h, 0:g.n_samp], t["bias_sa"][j + 3 * h]).then_inc(sem, 16)
                    elif kind == "B":
                        sp.dma_start(add_p[:, b, h, :], t["bias_b"][2 * j + h]).then_inc(sem, 16)
                        sp.dma_start(add_s[:, b, h, :], t["bias_sb"][2 * j + h]).then_inc(sem, 16)
                    else:
                        head = slice(2 * j + h, 2 * j + h + 1)
                        sp.dma_start(add_p[:, b, h, :], t["cum_prompt"][head, :].broadcast_to([P, SEQ])).then_inc(sem, 16)
                        past = t["cum_past"].rearrange("(b h) n -> b h n", h=C_HEADS)[:, head, :]
                        sp.dma_start(add_s[:, b, h, 0:PAST], past.broadcast_to([DEC_BATCH, DEC_SEQ, PAST])).then_inc(sem, 16)
                        sp.dma_start(add_s[:, b, h, PAST:g.n_samp], t["cum_new"][head, :].broadcast_to([P, P])).then_inc(sem, 16)
                sp.wait_ge(q_zeroed[b], sum(x.index % 2 == b and fresh(x) for x in groups[:g.index + 1]))
                for m in range(g.maps):
                    sp.dma_start(qT[m * g.D:(m + 1) * g.D, b, m, :], t["qkT"][g.q_row(m):g.q_row(m) + g.D, :]).then_inc(sem, 16)
                if g.index >= 2:
                    sp.wait_ge(multiplied, (g.index - 1) * UG)
                sp.dma_start(vn[:, b, :, :], qkv[:, :, g.v_col:g.v_col + P]).then_inc(v_in[b], 16)

            def load_past(g):
                low, D = g.kind.lower(), g.D
                src = t[f"cache_{low}_k"][layer]
                src = src.rearrange("b p h m d -> b p (h m) d") if g.kind == "B" else src
                if g.index:
                    sp.wait_ge(turned, place["past", g.index - 1, groups[g.index - 1].past_chunks - 1] + 1)
                for f in range(g.halves):
                    for m in range(g.maps):
                        head = m if g.kind == "A" else g.j * g.maps + m
                        at = (f * g.maps + m) * DEC_BATCH * D
                        sp.dma_start(kp[:].rearrange("p x n -> p (x n)")[:, at:at + DEC_BATCH * D].rearrange("p (b d) -> p b d", d=D),
                                     src[:, f * P:(f + 1) * P, head, :].rearrange("b p d -> p b d")).then_inc(kp_in, 16)
                if g.index:
                    sp.wait_ge(multiplied, g.index * UG)
                src = t[f"cache_{low}_v"][layer].rearrange("b p h d -> p b (h d)")
                for f in range(g.halves):
                    cols = slice(0, P) if g.kind == "A" else slice(g.j * P, (g.j + 1) * P)
                    sp.dma_start(vp[:, f, :, :], src[f * P:(f + 1) * P, :, cols]).then_inc(vp_in, 16)
                sp.wait_ge(qpast_zeroed, g.index + 1)
                with nc.allow_non_contiguous_dma(reason="16 tokens per batch"):
                    for m in range(g.maps):
                        for r in range(g.packed):
                            dst = qpast[r * D:(r + 1) * D, m * g.nb, r * DEC_SEQ:(r + 1) * DEC_SEQ]
                            dst = bass.AP(dst.tensor, dst.offset, [list(dst.ap[0]), [P + g.packed * DEC_SEQ, g.nb], [1, DEC_SEQ]])
                            row = t["qkT"][g.q_row(m):g.q_row(m) + D, SEQ:TOK]
                            sp.dma_start(dst, row.rearrange("d (c r s) -> d c r s", r=g.packed, s=DEC_SEQ)[:, :, r, :]).then_inc(qpast_in, 16)

            load_front(groups[0])
            sp.dma_start(mask_f[:], t["c_causal"]).then_inc(const_in, 16)
            sp.dma_start(mask_s[:], t["c_batch_causal"]).then_inc(const_in, 16)
            sp.dma_start(sink[:], t["sinks_a"][layer].unsqueeze(0).broadcast_to([P, A_HEADS])).then_inc(const_in, 16)
            sp.dma_start(subln[:], t["subln_b"][layer].unsqueeze(0).broadcast_to([P, HEAD])).then_inc(const_in, 16)
            sp.dma_start(keep[:], t["c_lam"][1:2, bass.ds(layer, 1)].broadcast_to([P, 1])).then_inc(const_in, 16)
            load_past(groups[0])
            load_front(groups[1])
            for g in groups:
                if g.index + 1 < NG:
                    load_past(groups[g.index + 1])
                if g.index + 2 < NG:
                    load_front(groups[g.index + 2])
                sp.wait_ge(evacuated, place["mix", g.index, 2] + 1)
                sp.dma_start(t["mixT"][g.tile * P:(g.tile + 1) * P, :], mixTb[:]).then_inc(mix_stored, 16)
            sp.wait_ge(mix_stored, 16 * NG)

        @block.gpsimd
        def _(pool):
            for b in range(2):
                pool.memset(qT[:, b, 0:2, :], 0.0).then_inc(q_zeroed[b], 1)
            for g in groups:
                if g.index:
                    pool.wait_ge(scored, jobs_to[g.index * UG])
                pool.memset(qpast[:], 0.0).then_inc(qpast_zeroed, 1)
                if 1 <= g.index < NG - 1 and fresh(groups[g.index + 1]):
                    pool.memset(qT[:, (g.index + 1) % 2, :, :], 0.0).then_inc(q_zeroed[(g.index + 1) % 2], 1)

        @block.tensor
        def _(pe):
            def score(u):
                g, h, i = units[u]
                b = g.index % 2
                if u % UG == 0:
                    pe.wait_ge(qk_in[b], qk_to(g))
                if i == TP:
                    pe.wait_ge(qpast_in, to(g, None, lambda x: x.maps * x.packed))
                    pe.wait_ge(evacuated, place["past", g.index, g.past_chunks - 1] + 1)
                if g.kind == "C" and u % UG == 0:
                    pe.wait_ge(prepared, 1)
                for r in range(g.per_head):
                    job = jobs_to[u] + r
                    m = h * g.per_head + r
                    if job >= 2:
                        pe.wait_ge(biased, job - 1)
                    out, q = S[:, job % 2, :], qT[:, b, m, i * P:(i + 1) * P]
                    if i < TP:
                        k0, n = g.keys(i)[0] * P, g.n_cols(i)
                        for c in range(0, n, 512):
                            w = min(512, n - c)
                            last = pe.matmul(out[:, c:c + w], q, kT[:, b, k0 + c:k0 + c + w], start=True,
                                             stop=not (g.kind == "C" and c + w == n))
                        if g.kind == "C":
                            last = pe.matmul(out[:, n - P:n], ident_b[:], mask_b[:], start=False, stop=True)
                    else:
                        for c in range(g.nb):
                            x = m * g.nb + c
                            pe.matmul(out[:, 0:g.n_past], qpast[:, x, :], kpT[:, x * g.n_past:(x + 1) * g.n_past],
                                      start=(c == 0), stop=(c == g.nb - 1))
                        last = pe.matmul(out[:, g.n_past:g.n_samp], q, kT[:, b, SEQ:TOK], start=True, stop=True)
                    last.then_inc(scored, 1)

            def turn(u):
                g, h, i = units[u]
                if i == TP:
                    pe.wait_ge(normed, samples_to[u + 1])
                elif g.kind == "B":
                    pe.wait_ge(weighed, weighed_to[u + 1])
                else:
                    pe.wait_ge(exped, jobs_to[u + 1])
                for c in range(g.n_chunks(i)):
                    n = place["p", u, c]
                    if n >= 2:
                        pe.wait_ge(evacuated, n - 1)
                    for x in range(4 * c, min(4 * c + 4, g.n_cols(i) // P)):
                        last = pe.transpose(TR[:, n % 2, x % 4 * P:(x % 4 + 1) * P], p[:, u % 3, 0, x * P:(x + 1) * P], k["ident"][:])
                    last.then_inc(turned, 1)

            def turn_extra(what, g, c):
                n = place[what, g.index, c]
                if n >= 2:
                    pe.wait_ge(evacuated, n - 1)
                if what == "past":
                    if c == 0:
                        pe.wait_ge(kp_in, to(g, None, lambda x: x.halves * x.maps))
                    for x in range(4 * c, 4 * c + 4):
                        mb, f = divmod(x, g.halves)
                        m, nb = divmod(mb, g.nb)
                        at = ((f * g.maps + m) * g.nb + nb)
                        last = pe.transpose(TR[:, n % 2, x % 4 * P:(x % 4 + 1) * P], kp[:, at, :], k["ident"][:])
                else:
                    if c == 0 and g.kind == "B":
                        pe.wait_ge(sub_done, g.j + 1)
                    elif c == 0:
                        pe.wait_ge(taken_out, (g.index + 1) * UG)
                    a, e = chunk_of_mix(c)
                    for x in range(a, e):
                        last = pe.transpose(TR[:, n % 2, (x - a) * P:(x - a + 1) * P], mixn[:, g.index % 2, x, :], k["ident"][:])
                last.then_inc(turned, 1)

            def values(u):
                g, h, i = units[u]
                b = g.index % 2
                if u % UG == 0:
                    pe.wait_ge(v_in[b], to(g, b, lambda x: 1))
                pe.wait_ge(evacuated, place["p", u, g.n_chunks(i) - 1] + 1)
                if u >= 2:
                    pe.wait_ge(taken_out, u - 1)
                v = slice(h * HEAD, (h + 1) * HEAD)
                if i < TP:
                    ks = g.keys(i)
                    for x, kt in enumerate(ks):
                        last = pe.matmul(O[:, u % 2, 0:HEAD], pT[:, u % 2, x * P:(x + 1) * P], vn[:, b, kt, v],
                                         start=(x == 0), stop=(x == len(ks) - 1))
                else:
                    pe.wait_ge(vp_in, to(g, None, lambda x: x.halves))
                    pe.matmul(O[0:HEAD, u % 2, 0:P], vn[:, b, TP, v], pT[:, u % 2, g.n_past:g.n_samp], start=True, stop=False,
                              skip_group_check=True)
                    for d in range(DEC_BATCH):
                        for f in range(g.halves):
                            own = slice(d * DEC_SEQ, (d + 1) * DEC_SEQ)
                            last = pe.matmul(O[0:HEAD, u % 2, own], vp[:, f, d, v], pT[:, u % 2, f * P + d * DEC_SEQ:f * P + (d + 1) * DEC_SEQ],
                                             start=False, stop=(d == DEC_BATCH - 1 and f == g.halves - 1), skip_group_check=True)
                last.then_inc(multiplied, 1)

            def turn_back(u):
                if units[u][2] == TP:
                    pe.wait_ge(oT_ready, samples_to[u + 1])
                    pe.transpose(O[:, u % 2, P:P + HEAD], oT[:], k["ident"][0:HEAD, 0:HEAD]).then_inc(turned_back, 1)

            for u in range(N_ITER):
                if u < NU:
                    score(u)
                if 2 <= u <= NU + 1:
                    turn(u - 2)
                for what, g, c in extra.get(u, []):
                    turn_extra(what, g, c)
                if 3 <= u <= NU + 2:
                    values(u - 3)
                if 4 <= u <= NU + 3:
                    turn_back(u - 4)

        @block.scalar
        def _(act):
            def exps(u):
                g, h, i = units[u]
                n = g.n_cols(i)
                if u >= 3:
                    g3, _, i3 = units[u - 3]
                    act.wait_ge(turned, place["p", u - 3, g3.n_chunks(i3) - 1] + 1)
                for r in range(g.per_head):
                    job = jobs_to[u] + r
                    act.wait_ge(bias_ready, job + 1)
                    act.activation(p[:, u % 3, r, 0:n], s[:, job % 2, 0:n], ACT.Exp, bias=bias[:, job:job + 1],
                                   accum_out=total[:, job:job + 1]).then_inc(exped, 1)
                    if g.kind == "A":
                        head = g.j + 3 * h
                        act.activation(esink[:, job:job + 1], sink[:, head:head + 1], ACT.Exp, bias=bias[:, job:job + 1]).then_inc(sink_ready, 1)

            def evacuate(u):
                g, h, i = units[u]
                for c in range(g.n_chunks(i)):
                    n = place["p", u, c]
                    act.wait_ge(turned, n + 1)
                    if u >= 2 and c == 0:
                        act.wait_ge(multiplied, u - 1)
                    w = min(512, g.n_cols(i) - c * 512)
                    act.activation(pT[:, u % 2, c * 512:c * 512 + w], TR[:, n % 2, 0:w], ACT.Copy).then_inc(evacuated, 1)

            def evacuate_extra(what, g, c):
                n = place[what, g.index, c]
                act.wait_ge(turned, n + 1)
                if what == "past":
                    if c == 0 and g.index:
                        act.wait_ge(scored, jobs_to[g.index * UG])
                    act.activation(kpT[:, c * 512:(c + 1) * 512], TR[:, n % 2, :], ACT.Copy).then_inc(evacuated, 1)
                else:
                    if c == 0 and g.index:
                        act.wait_ge(mix_stored, 16 * g.index)
                    a, e = chunk_of_mix(c)
                    act.activation(mixTb[:, a * P:e * P], TR[:, n % 2, 0:(e - a) * P], ACT.Copy).then_inc(evacuated, 1)

            def take_oT(u):
                if units[u][2] == TP:
                    act.wait_ge(multiplied, u + 1)
                    if samples_to[u]:
                        act.wait_ge(turned_back, samples_to[u])
                    act.activation(oT[:], O[0:HEAD, u % 2, 0:P], ACT.Copy).then_inc(oT_ready, 1)

            def sub_root_of(g):
                act.wait_ge(sub_mean, g.j + 1)
                act.activation(sub_root[:], sub_ms[:], ACT.Sqrt).then_inc(sub_rooted, 1)

            for u in range(N_ITER):
                if 2 <= u <= NU + 1:
                    evacuate(u - 2)
                for what, g, c in extra.get(u, []):
                    evacuate_extra(what, g, c)
                if u < NU:
                    exps(u)
                if 3 <= u <= NU + 2:
                    take_oT(u - 3)
                for g in groups:
                    if g.kind == "B" and u == (g.index + 1) * UG + 5:
                        sub_root_of(g)

        @block.vector
        def _(dve):
            chain = Count(steps)

            def then(ins):
                dve.wait_ge(steps, chain.on(ins))

            dve.wait_ge(const_in, 16 * 5)
            then(dve.tensor_scalar(neg_lam[:], k["lam"][:], -1.0, None, ALU.mult))
            then(dve.tensor_scalar(subln[:], subln[:], keep[:, 0:1], None, ALU.mult))
            dve.tensor_copy(mask_b[:], mask_f[:])
            dve.tensor_copy(ident_b[:], k["ident"][:]).then_inc(prepared, 1)

            def front(u):
                g, h, i = units[u]
                b, n = g.index % 2, g.n_cols(i)
                if u % UG == 0:
                    dve.wait_ge(qk_in[b], qk_to(g))
                    if g.kind == "C":
                        for x in range(2):
                            last = dve.tensor_tensor(add_s[:, b, x, PAST:g.n_samp], add_s[:, b, x, PAST:g.n_samp], mask_s[:], ALU.add)
                        then(last)
                for r in range(g.per_head):
                    job = jobs_to[u] + r
                    dve.wait_ge(scored, job + 1)
                    if job >= 2:
                        dve.wait_ge(exped, job - 1)
                    extra_row = (add_s[:, b, h, 0:n] if i == TP else add_p[:, b, h, 0:n] if g.kind == "C"
                                 else add_p[:, b, h, g.width - n:g.width])
                    one = slice(job, job + 1)
                    dve.tensor_tensor_reduce(s[:, job % 2, 0:n], S[:, job % 2, 0:n], extra_row, 1.0, -3e38, ALU.add, ALU.max, mx[:, one]).then_inc(biased, 1)
                    dve.wait_ge(biased, job + 1)
                    if g.kind == "A":
                        head = g.j + 3 * h
                        dve.tensor_scalar(bias[:, one], mx[:, one], sink[:, head:head + 1], -1.0, ALU.max, ALU.mult).then_inc(bias_ready, 1)
                    elif g.kind == "B":
                        dve.tensor_scalar(bias[:, one], mx[:, one], -1.0, None, ALU.mult).then_inc(bias_ready, 1)
                    else:
                        own = k["cumq"][:, i, 2 * g.j + h:2 * g.j + h + 1]
                        then(dve.tensor_tensor(mx[:, one], mx[:, one], own, ALU.add))
                        dve.tensor_tensor(bias[:, one], own, mx[:, one], ALU.subtract).then_inc(bias_ready, 1)

            def back(u):
                g, h, i = units[u]
                n = g.n_cols(i)
                a, e = jobs_to[u], jobs_to[u + 1]
                dve.wait_ge(exped, e)
                if g.kind == "A":
                    dve.wait_ge(sink_ready, sinks_to[u + 1])
                    then(dve.tensor_tensor(total[:, a:e], total[:, a:e], esink[:, a:e], ALU.add))
                dve.reciprocal(inv[:, a:e], total[:, a:e]).then_inc(inv_ready, 1)
                if g.kind != "B" and i < TP:
                    return
                dve.wait_ge(inv_ready, u + 1)
                if g.kind == "B":
                    then(dve.scalar_tensor_tensor(out=coef[:, u:u + 1], in0=total[:, a:a + 1], scalar=inv[:, a + 1:a + 2],
                                                  in1=neg_lam[:], op0=ALU.mult, op1=ALU.mult))
                    dve.scalar_tensor_tensor(out=p[:, u % 3, 0, 0:n], in0=p[:, u % 3, 1, 0:n], scalar=coef[:, u:u + 1],
                                             in1=p[:, u % 3, 0, 0:n], op0=ALU.mult, op1=ALU.add).then_inc(weighed, 1)
                    if i == TP:
                        dve.wait_ge(weighed, weighed_to[u + 1])
                if i == TP:
                    dve.tensor_scalar(p[:, u % 3, 0, 0:n], p[:, u % 3, 0, 0:n], inv[:, a:a + 1], None, ALU.mult).then_inc(normed, 1)

            def take_out(u, late):
                g, h, i = units[u]
                if (i == TP) != late:
                    return
                if h == 0 and i == 0 and g.index >= 2:
                    dve.wait_ge(turned, place["mix", g.index - 2, 2] + 1)
                dst = mixn[:, g.index % 2, i, h * HEAD:(h + 1) * HEAD]
                if late:
                    dve.wait_ge(turned_back, samples_to[u + 1])
                    dve.tensor_copy(dst, O[:, u % 2, P:P + HEAD]).then_inc(taken_out, 1)
                else:
                    dve.wait_ge(multiplied, u + 1)
                    dve.wait_ge(inv_ready, u + 1)
                    a = jobs_to[u]
                    dve.tensor_scalar(dst, O[:, u % 2, 0:HEAD], inv[:, a:a + 1], None, ALU.mult).then_inc(taken_out, 1)

            def sub_norm(g):
                rows_ = mixn[:, g.index % 2, :, :].rearrange("p t (h d) -> p (t h) d", d=HEAD)
                sq = sub_sq[:].rearrange("p t (h d) -> p (t h) d", d=HEAD)
                dve.wait_ge(taken_out, (g.index + 1) * UG)
                then(dve.tensor_tensor(sq, rows_, rows_, ALU.mult))
                then(dve.tensor_reduce(sub_ms[:], sq, AX.X, ALU.add))
                dve.tensor_scalar(sub_ms[:], sub_ms[:], 1.0 / HEAD, EPS, ALU.mult, ALU.add).then_inc(sub_mean, 1)

            def sub_scale(g):
                rows_ = mixn[:, g.index % 2, :, :].rearrange("p t (h d) -> p (t h) d", d=HEAD)
                dve.wait_ge(sub_rooted, g.j + 1)
                then(dve.reciprocal(sub_ms[:], sub_root[:]))
                then(dve.tensor_tensor(rows_, rows_, sub_ms[:].unsqueeze(2).broadcast_to([P, UG, HEAD]), ALU.mult))
                dve.tensor_tensor(rows_, rows_, subln[:].unsqueeze(1).broadcast_to([P, UG, HEAD]), ALU.mult).then_inc(sub_done, 1)

            for u in range(N_ITER):
                if u < NU:
                    front(u)
                if 1 <= u <= NU:
                    back(u - 1)
                if 4 <= u <= NU + 3:
                    take_out(u - 4, True)
                if 3 <= u <= NU + 2:
                    take_out(u - 3, False)
                for g in groups:
                    if g.kind == "B" and u == (g.index + 1) * UG + 4:
                        sub_norm(g)
                    if g.kind == "B" and u == (g.index + 1) * UG + 6:
                        sub_scale(g)
    ph.close()

def mix(nc, t, k, layer):
    ph = Phase(nc, "mix")
    BANKS = 8
    w_raw, m_raw = ph.sb("w_raw", [P, 2, D_MODEL]), ph.sb("m_raw", [P, 2, TOK])
    w_hi, w_lo = ph.sb("w_hi", [P, KD, D_MODEL], F32R), ph.sb("w_lo", [P, KD, D_MODEL], F32R)
    m_hi, m_lo = ph.sb("m_hi", [P, KD, TOK], F32R), ph.sb("m_lo", [P, KD, TOK], F32R)
    squares = ph.sb("squares", [P, D_MODEL])
    acc = ph.ps("acc", [P, BANKS, 512])
    came = [ph.sem(f"came{i}") for i in range(2)]
    high, cut, done, added, squared = (ph.sem(n) for n in ("high", "cut", "done", "added", "squared"))
    src = t["w_out"][layer]
    pieces = [3 if g < 3 else 2 for g in range(KD)]

    def came_by(g):
        return 16 * sum(pieces[g % 2:g + 1:2])

    def product(pe, u, g):
        i, c = divmod(u, 2)
        tok, col = slice(i * P, (i + 1) * P), slice(c * 512, (c + 1) * 512)
        return three_passes(pe, acc[:, u % BANKS, :], m_hi[:, g, tok], m_lo[:, g, tok],
                            w_hi[:, g, col], w_lo[:, g, col], g == 0, g == KD - 1)

    with nc.Block() as block:
        @block.sync
        def _(sp):
            for g in range(KD):
                if g >= 2:
                    sp.wait_ge(cut, 2 * (g - 1))
                sp.dma_start(m_raw[:, g % 2, :], t["mixT"][g * P:(g + 1) * P, :]).then_inc(came[g % 2], 16)
                if g < 3:
                    for h in range(2):
                        r = (g + 3 * h) * HEAD
                        sp.dma_start(w_raw[h * HEAD:(h + 1) * HEAD, g % 2, :], src[r:r + HEAD, :]).then_inc(came[g % 2], 16)
                else:
                    sp.dma_start(w_raw[:, g % 2, :], src[g * P:(g + 1) * P, :]).then_inc(came[g % 2], 16)

        @block.tensor
        def _(pe):
            for g in range(KD):
                pe.wait_ge(cut, 2 * g + 2)
                for u in range(BANKS):
                    last = product(pe, u, g)
                    if g == KD - 1:
                        last.then_inc(done, 1)
            for u in range(BANKS, 2 * T):
                pe.wait_ge(added, u - BANKS + 1)
                for g in range(KD):
                    last = product(pe, u, g)
                last.then_inc(done, 1)

        @block.scalar
        def _(act):
            for g in range(KD):
                act.wait_ge(came[g % 2], came_by(g))
                split_hi(act, m_hi[:, g, :], m_raw[:, g % 2, :]).then_inc(high, 1)
                split_hi(act, w_hi[:, g, :], w_raw[:, g % 2, :]).then_inc(high, 1)
            for i in range(T):
                act.wait_ge(added, 2 * i + 2)
                if i:
                    act.wait_ge(squared, i)
                act.activation(squares[:], k["x"][:, i, :], ACT.Square, accum_out=k["ms"][:, i:i + 1]).then_inc(squared, 1)

        @block.vector
        def _(dve):
            for g in range(KD):
                dve.wait_ge(high, 2 * g + 1)
                split_lo(dve, m_lo[:, g, :], m_raw[:, g % 2, :], m_hi[:, g, :]).then_inc(cut, 1)
                dve.wait_ge(high, 2 * g + 2)
                split_lo(dve, w_lo[:, g, :], w_raw[:, g % 2, :], w_hi[:, g, :]).then_inc(cut, 1)
            for u in range(2 * T):
                i, c = divmod(u, 2)
                x = k["x"][:, i, c * 512:(c + 1) * 512]
                dve.wait_ge(done, u + 1)
                dve.tensor_tensor(x, x, acc[:, u % BANKS, :], ALU.add).then_inc(added, 1)
    ph.close()


def feed(nc, t, k, layer):
    ph = Phase(nc, "ffn")
    h_hi, h_lo = ph.sb("h_hi", [P, KD, TOK], F32R), ph.sb("h_lo", [P, KD, TOK], F32R)
    gain = ph.sb("gain", [P, KD])
    NT = 3
    ND = 2 * T
    TURNS = [((0, 1, 2, 3), (4, 5)), ((6,), (7, 8)), ((), ())]
    raw = {n: ph.sb(f"raw_{n}", shape) for n, shape in (("g", [P, KD, P]), ("u", [P, KD, P]), ("d", [P, D_MODEL]))}
    hi = {n: ph.sb(f"hi_{n}", [P, 2] + shape, F32R) for n, shape in (("g", [KD, P]), ("u", [KD, P]), ("d", [D_MODEL]))}
    lo = {n: ph.sb(f"lo_{n}", [P, 2] + shape, F32R) for n, shape in (("g", [KD, P]), ("u", [KD, P]), ("d", [D_MODEL]))}
    xn, h32 = ph.sb("xn", [P, 2, D_MODEL]), ph.sb("h32", [P, 2, D_MODEL])
    sg, a32 = xn[:, 0, 0:768].rearrange("p (b n) -> p b n", b=2), xn[:, 1, 0:768].rearrange("p (b n) -> p b n", b=2)
    squares = ph.sb("squares", [P, D_MODEL])
    a_hi, a_lo = ph.sb("a_hi", [P, 2, TOK], F32R), ph.sb("a_lo", [P, 2, TOK], F32R)
    up = ph.ps("up", [P, 2, 2, 512])
    down = ph.ps("down", [P, 4, 512])
    norm = NormTranspose(ph, k, gain, h_hi, h_lo, xn, h32, down[:].rearrange("p (a b) n -> p a (b n)", a=2))
    g_in, squared, y_out = ph.sem("g_in"), ph.sem("squared"), ph.sem("y_out")
    came = {n: ph.sem(f"came_{n}") for n in "gud"}
    high = {n: ph.sem(f"high_{n}") for n in "gud"}
    cut = {n: ph.sem(f"cut_{n}") for n in "gud"}
    upped, activated, gated, a_high, a_cut, downed, added = (
        ph.sem(n) for n in ("upped", "activated", "gated", "a_high", "a_cut", "downed", "added"))
    src = {"g": t["w_gate"][layer].rearrange("(k p) n -> p k n", p=P),
           "u": t["w_up"][layer].rearrange("(k p) n -> p k n", p=P)}

    def steps(eng, step):
        step(0, 0)
        step(1, 1)
        with eng.Fori(1, KF // 2 - 1) as pair:
            for q in range(2):
                step(2 * pair + q, q)
        step(KF - 2, 0)
        step(KF - 1, 1)

    EARLY = 2

    def at(f, *tiles):
        return isinstance(f, int) and f in tiles

    with nc.Block() as block:
        @block.sync
        def _(sp):
            def load(n, f):
                if not at(f, 0):
                    sp.wait_ge(cut[n], f)
                piece = t["w_down"][layer][bass.ds(f * P, P), :] if n == "d" else src[n][:, :, bass.ds(f * P, P)]
                sp.dma_start(raw[n][:], piece).then_inc(came[n], 16)

            def step(f, q):
                if not at(f, KF - 1):
                    load("g", f + 1)
                    load("u", f + 1)
                load("d", f)

            with nc.allow_non_contiguous_dma(reason="gain vector"):
                sp.dma_start(gain[:], t["norm_ffn"][layer].rearrange("(k p) -> p k", p=P)).then_inc(g_in, 16)
            load("g", 0)
            load("u", 0)
            steps(sp, step)
            for i in range(T):
                sp.wait_ge(added, (KF - 1) * ND + 2 * i + 2)
                dst = t["y_sample"].rearrange("b s d -> (b s) d") if i == TP else t["y_prompt"][0, i * P:(i + 1) * P, :]
                sp.dma_start(dst, k["x"][:, i, :]).then_inc(y_out, 16)
            sp.wait_ge(y_out, 16 * T)

        @block.tensor
        def _(pe):
            def ups(f, q):
                for n in range(NT):
                    v = f * NT + n
                    b = (q * NT + n) % 2
                    if at(f, 0):
                        for i in TURNS[n][0]:
                            norm.pe_turn(pe, i)
                        pe.wait_ge(norm.ready, 3 * n + 3)
                    if not (at(f, 0) and n < 2):
                        pe.wait_ge(gated, v - 1)
                    span = slice(n * 384, (n + 1) * 384)
                    for which, w in ((0, "g"), (1, "u")):
                        if at(f, 0) and which:
                            for i in TURNS[n][1]:
                                norm.pe_turn(pe, i)
                        if n == 0:
                            pe.wait_ge(cut[w], f + 1)
                        for c in range(KD):
                            last = three_passes(pe, up[:, b, which, 0:384], hi[w][:, q, c, :], lo[w][:, q, c, :],
                                                h_hi[:, c, span], h_lo[:, c, span], c == 0, c == KD - 1)
                    last.then_inc(upped, 1)

            def downs(f, q):
                pe.wait_ge(cut["d"], f + 1)
                pe.wait_ge(a_cut, f * NT + NT)
                for n in range(ND):
                    i, c = divmod(n, 2)
                    if not (at(f, 0) and n < 4):
                        pe.wait_ge(added, f * ND + n - 3)
                    tok, col = slice(i * P, (i + 1) * P), slice(c * 512, (c + 1) * 512)
                    three_passes(pe, down[:, (q * ND + n) % 4, :], a_hi[:, q, tok], a_lo[:, q, tok],
                                 hi["d"][:, q, col], lo["d"][:, q, col], True, True).then_inc(downed, 1)

            def step(f, q):
                ups(f, q)
                if not at(f, 0):
                    downs(f - 1, 1 - q)

            steps(pe, step)
            downs(KF - 1, 1)

        @block.scalar
        def _(act):
            def raise_weight(n, f, q):
                act.wait_ge(came[n], f * 16 + 16)
                if not at(f, 0, 1):
                    act.wait_ge(*((downed, (f - 1) * ND) if n == "d" else (upped, (f - 1) * NT)))
                split_hi(act, hi[n][:, q], raw[n][:]).then_inc(high[n], 1)

            def raise_next(f, q):
                if not at(f, KF - 1):
                    raise_weight("g", f + 1, 1 - q)
                    raise_weight("u", f + 1, 1 - q)
                raise_weight("d", f, q)

            def step(f, q):
                if not at(f, 0):
                    raise_next(f, q)
                for n in range(NT):
                    if at(f, 0) and n == 1:
                        raise_next(f, q)
                    v = f * NT + n
                    b = (q * NT + n) % 2
                    span = slice(n * 384, (n + 1) * 384)
                    act.wait_ge(upped, v + 1)
                    if not (at(f, 0) and n < 2):
                        act.wait_ge(gated, v - 1)
                    act.activation(sg[:, b, :], up[:, b, 0, 0:384], ACT.Silu).then_inc(activated, 1)
                    act.wait_ge(gated, v + 1)
                    split_hi(act, a_hi[:, q, span], a32[:, b, :]).then_inc(a_high, 1)

            norm.act_start(act)
            for i in range(T + 1):
                if i < T:
                    norm.act_norm(act, i)
                if i == 1:
                    raise_weight("g", 0, 0)
                if i == 4:
                    raise_weight("u", 0, 0)
                if i >= 1:
                    norm.act_hi(act, i - 1)
            act.wait_ge(norm.turned, T)
            steps(act, step)
            for i in range(T):
                act.wait_ge(added, (KF - 1) * ND + 2 * i + 2)
                if i:
                    act.wait_ge(squared, i)
                act.activation(squares[:], k["x"][:, i, :], ACT.Square, accum_out=k["ms"][:, i:i + 1]).then_inc(squared, 1)

        @block.vector
        def _(dve):
            def cut_weight(n, f, q):
                dve.wait_ge(high[n], f + 1)
                split_lo(dve, lo[n][:, q], raw[n][:], hi[n][:, q]).then_inc(cut[n], 1)

            def add(f, q, products):
                for n in products:
                    i, c = divmod(n, 2)
                    x = k["x"][:, i, c * 512:(c + 1) * 512]
                    dve.wait_ge(downed, f * ND + n + 1)
                    dve.tensor_tensor(x, x, down[:, (q * ND + n) % 4, :], ALU.add).then_inc(added, 1)

            def cut_next(f, q):
                if not at(f, KF - 1):
                    cut_weight("g", f + 1, 1 - q)
                    cut_weight("u", f + 1, 1 - q)
                cut_weight("d", f, q)

            def step(f, q):
                if not at(f, 0):
                    cut_next(f, q)
                for n in range(NT):
                    if at(f, 0) and n == 1:
                        cut_next(f, q)
                    v = f * NT + n
                    b = (q * NT + n) % 2
                    span = slice(n * 384, (n + 1) * 384)
                    dve.wait_ge(activated, v + 1)
                    if not (at(f, 0) and n < 2):
                        dve.wait_ge(a_cut, v - 1)
                    if n == 0 and not at(f, 0, 1):
                        dve.wait_ge(downed, (f - 1) * ND)
                    dve.tensor_tensor(a32[:, b, :], sg[:, b, :], up[:, b, 1, 0:384], ALU.mult).then_inc(gated, 1)
                    if n == NT - 1 and not at(f, 0):
                        add(f - 1, 1 - q, range(EARLY))
                    dve.wait_ge(gated, v + 1)
                    dve.wait_ge(a_high, v + 1)
                    split_lo(dve, a_lo[:, q, span], a32[:, b, :], a_hi[:, q, span]).then_inc(a_cut, 1)
                if not at(f, 0):
                    add(f - 1, 1 - q, range(EARLY, ND))

            norm.dve_start(dve)
            norm.dve_scales(dve)
            dve.wait_ge(g_in, 16)
            for i in range(T + 1):
                if i < T:
                    norm.dve_gain(dve, i)
                if i == 1:
                    cut_weight("g", 0, 0)
                if i == 4:
                    cut_weight("u", 0, 0)
                if i >= 1:
                    norm.dve_lo(dve, i - 1)
            steps(dve, step)
            add(KF - 1, 1, range(ND))
    ph.close()


_INS = ["x_prompt", "x_sample", "cache_a_k", "cache_a_v", "cache_b_k", "cache_b_v", "cache_c_k", "cache_c_v",
        "cache_c_logf", "rel_bias_table", "norm_mix", "w_in", "b_forget", "q_norm_a", "k_norm_a", "sinks_a",
        "q_norm_b", "k_norm_b", "lam_q1", "lam_k1", "lam_q2", "lam_k2", "subln_b", "q_norm_c", "k_norm_c",
        "w_out", "norm_ffn", "w_gate", "w_up", "w_down"]


def _heads(lead):
    return {"a_k": lead + (A_KV, HEAD), "a_v": lead + (A_KV, HEAD), "b_k": lead + (B_HEADS, 2, B_DIM),
            "b_v": lead + (B_HEADS, HEAD), "c_k": lead + (C_HEADS, HEAD), "c_v": lead + (C_HEADS, HEAD),
            "c_logf": lead + (C_HEADS,)}


_OUTS = {"y_prompt": (1, SEQ, D_MODEL), "y_sample": (DEC_BATCH, DEC_SEQ, D_MODEL)}
_OUTS.update({"p_" + n: v for n, v in _heads((DEPTH, 1, SEQ)).items()})
_OUTS.update({"s_" + n: v for n, v in _heads((DEPTH, DEC_BATCH, DEC_SEQ)).items()})
for _kv in "kv":
    _OUTS[f"p_a_{_kv}"] = (DEPTH, 1, WINDOW, A_KV, HEAD)
    _OUTS[f"s_a_{_kv}"] = (DEPTH, DEC_BATCH, WINDOW, A_KV, HEAD)

_SCRATCH = {"qkv": (TOK, FZ), "qkT": (1792, TOK), "mixT": (D_MODEL, TOK), "bias_rows": (A_HEADS + B_HEADS, COPIES, REL), "bias_a": (A_HEADS, P, 2 * P),
            "bias_b": (B_HEADS, P, SEQ), "bias_sa": (A_HEADS, P, 2 * P), "bias_sb": (B_HEADS, P, 3 * P),
            "cum_prompt": (C_HEADS, SEQ), "cum_past": (DEC_BATCH * C_HEADS, PAST), "cum_new": (C_HEADS, P)}


def kernel(**inputs):
    import concourse.bacc as _bacc
    from concourse.bass_utils import run_bass_kernel_spmd as _run

    nc = _bacc.Bacc("TRN2", target_bir_lowering=False, num_devices=1)
    arrays, t = {}, {}
    for name in _INS:
        arrays[f"in_{name}"] = np.ascontiguousarray(inputs[name])
    for name, a in constants().items():
        arrays[f"in_{name}"] = a
    for name, a in arrays.items():
        t[name[3:]] = nc.dram_tensor(name, a.shape, mybir.dt.from_np(a.dtype), kind="ExternalInput").ap()
    for name, shape in _OUTS.items():
        t[name] = nc.dram_tensor(f"out_{name}", shape, F32, kind="ExternalOutput").ap()
    for name, shape in _SCRATCH.items():
        t[name] = nc.dram_tensor(f"scratch_{name}", shape, F32).ap()
    build(nc, t)
    r = _run(nc, [arrays], core_ids=[0])
    return tuple(r.results[0][f"out_{name}"] for name in _OUTS)
```
